# Optimizing a Trainium2 kernel written in Bass

```python
import math
import jax
import jax.numpy as jnp
from jax import lax
import numpy as np

D_MODEL = 2048
BATCH = 1
SEQ = 512
DEPTH = 1
DEC_BATCH = 8
DEC_SEQ = 4
PAST_LEN = 4096
PAGE_SIZE = 128

MIX_A = D_MODEL // 2
MIX_B = D_MODEL - MIX_A
GDN_HEADS = 8
GDN_DK = MIX_A // GDN_HEADS
GDN_DV = MIX_A // GDN_HEADS
QK_W = GDN_HEADS * GDN_DK
QKV_W = 2 * QK_W + GDN_HEADS * GDN_DV
CONV_W = 4
CHUNK = 64
POOL_WINDOWS = (2, 4, 8, 16)
POOL_GROUPS = len(POOL_WINDOWS)
POOL_CH = MIX_B // POOL_GROUPS
POOL_BUF = max(POOL_WINDOWS) - 1
N_MEM = 256
X_HEADS = 4
X_HEAD_DIM = D_MODEL // X_HEADS
EPS = 1e-6
COL_ZA = QKV_W
COL_A = COL_ZA + GDN_HEADS * GDN_DV
COL_B = COL_A + GDN_HEADS
COL_U = COL_B + GDN_HEADS
COL_ZB = COL_U + MIX_B
IN_COLS = COL_ZB + MIX_B

kernel_name = "hymba_gdn_pool_memxattn_step"

def rmsnorm(x, g):
    xf = x.astype(jnp.float32)
    y = xf * lax.rsqrt(jnp.mean(xf * xf, axis=-1, keepdims=True) + EPS) * g.astype(jnp.float32)
    return y.astype(x.dtype)

def l2norm(x):
    xf = x.astype(jnp.float32)
    return xf * lax.rsqrt(jnp.sum(xf * xf, axis=-1, keepdims=True) + EPS)

def short_conv(x, buf, w):
    t_len = x.shape[1]
    ext = jnp.concatenate([buf.astype(x.dtype), x], axis=1)
    y = sum(ext[:, j:j + t_len] * w[j] for j in range(CONV_W))
    return jax.nn.silu(y), ext[:, ext.shape[1] - (CONV_W - 1):]

def gated_delta_rule(q, k, v, g, beta, s0, chunk):
    bsz, t_len, n_h, _ = q.shape
    dv = v.shape[-1]
    n_c = t_len // chunk

    def blocks(a):
        a = a.astype(jnp.float32).reshape((bsz, n_c, chunk, n_h) + a.shape[3:])
        return jnp.moveaxis(a, (1, 3), (0, 2))

    qc, kc, vc, bc = blocks(q), blocks(k), blocks(v), blocks(beta)
    gc = jnp.cumsum(blocks(g), axis=-1)
    kb = kc * bc[..., None]
    vb = vc * bc[..., None]
    idx = jnp.arange(chunk)
    incl = idx[:, None] >= idx[None, :]
    strict = idx[:, None] > idx[None, :]
    diff = gc[..., :, None] - gc[..., None, :]
    decay_incl = jnp.exp(jnp.where(incl, diff, -jnp.inf))
    decay_strict = jnp.where(strict, decay_incl, 0.0)
    low = jnp.einsum('nbhik,nbhjk->nbhij', kb, kc) * decay_strict
    eye = jnp.eye(chunk, dtype=jnp.float32)
    t_inv = lax.linalg.triangular_solve(low + eye, jnp.broadcast_to(eye, low.shape),
                                        left_side=True, lower=True, unit_diagonal=True)
    u = jnp.einsum('nbhij,nbhjv->nbhiv', t_inv, vb)
    w = jnp.einsum('nbhij,nbhjk->nbhik', t_inv, kb * jnp.exp(gc)[..., None])
    a_intra = jnp.einsum('nbhik,nbhjk->nbhij', qc, kc) * decay_incl

    def step(s, xs):
        q_, k_, u_, w_, g_, a_ = xs
        v_new = u_ - jnp.einsum('bhck,bhkv->bhcv', w_, s)
        o = (jnp.einsum('bhck,bhkv->bhcv', q_ * jnp.exp(g_)[..., None], s)
             + jnp.einsum('bhij,bhjv->bhiv', a_, v_new))
        g_last = g_[..., -1]
        k_dec = k_ * jnp.exp(g_last[..., None] - g_)[..., None]
        s = s * jnp.exp(g_last)[..., None, None] + jnp.einsum('bhck,bhcv->bhkv', k_dec, v_new)
        return s, o

    s_fin, o = lax.scan(step, s0.astype(jnp.float32), (qc, kc, u, w, gc, a_intra))
    o = jnp.moveaxis(o, (0, 2), (1, 3)).reshape(bsz, t_len, n_h, dv)
    return o, s_fin

def multiscale_pool(u, buf, pos0, pool_w, pool_scale):
    bsz, t_len, c = u.shape
    ext = jnp.concatenate([buf.astype(u.dtype), u], axis=1)
    cs = jnp.cumsum(ext.astype(jnp.float32), axis=1)
    cs = jnp.concatenate([jnp.zeros((bsz, 1, c), jnp.float32), cs], axis=1)
    pos = pos0 + jnp.arange(t_len)
    outs = []
    for gi, win in enumerate(POOL_WINDOWS):
        sl = slice(gi * POOL_CH, (gi + 1) * POOL_CH)
        hi = cs[:, POOL_BUF + 1:POOL_BUF + 1 + t_len, sl]
        lo = cs[:, POOL_BUF + 1 - win:POOL_BUF + 1 - win + t_len, sl]
        cnt = jnp.minimum(win, pos + 1).astype(jnp.float32)[None, :, None]
        d = (hi - lo) / cnt - u[:, :, sl].astype(jnp.float32)
        outs.append(jnp.einsum('btc,cd->btd', d.astype(u.dtype), pool_w[gi]))
    y = jnp.concatenate(outs, axis=-1) * pool_scale
    return y, ext[:, ext.shape[1] - POOL_BUF:]

def memory_kv(mem, norm_mem, w_ck, w_cv):
    bsz, n_mem, _ = mem.shape
    hm = rmsnorm(mem, norm_mem)
    mk = (hm @ w_ck).reshape(bsz, n_mem, X_HEADS, X_HEAD_DIM)
    mv = (hm @ w_cv).reshape(bsz, n_mem, X_HEADS, X_HEAD_DIM)
    return mk, mv

def hybrid_layer(x, mem_k, mem_v, s0, conv_buf, pool_buf, pos0, chunk,
                 norm_mix, w_in, conv_w, a_log, dt_bias, gdn_norm, pool_w, pool_scale, w_out,
                 norm_cross, w_cq, w_co):
    bsz, t_len, _ = x.shape
    h = rmsnorm(x, norm_mix)
    proj = h @ w_in
    qkv, conv_new = short_conv(proj[..., :QKV_W], conv_buf, conv_w)
    q = l2norm(qkv[..., :QK_W].reshape(bsz, t_len, GDN_HEADS, GDN_DK)) * (GDN_DK ** -0.5)
    k = l2norm(qkv[..., QK_W:2 * QK_W].reshape(bsz, t_len, GDN_HEADS, GDN_DK))
    v = qkv[..., 2 * QK_W:].reshape(bsz, t_len, GDN_HEADS, GDN_DV)
    z_a = proj[..., COL_ZA:COL_A].reshape(bsz, t_len, GDN_HEADS, GDN_DV)
    beta = jax.nn.sigmoid(proj[..., COL_B:COL_U].astype(jnp.float32))
    g = -jnp.exp(a_log.astype(jnp.float32)) * jax.nn.softplus(
        proj[..., COL_A:COL_B].astype(jnp.float32) + dt_bias.astype(jnp.float32))
    o, s_new = gated_delta_rule(q, k, v, g, beta, s0, chunk)
    o_a = (rmsnorm(o.astype(x.dtype), gdn_norm) * jax.nn.silu(z_a)).reshape(bsz, t_len, MIX_A)
    pooled, pool_new = multiscale_pool(proj[..., COL_U:COL_ZB], pool_buf, pos0, pool_w, pool_scale)
    o_b = pooled * jax.nn.silu(proj[..., COL_ZB:])
    x = x + jnp.concatenate([o_a, o_b], axis=-1) @ w_out
    h2 = rmsnorm(x, norm_cross)
    qx = (h2 @ w_cq).reshape(bsz, t_len, X_HEADS, X_HEAD_DIM)
    scores = jnp.einsum('bthd,bmhd->bhtm', qx, mem_k).astype(jnp.float32) * (X_HEAD_DIM ** -0.5)
    probs = jax.nn.softmax(scores, axis=-1).astype(x.dtype)
    ctx = jnp.einsum('bhtm,bmhd->bthd', probs, mem_v).reshape(bsz, t_len, D_MODEL)
    x = x + ctx @ w_co
    return x, s_new, conv_new, pool_new

def setup_inputs(seed: int = 0) -> dict:
    key = jax.random.key(seed)
    ks = jax.random.split(key, 26)
    f32 = jnp.float32
    n_l = DEPTH

    def nrm(k, shape, scale):
        return jax.random.normal(k, shape, f32) * scale

    def gain(k, shape):
        return 1.0 + 0.02 * jax.random.normal(k, shape, f32)

    dt = jnp.exp(jax.random.uniform(ks[11], (n_l, GDN_HEADS), f32, math.log(1e-3), math.log(1e-1)))
    dt_bias = dt + jnp.log(-jnp.expm1(-dt))
    a_log = jnp.log(jax.random.uniform(ks[12], (n_l, GDN_HEADS), f32, 1.0, 16.0))
    return {
        "x_prompt": nrm(ks[0], (BATCH, SEQ, D_MODEL), 1.0),
        "x_sample": nrm(ks[1], (DEC_BATCH, DEC_SEQ, D_MODEL), 1.0),
        "mem_prompt": nrm(ks[2], (BATCH, N_MEM, D_MODEL), 1.0),
        "cache_mem_k": nrm(ks[3], (n_l, DEC_BATCH, N_MEM, X_HEADS, X_HEAD_DIM), 1.0),
        "cache_mem_v": nrm(ks[4], (n_l, DEC_BATCH, N_MEM, X_HEADS, X_HEAD_DIM), 1.0),
        "state_delta": nrm(ks[5], (n_l, DEC_BATCH, GDN_HEADS, GDN_DK, GDN_DV), 0.1),
        "state_conv": nrm(ks[6], (n_l, DEC_BATCH, CONV_W - 1, QKV_W), 1.0),
        "state_pool": nrm(ks[7], (n_l, DEC_BATCH, POOL_BUF, MIX_B), 1.0),
        "norm_mix": gain(ks[8], (n_l, D_MODEL)),
        "w_in": nrm(ks[9], (n_l, D_MODEL, IN_COLS), D_MODEL ** -0.5),
        "conv_w": nrm(ks[10], (n_l, CONV_W, QKV_W), CONV_W ** -0.5),
        "a_log": a_log,
        "dt_bias": dt_bias,
        "gdn_norm": gain(ks[13], (n_l, GDN_DV)),
        "pool_w": nrm(ks[14], (n_l, POOL_GROUPS, POOL_CH, POOL_CH), POOL_CH ** -0.5),
        "pool_scale": gain(ks[15], (n_l, MIX_B)),
        "w_out": nrm(ks[16], (n_l, D_MODEL, D_MODEL), D_MODEL ** -0.5),
        "norm_mem": gain(ks[17], (n_l, D_MODEL)),
        "norm_cross": gain(ks[18], (n_l, D_MODEL)),
        "w_cq": nrm(ks[19], (n_l, D_MODEL, D_MODEL), D_MODEL ** -0.5),
        "w_ck": nrm(ks[20], (n_l, D_MODEL, D_MODEL), D_MODEL ** -0.5),
        "w_cv": nrm(ks[21], (n_l, D_MODEL, D_MODEL), D_MODEL ** -0.5),
        "w_co": nrm(ks[22], (n_l, D_MODEL, D_MODEL), D_MODEL ** -0.5),
        "norm_final": gain(ks[23], (D_MODEL,)),
    }

def reference(x_prompt, x_sample, mem_prompt, cache_mem_k, cache_mem_v, state_delta, state_conv,
              state_pool, norm_mix, w_in, conv_w, a_log, dt_bias, gdn_norm, pool_w, pool_scale,
              w_out, norm_mem, norm_cross, w_cq, w_ck, w_cv, w_co, norm_final):
    xp, xs = x_prompt, x_sample
    bp, tp, _ = xp.shape
    ts = xs.shape[1]
    chunk_p = min(CHUNK, tp)
    mk_l, mv_l, dp_l, cp_l, pp_l, ds_l, cs_l, ps_l = [], [], [], [], [], [], [], []
    for l in range(DEPTH):
        lw = dict(norm_mix=norm_mix[l], w_in=w_in[l], conv_w=conv_w[l], a_log=a_log[l],
                  dt_bias=dt_bias[l], gdn_norm=gdn_norm[l], pool_w=pool_w[l],
                  pool_scale=pool_scale[l], w_out=w_out[l], norm_cross=norm_cross[l],
                  w_cq=w_cq[l], w_co=w_co[l])
        mk_p, mv_p = memory_kv(mem_prompt, norm_mem[l], w_ck[l], w_cv[l])
        xp, d_p, c_p, p_p = hybrid_layer(
            xp, mk_p, mv_p,
            jnp.zeros((bp, GDN_HEADS, GDN_DK, GDN_DV), jnp.float32),
            jnp.zeros((bp, CONV_W - 1, QKV_W), xp.dtype),
            jnp.zeros((bp, POOL_BUF, MIX_B), xp.dtype),
            0, chunk_p, **lw)
        xs, d_s, c_s, p_s = hybrid_layer(
            xs, cache_mem_k[l], cache_mem_v[l], state_delta[l], state_conv[l], state_pool[l],
            PAST_LEN, ts, **lw)
        mk_l.append(mk_p); mv_l.append(mv_p); dp_l.append(d_p); cp_l.append(c_p); pp_l.append(p_p)
        ds_l.append(d_s); cs_l.append(c_s); ps_l.append(p_s)
    y_prompt = rmsnorm(xp, norm_final)
    y_sample = rmsnorm(xs, norm_final)
    return (y_prompt, y_sample, jnp.stack(mk_l), jnp.stack(mv_l), jnp.stack(dp_l), jnp.stack(cp_l),
            jnp.stack(pp_l), jnp.stack(ds_l), jnp.stack(cs_l), jnp.stack(ps_l))


_drawn_inputs = setup_inputs


def setup_inputs(seed=0):
    import zlib

    import numpy as np

    out = dict(_drawn_inputs(seed))
    spreads = {}
    factors = {'gdn_norm': 7.543,
     'pool_scale': 8.0,
     'norm_mem': 2.824,
     'norm_cross': 8.0,
     'norm_final': 2.868}
    for name, (base, spread) in spreads.items():
        noise = np.random.default_rng([zlib.crc32(name.encode()), seed]).standard_normal(out[name].shape)
        drawn = base * np.exp(spread * noise) if base else spread * noise
        out[name] = jnp.asarray(drawn.astype(out[name].dtype))
    for name, factor in factors.items():
        out[name] = (out[name] * factor).astype(out[name].dtype)
    return out
```

```python
from contextlib import ExitStack

import numpy as np

import concourse.bass as bass
from concourse import mybir

F32 = mybir.dt.float32
F32R = mybir.dt.float32r
ALU = mybir.AluOpType
ACT = mybir.ActivationFunctionType
AX_X = mybir.AxisListType.X

P = 128
D = 2048
KT = D // P
SEQ = 512
NB, NT = 8, 4
NS = NB * NT
TOK = SEQ + NS
HALF = TOK // 2
HEADS = 8
MEM = 256
XH, XD = 4, 512
DT = XD // P
MIX = 1024
QKV = 3 * MIX
NQKV = QKV // P
COL_A = 4 * MIX
COL_U = COL_A + 2 * HEADS
COL_ZB = COL_U + MIX
WINDOWS = (2, 4, 8, 16)
NG = 4
BUF = 15
EPS = 1e-6
CH = SEQ // P
LEVELS = 7
CSEG = 3 + NT
EXTN = 3 + SEQ + NB * CSEG
YN = EXTN - 3
USEG = BUF + NT
UN = BUF + SEQ + NB * USEG
NTILE = 128

C_ID, C_ONE, C_INCL, C_LEV = 0, 128, 256, 384
C_SINCL = C_LEV + LEVELS * P
C_SL1, C_SL2, C_BM = C_SINCL + 32, C_SINCL + 64, C_SINCL + 96
C_INV = C_BM + NB
C_EPS = C_INV + NG * 16
C_LNQ = C_EPS + 1
NCONST = C_EPS + 2

G_MIX, G_MEM, G_CROSS, G_FINAL, G_GDN, G_POOL = 0, 16, 32, 48, 64, 65
NGAIN = 73
NCONV = 4 * NQKV


def constants():
    c = np.zeros((P, NCONST), np.float32)
    j, i = np.arange(P)[:, None], np.arange(P)[None, :]

    def level(s, j, i):
        return (i // (2 * s) == j // (2 * s)) & ((i // s) % 2 == 1) & ((j // s) % 2 == 0)

    c[:, C_ID:C_ID + P] = np.eye(P)
    c[:, C_ONE:C_ONE + P] = 1
    c[:, C_INCL:C_INCL + P] = i >= j
    for n in range(LEVELS):
        c[:, C_LEV + n * P:C_LEV + (n + 1) * P] = level(1 << n, j, i) * (-1.0 if n == 0 else 1.0)
    j, i = j[:NS], i[:, :NS]
    c[:NS, C_SINCL:C_SINCL + NS] = (i // NT == j // NT) & (i >= j)
    c[:NS, C_SL1:C_SL1 + NS] = -1.0 * level(1, j, i)
    c[:NS, C_SL2:C_SL2 + NS] = level(2, j, i)
    c[:NS, C_BM:C_BM + NB] = j // NT == np.arange(NB)[None, :]
    for g, w in enumerate(WINDOWS):
        c[:, C_INV + 16 * g:C_INV + 16 * g + 16] = 1.0 / np.minimum(w, np.arange(16) + 1)
    c[:, C_EPS] = EPS
    c[:, C_LNQ] = -0.5 * np.log(P)
    return c


class Reused:

    def __init__(self, sem, left_at):
        self.sem, self.left_at = sem, left_at

    def at(self, v):
        return v + self.left_at


def build(nc, t):
    with ExitStack() as ctx:
        ARENA, ARENA_END = 16512, 229344

        def sem(name):
            return ctx.enter_context(nc.semaphore(name))

        def put(name, shape, dtype, at):
            return nc.alloc_sbuf_tensor_at(name, [P] + list(shape), dtype, offset=ARENA + 4 * at)

        def area(start, end):
            pos = [start]

            def take(name, shape, dtype=F32):
                n = int(np.prod(shape))
                o = put(name, shape, dtype, pos[0])
                pos[0] += -(-n // 8) * 8
                assert pos[0] <= end, (name, pos[0], end)
                return o
            take.pos = pos
            return take

        M_RAW = 0
        M_HIGH = M_RAW + 4 * D
        M_A = M_HIGH + 2 * D
        M_B = M_A + 2 * KT * TOK
        M_C = M_B + KT * TOK
        M_END = (ARENA_END - ARENA) // 32 * 8
        raw = [put(f"w_raw{i}", [KT, P], F32, M_RAW + i * D) for i in range(4)]
        low = [put(f"w_low{i}", [KT, P], F32R, M_RAW + i * D) for i in range(4)]
        high = [put(f"w_high{i}", [KT, P], F32R, M_HIGH + i * D) for i in range(2)]
        a_hi = put("a_hi", [KT, TOK], F32R, M_A)
        a_lo = put("a_lo", [KT, TOK], F32R, M_A + KT * TOK)
        keep = area(M_C, M_END)
        cst = keep("cst", [NCONST])
        gain = keep("gain", [NGAIN])
        convw = keep("convw", [4, 3, HEADS])
        cols = keep("cols", [4, 5, HEADS])
        stat = keep("stat", [16])
        M_W = keep.pos[0]
        M_HIMIX = M_END - KT * TOK
        ident = cst[:, C_ID:C_ID + P]
        ones = cst[:, C_ONE:C_ONE + P]
        eps_col = cst[:, C_EPS:C_EPS + 1]

        pj = ctx.enter_context(nc.psum_tensor("pj", [P, 4, 512], F32))
        dk = ctx.enter_context(nc.psum_tensor("dk", [P, 4, 512], F32))

        xT_d = nc.dram_tensor("xT_scratch", [KT, P, TOK], F32, kind="Internal").ap()
        x2T_d = nc.dram_tensor("x2T_scratch", [KT, P, TOK], F32, kind="Internal").ap()
        kT_d = nc.dram_tensor("kT_scratch", [KT, P, MEM], F32, kind="Internal").ap()
        row_d = nc.dram_tensor("row_scratch", [2, HEADS, TOK], F32, kind="Internal").ap()

        def at_least(eng, s, v):
            if not (isinstance(v, int) and v <= 0):
                if isinstance(s, Reused):
                    eng.wait_ge(s.sem, s.at(v))
                else:
                    eng.wait_ge(s, v)

        w_loaded = [sem(f"w_loaded{i}") for i in range(4)]
        hi_cast = sem("hi_cast")
        lo_split = sem("lo_split")
        tile_done = sem("tile_done")
        pj_read = sem("pj_read")

        STAGES = ("mem", "head", "pool", "out", "cq", "co")
        FIRST = {"mem": 0, "head": 8, "pool": 16, "out": 20, "cq": 24, "co": 28}
        COUNT = {"mem": 8, "head": 8, "pool": 4, "out": 4, "cq": 4, "co": 4}
        w_in, w_out, w_cq, w_ck, w_cv, w_co = (t[n].rearrange("o (k p) n -> p (o k) n", p=P)
                                               for n in ("w_in", "w_out", "w_cq", "w_ck", "w_cv", "w_co"))

        def source(stage, j, q, v=False):
            if stage == "mem":
                return w_cv[:, :, bass.ds((j - 4) * 512 + q * P, P)] if v else w_ck[:, :, bass.ds(j * 512 + q * P, P)]
            if stage == "head":
                return w_in[:, :, bass.ds(j * P + q * MIX, P)]
            if stage == "pool":
                return w_in[:, :, bass.ds(j * 256 + (COL_ZB if q < 2 else COL_U) + (q % 2) * P, P)]
            return {"out": w_out, "cq": w_cq, "co": w_co}[stage][:, :, bass.ds(j * 512 + q * P, P)]

        def load_ahead(sp, stage, j, q, v=False):
            n = FIRST[stage] + j
            if q == 0:
                src = source(stage, j, 3, v)
            elif isinstance(j, int) and j + 1 == COUNT[stage]:
                if stage == "co":
                    return
                src = source(STAGES[STAGES.index(stage) + 1], 0, q - 1)
            else:
                src = source(stage, j + 1, q - 1, v or (isinstance(j, int) and j == 3))
            at_least(sp, tile_done, 4 * n + q)
            sp.dma_start(raw[(q + 3) % 4][:], src).then_inc(w_loaded[(q + 3) % 4], 16)

        def cast_high(act, stage, j, q):
            n = FIRST[stage] + j + q // 4
            q = q % 4
            if isinstance(n, int) and 4 * n >= NTILE:
                return
            act.wait_ge(w_loaded[q], 16 * n + 16)
            at_least(act, tile_done, 4 * n + q - 1)
            act.activation(high[q % 2][:], raw[q][:], ACT.Copy).then_inc(hi_cast, 1)

        def split_low(dve, stage, j, q):
            n = FIRST[stage] + j + q // 4
            q = q % 4
            if isinstance(n, int) and 4 * n >= NTILE:
                return
            dve.wait_ge(hi_cast, 4 * n + q + 1)
            dve.tensor_tensor(low[q][:], raw[q][:], high[q % 2][:].bitcast(F32), ALU.subtract).then_inc(lo_split, 1)

        def multiply(pe, stage, j, q, xh, xl, n_tok=TOK, steps=None):
            w = 4 * (FIRST[stage] + j) + q
            steps = steps or {}
            pe.wait_ge(lo_split, w + 1)
            at_least(pe, pj_read, w - 1)
            parts = [(0, HALF), (HALF, HALF)] if n_tok == TOK else [(0, n_tok)]
            for k in range(KT):
                for m, (wt, x) in enumerate(((high[q % 2], xh), (high[q % 2], xl), (low[q], xh))):
                    for b, (o, n) in enumerate(parts):
                        mm = pe.matmul(pj[:, 2 * (q % 2) + b, 0:n], wt[:, k, :], x(k, o, n),
                                       start=(k == 0 and m == 0), stop=(k == KT - 1 and m == 2))
                if k == KT - 1:
                    mm.then_inc(tile_done, 1)
                for step in steps.get(k, ()):
                    step(pe)

        def tokens(x):
            return lambda k, o, n: x[:, k, o:o + n]

        def product(q, n_tok=TOK):
            return pj[:, 2 * (q % 2):2 * (q % 2) + 2, 0:HALF] if n_tok == TOK else pj[:, 2 * (q % 2), 0:n_tok]

        def halves(x):
            return x.rearrange("p (b n) -> p b n", b=2)

        hm_hi = put("hm_hi", [KT, MEM], F32R, M_B)
        hm_lo = put("hm_lo", [KT, MEM], F32R, M_B + KT * MEM)
        vrow = put("vrow", [2, P], F32, M_A)
        scrow = put("scrow", [QKV], F32, M_A + 2 * P)
        sct = put("sct", [3, HEADS, NB, 3], F32, M_END - 3 * HEADS * NB * 3)
        take = area(M_W, M_END - 576)
        xin = [take(f"xin{i}", [D]) for i in range(2)]
        xs = take("xs", [D])
        xts = take("xts", [KT, P])
        kts = take("kts", [4, MEM])
        mst = take("mst", [2, 512])

        const_loaded, vec_loaded, vec_turned, vec_ready = (sem(n) for n in (
            "const_loaded", "vec_loaded", "vec_turned", "vec_ready"))
        x_loaded, squared, rooted, inverted, x_scaled = (sem(n) for n in (
            "x_loaded", "squared", "rooted", "inverted", "x_scaled"))
        x_turned = sem("x_turned")
        x_high = sem("x_high")
        x_bank = sem("x_bank")
        xts_stored, kts_stored, m_turned, mst_ready, mst_stored = (sem(n) for n in (
            "xts_stored", "kts_stored", "m_turned", "mst_ready", "mst_stored"))

        def banks_before(n):
            return 4 * n if isinstance(n, int) and n < 2 else 8 * (n - 1)

        def x_stats(act, n, src, rows):
            act.wait_ge(x_loaded, 16 * (n + 1))
            at_least(act, x_turned, banks_before(n))
            act.activation(xs[0:rows, :], src[0:rows, :], ACT.Square,
                           accum_out=stat[0:rows, 0:1]).then_inc(squared, 1)
            act.wait_ge(squared, n + 1)
            act.activation(stat[0:rows, 1:2], stat[0:rows, 0:1], ACT.Sqrt, scale=1.0 / D,
                           bias=eps_col[0:rows, :]).then_inc(rooted, 1)

        def x_scale(dve, n, src, rows):
            dve.wait_ge(rooted, n + 1)
            dve.reciprocal(stat[0:rows, 2:3], stat[0:rows, 1:2]).then_inc(inverted, 1)
            dve.wait_ge(inverted, n + 1)
            dve.tensor_scalar(xs[0:rows, :], src[0:rows, :], stat[0:rows, 2:3], None, ALU.mult).then_inc(x_scaled, 1)

        def x_turn(pe, src, c, slot, part, rows):
            at_least(pe, x_bank, c - 1)
            for m in range(4):
                k = 4 * part + m
                mm = pe.transpose(dk[:, slot % 3, m * rows:(m + 1) * rows], src[0:rows, k * P:(k + 1) * P],
                                  ident[0:rows, 0:rows])
            mm.then_inc(x_turned, 1)

        def x_take_high(act, c, nhigh, slot, part, dst, lo, rows, g0):
            act.wait_ge(x_turned, c + 1)
            for m in range(4):
                k = 4 * part + m
                a = act.activation(dst[:, k, bass.ds(lo, rows)], dk[:, slot % 3, m * rows:(m + 1) * rows], ACT.Copy,
                                   scale=gain[:, g0 + k:g0 + k + 1])
            a.then_inc(x_high, 1)

        def x_take_low(dve, nhigh, slot, part, hi, dst, lo, rows, g0):
            dve.wait_ge(x_high, nhigh + 1)
            for m in range(4):
                k = 4 * part + m
                a = dve.scalar_tensor_tensor(dst[:, k, bass.ds(lo, rows)], dk[:, slot % 3, m * rows:(m + 1) * rows],
                                             gain[:, g0 + k:g0 + k + 1], hi[:, k, bass.ds(lo, rows)].bitcast(F32),
                                             ALU.mult, ALU.subtract)
            a.then_inc(x_bank, 1)

        def store_k_or_v(sp, j, v):
            dst = (t["mem_v_prompt"] if v else t["mem_k_prompt"])[0, 0].rearrange("(m p) h d -> p m (h d)", p=P)
            if not v:
                sp.wait_ge(pj_read, 4 * j + 4)
                sp.dma_start(kT_d[bass.ds(4 * j, 4), :, :].rearrange("k p r -> p k r"), kts[:]).then_inc(kts_stored, 16)
            sp.wait_ge(mst_ready, 4 * j + 4)
            sp.dma_start(dst[:, :, bass.ds((j - 4 if v else j) * 512, 512)], mst[:]).then_inc(mst_stored, 16)

        def sp_mem(sp):
            sp.dma_start(xin[0][:], t["mem_prompt"][0, 0:P, :]).then_inc(x_loaded, 16)
            sp.dma_start(cst[:], t["consts"]).then_inc(const_loaded, 16)
            for name, o, n in (("norm_mix", G_MIX, 16), ("norm_mem", G_MEM, 16), ("norm_cross", G_CROSS, 16),
                               ("norm_final", G_FINAL, 16), ("gdn_norm", G_GDN, 1), ("pool_scale", G_POOL, 8)):
                src = t[name].rearrange("(o n) -> o n", o=1) if name == "norm_final" else t[name]
                sp.dma_start(vrow[o:o + n, 0, :], src.rearrange("o (k p) -> (o k) p", p=P)).then_inc(vec_loaded, 16)
            sp.dma_start(vrow[0:NCONV, 1, :], t["conv_w"].rearrange("o j (k p) -> (o j k) p", p=P)).then_inc(vec_loaded, 16)
            sp.dma_start(scrow[0:24, :], t["state_conv"].rearrange("o b j n -> (o b j) n")).then_inc(vec_loaded, 16)
            sp.wait_ge(x_loaded, 16)
            sp.dma_start(xin[1][:], t["mem_prompt"][0, P:MEM, :]).then_inc(x_loaded, 16)
            for q in range(3):
                sp.dma_start(raw[q][:], source("mem", 0, q)).then_inc(w_loaded[q], 16)
            sp.wait_ge(x_loaded, 32)

            def group(j, v, x, store_v):
                for q in range(4):
                    load_ahead(sp, "mem", j, q, v)
                    if q == 0 and x is not None:
                        at_least(sp, x_turned, 4 if isinstance(j, int) and j == 0 else 8 * (j + 1))
                        if x == "sample":
                            sp.dma_start(xin[0][0:NS, :], t["x_sample"].rearrange("b t d -> (b t) d")).then_inc(x_loaded, 16)
                        else:
                            sp.dma_start(xin[0][:], t["x_prompt"][0, bass.ds(j * P, P), :]).then_inc(x_loaded, 16)
                    if q == 1 and not (isinstance(j, int) and j == 0):
                        store_k_or_v(sp, j - 1, store_v)
                    if q == 2 and x is not None:
                        rows = NS if x == "sample" else P
                        sp.wait_ge(x_bank, 8 * (j + 1) + 4)
                        sp.dma_start(xT_d[:, :, bass.ds((j + 1) * P - P, rows)].rearrange("k p r -> p k r"),
                                     xts[:, :, 0:rows]).then_inc(xts_stored, 16)

            group(0, False, "x", False)
            with sp.Fori(1, 3) as j:
                group(j, False, "x", False)
            group(3, False, "x", False)
            group(4, True, "sample", False)
            with sp.Fori(5, 7) as j:
                group(j, True, None, True)
            group(7, True, None, True)

        def pe_mem(pe):
            pe.wait_ge(const_loaded, 16)
            pe.wait_ge(vec_loaded, 16 * 8)
            pe.transpose(dk[:, 3, 0:NGAIN], vrow[0:NGAIN, 0, :], ident[0:NGAIN, 0:NGAIN])
            pe.transpose(dk[:, 3, P:P + NCONV], vrow[0:NCONV, 1, :], ident[0:NCONV, 0:NCONV]).then_inc(vec_turned, 1)
            for k in range(NQKV):
                mm = pe.transpose(pj[:, k // 16, (k % 16) * 24:(k % 16) * 24 + 24], scrow[0:24, k * P:(k + 1) * P],
                                  ident[0:24, 0:24])
            mm.then_inc(vec_turned, 1)
            for n in range(2):
                pe.wait_ge(x_scaled, n + 1)
                for part in range(4):
                    x_turn(pe, xs, 4 * n + part, 4 * n + part, part, P)
            pe.wait_ge(x_bank, 8)
            pe.wait_ge(vec_ready, 2)

            def turn_out(q, w):
                def step(pe):
                    pe.wait_ge(pj_read, w)
                    at_least(pe, mst_ready, w - 1)
                    for m in range(2):
                        mm = pe.transpose(dk[:, 3, m * P:(m + 1) * P], kts[:, (q + 3) % 4, m * P:(m + 1) * P], ident)
                    mm.then_inc(m_turned, 1)
                return step

            def group(j, x):
                rows = NS if x == "sample" else P
                for q in range(4):
                    steps = {}
                    if x is not None:
                        def turn(b):
                            def step(pe):
                                if b == 0:
                                    pe.wait_ge(x_loaded, 16 * (j + 3))
                                if b == 4:
                                    pe.wait_ge(x_scaled, j + 3)
                                x_turn(pe, xin[0] if b < 4 else xs, 8 * (j + 1) + b, b + 2, b % 4, rows)
                            return step
                        steps = {5: [turn(2 * q)], 12: [turn(2 * q + 1)]}
                    if not (isinstance(j, int) and j == 0 and q == 0):
                        steps[8] = [turn_out(q, 4 * j + q)]
                    multiply(pe, "mem", j, q, tokens(hm_hi), tokens(hm_lo), MEM, steps)

            group(0, "x")
            with pe.Fori(1, 4) as j:
                group(j, "x")
            group(4, "sample")
            with pe.Fori(5, 8) as j:
                group(j, None)
            turn_out(0, 32)(pe)

        def act_mem(act):
            act.wait_ge(const_loaded, 16)
            for n in range(2):
                x_stats(act, n, xin[n], P)
                act.wait_ge(vec_ready, 1)
                for part in range(4):
                    x_take_high(act, 4 * n + part, 4 * n + part, 4 * n + part, part, hm_hi, n * P, P, G_MEM)
                if n == 0:
                    cast_high(act, "mem", 0, 0)

            def group(j, x, keys):
                rows = NS if x == "sample" else P
                for q in range(4):
                    cast_high(act, "mem", j, q + 1)
                    if x is not None and q == 1:
                        x_stats(act, j + 2, xin[0], rows)
                    if x is not None and q > 1:
                        for b in (2 * q, 2 * q + 1):
                            x_take_high(act, 8 * (j + 1) + b, None, b + 2, b % 4, a_hi, j * P, rows, G_MIX)
                    act.wait_ge(tile_done, 4 * j + q + 1)
                    at_least(act, m_turned, 4 * j + q - 3)
                    if q == 0 and keys:
                        at_least(act, kts_stored, 16 * j)
                    act.activation(kts[:, q, :], product(q, MEM), ACT.Copy).then_inc(pj_read, 1)

            group(0, "x", True)
            with act.Fori(1, 4) as j:
                group(j, "x", True)
            group(4, "sample", True)
            with act.Fori(5, 8) as j:
                group(j, None, False)

        def dve_mem(dve):
            x_scale(dve, 0, xin[0], P)
            dve.wait_ge(vec_turned, 1)
            dve.tensor_copy(gain[:], dk[:, 3, 0:NGAIN])
            dve.tensor_copy(convw[:].rearrange("p j g h -> p (j g h)"), dk[:, 3, P:P + NCONV]).then_inc(vec_ready, 1)
            dve.wait_ge(vec_ready, 1)
            for part in range(4):
                x_take_low(dve, part, part, part, hm_hi, hm_lo, 0, P, G_MEM)
            dve.wait_ge(x_turned, 4)
            x_scale(dve, 1, xin[1], P)
            dve.wait_ge(vec_turned, 2)
            flat = sct[:].rearrange("p g h b j -> p (g h b j)")
            dve.tensor_copy(flat[:, 0:384], pj[:, 0, 0:384])
            dve.tensor_copy(flat[:, 384:576], pj[:, 1, 0:192]).then_inc(vec_ready, 1)
            for part in range(4):
                x_take_low(dve, 4 + part, 4 + part, part, hm_hi, hm_lo, P, P, G_MEM)
            split_low(dve, "mem", 0, 0)

            def read_out(q, w):
                dve.wait_ge(m_turned, w)
                if q == 1:
                    at_least(dve, mst_stored, 4 * (w - 1))
                dve.tensor_copy(mst[:, :, (q + 3) % 4 * P:(q + 3) % 4 * P + P],
                                dk[:, 3, 0:2 * P].rearrange("p (m n) -> p m n", m=2)).then_inc(mst_ready, 1)

            def group(j, x):
                rows = NS if x == "sample" else P
                for q in range(4):
                    split_low(dve, "mem", j, q + 1)
                    if x is not None:
                        for b in (2 * q, 2 * q + 1):
                            if b < 4:
                                dve.wait_ge(x_turned, 8 * (j + 1) + b + 1)
                                if b == 0:
                                    at_least(dve, xts_stored, 16 * j)
                                dve.tensor_copy(xts[:, 4 * b:4 * b + 4, 0:rows],
                                                dk[:, (b + 2) % 3, 0:4 * rows].rearrange("p (m r) -> p m r", m=4)).then_inc(x_bank, 1)
                            else:
                                x_take_low(dve, 8 + 4 * j + b - 4, b + 2, b % 4, a_hi, a_lo, j * P, rows, G_MIX)
                            if b == 2 * q and not (isinstance(j, int) and j == 0 and q == 0):
                                read_out(q, 4 * j + q)
                        if q == 1:
                            x_scale(dve, j + 2, xin[0], rows)
                    else:
                        read_out(q, 4 * j + q)

            group(0, "x")
            with dve.Fori(1, 4) as j:
                group(j, "x")
            group(4, "sample")
            with dve.Fori(5, 8) as j:
                group(j, None)
            read_out(0, 32)

        low_area = area(M_W, M_HIMIX)
        ext = low_area("ext", [EXTN])
        yq = low_area("yq", [3, EXTN])
        st = low_area("st", [3, 2, P])
        ecol = low_area("ecol", [NB, 3])
        ecol_ready = sem("ecol_ready")
        hw = low_area("hw", [4, 3])
        hc = low_area("hc", [4, 5])
        take = area(M_W + 3528, M_END - 576)
        kq = take("kq", [3, TOK])
        vs = take("vs", [TOK])
        gcb = take("gcb", [TOK])
        betab = take("betab", [TOK])
        dd = take("dd", [2, TOK])
        at_ = take("at", [CH, P])
        lt = take("lt", [CH, P])
        ltm = take("ltm", [CH, P])
        x1 = take("x1", [3, CH, P])
        vbk = take("vbk", [2 * TOK])
        smp = take("smp", [12, NS])
        SQ = put("sq", [2, TOK], F32, M_W + 3528 + 3 * TOK + 3 * TOK + 2 * TOK + 3 * CH * P)
        take = area(M_B + 10 * TOK, M_B + 16 * TOK)
        s0 = take("s0", [NB, P])
        zraw = take("zraw", [TOK])
        zs = take("zs", [TOK])
        sst = take("sst", [2, P])
        rr = take("rr", [P])
        vn = take("vn", [P])
        kds = take("kds", [P])
        rs_s = take("rs_s", [P])
        vns = take("vns", [P])
        mixo = put("mixo", [KT, TOK], F32, M_B)

        d_, db_ = dd[:, 0, 0:SEQ].rearrange("p (c n) -> p c n", c=CH), dd[:, 1, 0:SEQ].rearrange("p (c n) -> p c n", c=CH)
        tt_, uu, p1 = x1[:, 0], x1[:, 1], x1[:, 2]
        rn = vbk[:, 0:2 * TOK]
        vb = vbk[:, 0:SEQ].rearrange("p (c n) -> p c n", c=CH)
        kd = vbk[:, SEQ:2 * SEQ].rearrange("p (c n) -> p c n", c=CH)
        ds_, dbs, lts, us, ts_, p1s, ats, rt, tmp, qs_, os_, slm = (smp[:, i, :] for i in range(12))
        slm_ready = sem("slm_ready")
        incl = cst[:, C_INCL:C_INCL + P]
        lev = lambda l: cst[:, C_LEV + l * P:C_LEV + (l + 1) * P]
        S_ = slice(0, NS)

        def per_chunk(x):
            return x.unsqueeze(1).to_broadcast([P, CH, P])

        (row_ready, row_stored, row_loaded, s0_loaded, hw_ready, hc_ready, ext_state, ext_turned, st_ready, st_stored,
         conv_step, conv_done) = (sem(n) for n in (
            "row_ready", "row_stored", "row_loaded", "s0_loaded", "hw_ready", "hc_ready", "ext_state", "ext_turned",
            "st_ready", "st_stored", "conv_step", "conv_done"))
        (qk_silu, vz_silu, sq_done, ssq_done, ln_done, rn_done, d_ready, d_exp, eg_ready, kq_normed, qg_ready,
         dmi_ready, db_ready, kk_done, at_ready, lt_ready, u_seed, u_ready, kd_ready, v_turned, vb_ready) = (
            sem(n) for n in (
                "qk_silu", "vz_silu", "sq_done", "ssq_done", "ln_done", "rn_done", "d_ready", "d_exp", "eg_ready",
                "kq_normed", "qg_ready", "dmi_ready", "db_ready", "kk_done", "at_ready", "lt_ready", "u_seed",
                "u_ready", "kd_ready", "v_turned", "vb_ready"))
        (t0_done, t_ready, ltm_ready, p1_done, p1_ready, tu_done, u_next, sp1_done, sp1_ready, su_done, us_ready) = (
            sem(n) for n in ("t0_done", "t_ready", "ltm_ready", "p1_done", "p1_ready", "tu_done", "u_next", "sp1_done",
                             "sp1_ready", "su_done", "us_ready"))
        (ks_done, r_ready, vn_done, vn_ready, so_done, s_ready, s_stored, ksq_done, qs_ready, rt_step, rt_ready,
         rt_turned, rs_ready, vns_done, vns_ready, vx_ready, os_done, os_ready, s0_scaled, sup_done, s0_new,
         s0_stored) = (sem(n) for n in (
            "ks_done", "r_ready", "vn_done", "vn_ready", "so_done", "s_ready", "s_stored", "ksq_done", "qs_ready",
            "rt_step", "rt_ready", "rt_turned", "rs_ready", "vns_done", "vns_ready", "vx_ready", "os_done", "os_ready",
            "s0_scaled", "sup_done", "s0_new", "s0_stored"))
        o_squared, osum_done, oln_done, rno_ready, rz_ready, oa_done = (sem(n) for n in (
            "o_squared", "osum_done", "oln_done", "rno_ready", "rz_ready", "oa_done"))
        sqo, rno = dd[:, 0, :], dd[:, 1, :]
        vx = put("vx", [NB, P], F32, M_W + 3528 + 3 * TOK + 3 * TOK)

        def sample3(x):
            return x[:, SEQ:TOK].rearrange("p (b t) -> p b t", b=NB)

        take = area(M_W + 4096, M_W + 8192)
        ab_raw = take("ab_raw", [KT, 16])
        ab_f = take("ab_f", [KT, 64])
        ab_hi = take("ab_hi", [KT, 64], F32R)
        ab_lo = take("ab_lo", [KT, 64], F32R)
        take = area(M_B, M_B + 10 * TOK)
        r_x, r_e, r_w, r_l, r_g, r_h = (take(f"r_{n}", [TOK]) for n in "xewlgh")
        r_beta, r_egl, r_nb = (take(f"r_{n}", [TOK]) for n in ("beta", "egl", "nb"))
        head_col = take("head_col", [4])
        ab_loaded, ab_zero, ab_ready, ab_high, ab_low, ab_done, rowa, rowd, col_turned, cols_ready = (sem(n) for n in (
            "ab_loaded", "ab_zero", "ab_ready", "ab_high", "ab_low", "ab_done", "rowa", "rowd", "col_turned",
            "cols_ready"))
        H_ = slice(0, HEADS)

        def sp_rows(sp, q):
            if q == 0:
                sp.wait_ge(x_turned, 48)
                sp.wait_ge(xts_stored, 80)
                with nc.allow_non_contiguous_dma(reason="16 columns"):
                    sp.dma_start(ab_raw[:], w_in[:, :, COL_A:COL_A + 16]).then_inc(ab_loaded, 16)
                    sp.wait_ge(tile_done, 32)
                    sp.dma_start(head_col[H_, 0:1], t["dt_bias"].rearrange("o h -> h o")).then_inc(ab_loaded, 16)
                    sp.dma_start(head_col[H_, 1:2], t["a_log"].rearrange("o h -> h o")).then_inc(ab_loaded, 16)
            if q == 3:
                sp.wait_ge(row_ready, 1)
                sp.dma_start(row_d[0], r_g[H_, :]).then_inc(row_stored, 16)
                sp.dma_start(row_d[1], r_beta[H_, :]).then_inc(row_stored, 16)

        def pool_rows(pool):
            pool.wait_ge(x_turned, 48)
            pool.memset(ab_f[:], 0.0).then_inc(ab_zero, 1)
            pool.wait_ge(ab_zero, 1)
            pool.wait_ge(ab_loaded, 48)
            pool.tensor_copy(ab_f[:, :, 0:8], ab_raw[:, :, 0:8])
            pool.tensor_copy(ab_f[:, :, 32:40], ab_raw[:, :, 8:16]).then_inc(ab_ready, 1)

        def pe_rows(pe):
            pe.wait_ge(ab_low, 1)
            pe.wait_ge(mst_ready, 32)
            for k in range(KT):
                for m, (wt, x) in enumerate(((ab_hi, a_hi), (ab_hi, a_lo), (ab_lo, a_hi))):
                    for b in range(2):
                        mm = pe.matmul(dk[0:64, b, 0:HALF], wt[:, k, :], x[:, k, b * HALF:(b + 1) * HALF],
                                       start=(k == 0 and m == 0), stop=(k == KT - 1 and m == 2))
            mm.then_inc(ab_done, 1)

        def act_rows(act, q):
            na = [0]

            def step(ins):
                na[0] += 1
                ins.then_inc(rowa, 1)
                act.wait_ge(rowa, ACT_ROWS_BEFORE[q] + na[0])
            if q == 0:
                act.wait_ge(ab_ready, 1)
                act.activation(ab_hi[:], ab_f[:], ACT.Copy).then_inc(ab_high, 1)
                step(act.activation(head_col[H_, 2:3], head_col[H_, 1:2], ACT.Exp))
                step(act.activation(head_col[H_, 3:4], head_col[H_, 2:3], ACT.Copy, scale=-1.0))
            if q == 1:
                act.wait_ge(ab_done, 1)
                step(act.activation(halves(r_x[H_, :]), dk[H_, 0:2, 0:HALF], ACT.Identity, bias=head_col[H_, 0:1]))
                step(act.activation(halves(r_beta[H_, :]), dk[32:40, 0:2, 0:HALF], ACT.Sigmoid))
                step(act.activation(r_e[H_, :], r_x[H_, :], ACT.Abs))
                step(act.activation(r_e[H_, :], r_e[H_, :], ACT.Exp, scale=-1.0))
                act.wait_ge(rowd, 1)
                step(act.activation(r_l[H_, :], r_w[H_, :], ACT.Ln))
            if q == 2:
                act.wait_ge(rowd, ROWD_GC)
                step(act.activation(r_nb[H_, :], r_g[H_, :], ACT.Exp))
                step(act.activation(r_egl[H_, :], r_egl[H_, :], ACT.Exp))
        ACT_ROWS_BEFORE = {0: 0, 1: 2, 2: 7}

        def dve_rows(dve, q):
            def step(ins):
                rd[0] += 1
                ins.then_inc(rowd, 1)
                dve.wait_ge(rowd, rd[0])
            if q == 0:
                dve.wait_ge(ab_high, 1)
                dve.tensor_tensor(ab_lo[:], ab_f[:], ab_hi[:].bitcast(F32), ALU.subtract).then_inc(ab_low, 1)
            if q == 1:
                x, e, w, l, g, u = (r[H_, :] for r in (r_x, r_e, r_w, r_l, r_g, r_h))
                dve.wait_ge(rowa, 6)
                step(dve.tensor_scalar(w, e, 1.0, None, ALU.add))
                step(dve.tensor_scalar(g, w, 1.0, None, ALU.is_equal))
                step(dve.scalar_tensor_tensor(u, w, -1.0, g, ALU.add, ALU.add))
                step(dve.reciprocal(u, u))
                dve.wait_ge(rowa, 7)
                step(dve.tensor_tensor(l, l, g, ALU.add))
                step(dve.tensor_tensor(l, l, u, ALU.mult))
                step(dve.tensor_tensor(l, l, e, ALU.mult))
                step(dve.scalar_tensor_tensor(l, x, 0.0, l, ALU.max, ALU.add))
                step(dve.tensor_scalar(g, l, head_col[H_, 3:4], None, ALU.mult))
                src, dst = g, u
                for s in (1, 2, 4, 8, 16, 32, 64, 128):
                    if s < 128:
                        a, b = (r[:, 0:SEQ].rearrange("p (c n) -> p c n", c=CH) for r in (src, dst))
                        dve.tensor_copy(b[:, :, 0:s], a[:, :, 0:s])
                        dve.tensor_tensor(b[:, :, s:P], a[:, :, s:P], a[:, :, 0:P - s], ALU.add)
                    else:
                        dve.tensor_copy(dst[:, 0:SEQ], src[:, 0:SEQ])
                    a, b = (r[:, SEQ:TOK].rearrange("p (c n) -> p c n", c=NB) for r in (src, dst))
                    m = s if s < NT else NT
                    last = dve.tensor_copy(b[:, :, 0:m], a[:, :, 0:m])
                    if s < NT:
                        last = dve.tensor_tensor(b[:, :, s:NT], a[:, :, s:NT], a[:, :, 0:NT - s], ALU.add)
                    step(last)
                    src, dst = dst, src
                a, b = (r[H_, 0:SEQ].rearrange("p (c n) -> p c n", c=CH) for r in (r_g, r_egl))
                dve.tensor_tensor(b, a[:, :, P - 1:P].to_broadcast([HEADS, CH, P]), a, ALU.subtract)
                a, b = (r[H_, SEQ:TOK].rearrange("p (c n) -> p c n", c=NB) for r in (r_g, r_egl))
                step(dve.tensor_tensor(b, a[:, :, NT - 1:NT].to_broadcast([HEADS, NB, NT]), a, ALU.subtract))
                assert rd[0] == ROWD_GC
            if q == 2:
                dve.wait_ge(rowa, 9)
                dve.scalar_tensor_tensor(r_nb[H_, :], r_nb[H_, :], -1.0, r_beta[H_, :], ALU.mult, ALU.mult).then_inc(row_ready, 1)
            if q == 3:
                dve.wait_ge(col_turned, 1)
                dve.tensor_copy(cols[:, :, 0:4, :], dk[:, 2, 0:128].rearrange("p (q b h) -> p q b h", q=4, b=4))
                dve.tensor_copy(cols[S_, :, 4, :], dk[S_, 2, 128:160].rearrange("p (q h) -> p q h", q=4)).then_inc(cols_ready, 1)
        rd = [0]
        ROWD_GC = 18

        def pe_cols(pe):
            pe.wait_ge(row_ready, 1)
            for i, r in enumerate((r_g, r_beta, r_egl, r_nb)):
                for b in range(4):
                    pe.transpose(dk[:, 2, i * 32 + b * 8:i * 32 + b * 8 + 8], r[H_, b * P:(b + 1) * P], ident[H_, H_])
                mm = pe.transpose(dk[S_, 2, 128 + i * 8:136 + i * 8], r[H_, SEQ:TOK], ident[H_, H_])
            mm.then_inc(col_turned, 1)

        def ext_prompt(x):
            return x[:, 3:3 + SEQ]

        def ext_sample(x):
            return x[:, 3 + SEQ:EXTN].rearrange("p (b s) -> p b s", b=NB)

        def pool_ext(pool, h, q):
            if isinstance(h, int) and h == 0 and q == 0:
                pool.wait_ge(x_turned, 48)
                pool.memset(ext[:, 0:3], 0.0)
            at_least(pool, conv_done, 3 * h + q)
            at_least(pool, ext_turned, 3 * h + q)
            pool.tensor_copy(ext_sample(ext)[:, :, 0:3], sct[:, q, bass.ds(h, 1), :, :]).then_inc(ext_state, 1)

        def pool_last(pool, h, q):
            pool.wait_ge(pj_read, 4 * (8 + h) + q + 1)
            at_least(pool, ext_turned, 3 * h + q)
            pool.tensor_tensor(ecol[:], ext_sample(ext)[:, :, NT:CSEG], ones[:, 0:3 * NB].rearrange("p (b j) -> p b j", b=NB),
                               ALU.mult).then_inc(ecol_ready, 1)

        def act_take(act, h, q):
            act.wait_ge(tile_done, 4 * (8 + h) + q + 1)
            if q == 3:
                at_least(act, vz_silu, h)
                if isinstance(h, int) and h == 0:
                    act.wait_ge(tile_done, 32)
                act.activation(halves(zraw[:]), product(q), ACT.Copy).then_inc(pj_read, 1)
                return
            b = 2 * (q % 2)
            act.wait_ge(ext_state, 3 * h + q + 1)
            act.activation(ext[:, 3:3 + HALF], pj[:, b, 0:HALF], ACT.Copy)
            act.activation(ext[:, 3 + HALF:3 + SEQ], pj[:, b + 1, 0:SEQ - HALF], ACT.Copy)
            act.activation(ext_sample(ext)[:, :, 3:CSEG],
                           pj[:, b + 1, SEQ - HALF:HALF].rearrange("p (b t) -> p b t", b=NB), ACT.Copy).then_inc(pj_read, 1)

        def pe_ext(h, q):
            def step(pe):
                pe.wait_ge(ecol_ready, 3 * h + q + 1)
                pe.transpose(pj[0:3, 2 * (q % 2), 0:P], ext[:, SEQ:SEQ + 3], ident)
                pe.transpose(pj[0:24, 2 * (q % 2), P:2 * P], ecol[:].rearrange("p b j -> p (b j)"), ident).then_inc(ext_turned, 1)
            return step

        def act_st(act, h, q):
            act.wait_ge(ext_turned, 3 * h + q + 1)
            at_least(act, st_stored, 96 * h)
            act.activation(st[0:3, q, 0, :], pj[0:3, 2 * (q % 2), 0:P], ACT.Copy)
            act.activation(st[0:24, q, 1, :], pj[0:24, 2 * (q % 2), P:2 * P], ACT.Copy).then_inc(st_ready, 1)

        def sp_st(sp, h, q):
            sp.wait_ge(st_ready, 3 * h + q + 1)
            c = bass.ds((h + 1) * P + (q * MIX - P), P)
            sp.dma_start(t["conv_prompt"][0, 0, :, c], st[0:3, q, 0, :]).then_inc(st_stored, 16)
            sp.dma_start(t["conv_sample"].rearrange("o b j n -> (o b j) n")[:, c], st[0:24, q, 1, :]).then_inc(st_stored, 16)

        def dve_conv(dve, h, q):
            if q == 0:
                at_least(dve, conv_done, 3 * h)
                dve.tensor_copy(hw[:], convw[:, :, :, bass.ds(h, 1)].rearrange("p j g o -> p j (g o)")).then_inc(hw_ready, 1)
                dve.wait_ge(hw_ready, h + 1)
            dve.wait_ge(pj_read, 4 * (8 + h) + q + 1)
            at_least(dve, qk_silu if q < 2 else vz_silu, h)
            y = yq[:, q, 0:YN]
            dve.tensor_scalar(y, ext[:, 0:YN], hw[:, 0, q:q + 1], None, ALU.mult).then_inc(conv_step, 1)
            for j in range(1, 4):
                dve.wait_ge(conv_step, 9 * h + 3 * q + j)
                a = dve.scalar_tensor_tensor(y, ext[:, j:j + YN], hw[:, j, q:q + 1], y, ALU.mult, ALU.add)
                a.then_inc(conv_step if j < 3 else conv_done, 1)

        def act_delta(act, n, q):
            if q == 0:
                at_least(act, oa_done, n)
                act.wait_ge(conv_done, 3 * n + 3)
                for y, o in ((yq[:, 0], kq[:, 1]), (yq[:, 1], kq[:, 0])):
                    act.activation(o[:, 0:SEQ], y[:, 0:SEQ], ACT.Silu)
                    a = act.activation(sample3(o), ext_sample(y)[:, :, 0:NT], ACT.Silu)
                a.then_inc(qk_silu, 1)
                act.wait_ge(qk_silu, n + 1)
                act.activation(SQ[:], kq[:, 0:2], ACT.Square).then_inc(sq_done, 1)
                act.activation(vs[:, 0:SEQ], yq[:, 2, 0:SEQ], ACT.Silu)
                act.activation(sample3(vs), ext_sample(yq[:, 2])[:, :, 0:NT], ACT.Silu)
                act.wait_ge(pj_read, 4 * (8 + n) + 4)
                act.activation(zs[:], zraw[:], ACT.Silu).then_inc(vz_silu, 1)
                act.wait_ge(ssq_done, n + 1)
                act.activation(rn.rearrange("p (b m) -> p b m", b=4), dk[:, 0:4, 0:HALF], ACT.Ln, bias=eps_col).then_inc(ln_done, 1)
                act.wait_ge(ln_done, n + 1)
                act.activation(rn[:, 0:TOK], rn[:, 0:TOK], ACT.Exp, scale=-0.5)
                act.activation(rn[:, TOK:2 * TOK], rn[:, TOK:2 * TOK], ACT.Exp, scale=-0.5,
                               bias=cst[:, C_LNQ:C_LNQ + 1]).then_inc(rn_done, 1)
                act.wait_ge(d_ready, n + 1)
                act.activation(dd[:, 0, 0:SEQ], dd[:, 0, 0:SEQ], ACT.Exp)
                act.activation(ds_[S_, :], ds_[S_, :], ACT.Exp).then_inc(d_exp, 1)
                act.activation(gcb[:], gcb[:], ACT.Exp).then_inc(eg_ready, 1)
            if q == 1:
                act.wait_ge(t0_done, n + 1)
                act.activation(tt_, dk[:, 0, :].rearrange("p (c n) -> p c n", c=CH), ACT.Copy)
                act.activation(ts_[S_, :], dk[S_, 1, 0:NS], ACT.Copy).then_inc(t_ready, 1)
            for l in range(1, LEVELS):
                if LEVEL_PHASE[l] == q:
                    act.wait_ge(p1_done, 6 * n + l)
                    act.activation(p1, dk[:, 0, :].rearrange("p (c n) -> p c n", c=CH), ACT.Copy).then_inc(p1_ready, 1)
                    if l == 1:
                        act.wait_ge(sp1_done, n + 1)
                        act.activation(p1s[S_, :], dk[S_, 3, 0:NS], ACT.Copy).then_inc(sp1_ready, 1)
            if q == 3:
                act.wait_ge(so_done, 4 * n + 4)
                act.wait_ge(vx_ready, n + 1)
                act.wait_ge(sup_done, n + 1)
                act.activation(sqo[:, 0:SEQ], dk[:, 3, :], ACT.Square)
                act.wait_ge(os_ready, n + 1)
                act.activation(sqo[:, SEQ:TOK], os_, ACT.Square).then_inc(o_squared, 1)
                act.wait_ge(osum_done, n + 1)
                act.activation(halves(rno), dk[:, 0:2, 0:HALF], ACT.Ln, scale=1.0 / P, bias=eps_col).then_inc(oln_done, 1)
                act.wait_ge(oln_done, n + 1)
                act.activation(rno, rno, ACT.Exp, scale=-0.5).then_inc(rno_ready, 1)


        LEVEL_PHASE = {l: 1 if l < 4 else 2 for l in range(1, LEVELS)}

        def dve_delta(dve, n, q):
            if q == 0:
                at_least(dve, oa_done, n)
                dve.wait_ge(cols_ready, 1)
                dve.tensor_copy(hc[:, :, 0:4], cols[:, :, 0:4, bass.ds(n, 1)].rearrange("p q b o -> p q (b o)"))
                dve.tensor_copy(hc[S_, :, 4:5], cols[S_, :, 4, bass.ds(n, 1)]).then_inc(hc_ready, 1)
                dve.wait_ge(hc_ready, n + 1)
                dve.wait_ge(row_loaded, 32 * n + 32)
                for c in range(CH):
                    dve.tensor_scalar(d_[:, c, :], gcb[:, c * P:(c + 1) * P], hc[:, 0, c:c + 1], 0.0, ALU.subtract, ALU.min)
                dve.tensor_scalar(ds_[S_, :], gcb[S_, SEQ:TOK], hc[S_, 0, 4:5], 0.0, ALU.subtract, ALU.min).then_inc(d_ready, 1)
                dve.wait_ge(rn_done, n + 1)
                dve.tensor_tensor(kq[:, 0:2].rearrange("p r n -> p (r n)"), kq[:, 0:2].rearrange("p r n -> p (r n)"), rn,
                                  ALU.mult).then_inc(kq_normed, 1)
                dve.wait_ge(eg_ready, n + 1)
                dve.wait_ge(kq_normed, n + 1)
                dve.tensor_tensor(kq[:, 2], kq[:, 1], gcb[:], ALU.mult).then_inc(qg_ready, 1)
            if q == 1:
                kk = dk[:, 0:2, :].rearrange("p b (c n) -> p (b c) n", n=2 * P)
                dve.wait_ge(kk_done, n + 1)
                dve.wait_ge(db_ready, n + 1)
                dve.tensor_tensor(at_[:], kk[:, :, P:2 * P], d_, ALU.mult)
                dve.tensor_tensor(ats[S_, :], dk[S_, 2, NS:2 * NS], ds_[S_, :], ALU.mult).then_inc(at_ready, 1)
                dve.tensor_tensor(lt[:], kk[:, :, 0:P], db_, ALU.mult)
                dve.tensor_tensor(lts[S_, :], dk[S_, 2, 0:NS], dbs[S_, :], ALU.mult).then_inc(lt_ready, 1)
                dve.wait_ge(lt_ready, n + 1)
                dve.tensor_tensor(uu, lt[:], per_chunk(lev(0)), ALU.mult)
                dve.tensor_tensor(us[S_, :], lts[S_, :], cst[S_, C_SL1:C_SL1 + NS], ALU.mult).then_inc(u_seed, 1)
                dve.wait_ge(u_seed, n + 1)
                dve.tensor_tensor(uu, uu, per_chunk(ident), ALU.add)
                dve.tensor_tensor(us[S_, :], us[S_, :], ident[S_, S_], ALU.add).then_inc(u_ready, 1)
                dve.tensor_tensor(kd, dk[:, 3, :].rearrange("p (c n) -> p c n", c=CH),
                                  hc[:, 2, 0:4].unsqueeze(2).to_broadcast([P, CH, P]), ALU.mult)
                dve.tensor_scalar(kds[S_, :], dk[S_, 2, P:2 * P], hc[S_, 2, 4:5], None, ALU.mult).then_inc(kd_ready, 1)
                dve.wait_ge(v_turned, n + 1)
                dve.tensor_tensor(vb, dk[:, 3, :].rearrange("p (c n) -> p c n", c=CH),
                                  hc[:, 1, 0:4].unsqueeze(2).to_broadcast([P, CH, P]), ALU.mult).then_inc(vb_ready, 1)
            for l in range(1, LEVELS):
                if LEVEL_PHASE[l] == q:
                    dve.wait_ge(tu_done, 6 * n + l)
                    if l < LEVELS - 1:
                        dve.tensor_tensor(tt_, tt_, dk[:, 1, :].rearrange("p (c n) -> p c n", c=CH), ALU.subtract)
                    dve.tensor_tensor(uu, uu, dk[:, 2, :].rearrange("p (c n) -> p c n", c=CH), ALU.subtract).then_inc(u_next, 1)
                    if l == 2:
                        dve.wait_ge(su_done, n + 1)
                        dve.tensor_tensor(us[S_, :], us[S_, :], dk[S_, 3, NS:2 * NS], ALU.subtract).then_inc(us_ready, 1)
            if q == 3:
                for c in range(CH):
                    if c > 0:
                        dve.wait_ge(ks_done, 3 * n + c)
                        dve.scalar_tensor_tensor(rr[:], dk[:, 0, 0:P], hc[:, 3, c:c + 1], vb[:, c, :], ALU.mult,
                                                 ALU.add).then_inc(r_ready, 1)
                    dve.wait_ge(vn_done, 4 * n + c + 1)
                    if c == 0:
                        at_least(dve, s_stored, 16 * n)
                    dve.tensor_copy(vn[:], dk[:, 1, 0:P]).then_inc(vn_ready, 1)
                    if c == 1:
                        sample_r(dve, n)
                    if c == 2:
                        dve.wait_ge(rt_turned, n + 1)
                        dve.tensor_copy(rs_s[S_, :], dk[S_, 2, P:2 * P]).then_inc(rs_ready, 1)
                    if c == 3:
                        dve.wait_ge(vns_done, n + 1)
                        dve.tensor_copy(vns[S_, :], dk[S_, 0, P:2 * P]).then_inc(vns_ready, 1)
                    dve.wait_ge(so_done, 4 * n + c + 1)
                    if c == 0:
                        dve.tensor_copy(sst[:, 0, :], dk[:, 2, 0:P]).then_inc(s_ready, 1)
                    else:
                        dve.scalar_tensor_tensor(sst[:, c % 2, :], sst[:, (c + 1) % 2, :], gcb[:, c * P + P - 1:c * P + P],
                                                 dk[:, 2, 0:P], ALU.mult, ALU.add).then_inc(s_ready, 1)
                dve.wait_ge(os_done, n + 1)
                dve.tensor_tensor(os_, qs_, dk[:, 2, P:P + NS], ALU.add).then_inc(os_ready, 1)
                dve.wait_ge(sup_done, n + 1)
                dve.wait_ge(s0_scaled, n + 1)
                dve.tensor_tensor(s0[:].rearrange("p (r b) n -> p r (b n)", r=2), s0[:].rearrange("p (r b) n -> p r (b n)", r=2),
                                  dk[:, 0:2, :], ALU.add).then_inc(s0_new, 1)
                dve.wait_ge(rz_ready, n + 1)
                g = gain[:, G_GDN:G_GDN + 1]
                o = mixo[:, bass.ds(n, 1), :].rearrange("p o n -> p (o n)")
                dve.scalar_tensor_tensor(o[:, 0:SEQ], dk[:, 3, :], g, rno[:, 0:SEQ], ALU.mult, ALU.mult)
                dve.scalar_tensor_tensor(o[:, SEQ:TOK], os_, g, rno[:, SEQ:TOK], ALU.mult, ALU.mult).then_inc(oa_done, 1)

        def sample_r(dve, n):
            dve.wait_ge(ksq_done, n + 1)
            ks = dk[:, 2, 256:320].rearrange("p (b r t) -> p b r t", b=NB, r=2)
            dve.tensor_tensor(tmp.rearrange("p (b t) -> p b t", b=NB), ks[:, :, 0, :], sample3(gcb[:]), ALU.mult)
            dve.tensor_copy(qs_.rearrange("p (b t) -> p b t", b=NB), ks[:, :, 1, :]).then_inc(rt_step, 1)
            dve.wait_ge(rt_step, 2 * n + 1)
            dve.tensor_tensor(tmp, vs[:, SEQ:TOK], tmp, ALU.subtract).then_inc(rt_step, 1)
            dve.wait_ge(rt_step, 2 * n + 2)
            dve.tensor_tensor(rt, tmp, betab[:, SEQ:TOK], ALU.mult).then_inc(rt_ready, 1)

        def pool_delta(pool, n, q):
            if q == 0:
                pool.wait_ge(d_exp, n + 1)
                pool.wait_ge(row_loaded, 32 * n + 32)
                pool.tensor_tensor(d_, d_, per_chunk(incl), ALU.mult)
                pool.tensor_tensor(ds_[S_, :], ds_[S_, :], cst[S_, C_SINCL:C_SINCL + NS], ALU.mult).then_inc(dmi_ready, 1)
                pool.wait_ge(dmi_ready, n + 1)
                pool.tensor_tensor(db_, d_, betab[:, 0:SEQ].rearrange("p (c n) -> p c n", c=CH), ALU.mult)
                pool.tensor_tensor(dbs[S_, :], ds_[S_, :], betab[S_, SEQ:TOK], ALU.mult).then_inc(db_ready, 1)
            if q == 1:
                pool.wait_ge(lt_ready, n + 1)
                pool.tensor_tensor(slm[S_, :], lts[S_, :], cst[S_, C_SL2:C_SL2 + NS], ALU.mult).then_inc(slm_ready, 1)
            for l in range(1, LEVELS):
                if LEVEL_PHASE[l] == q:
                    pool.wait_ge(lt_ready, n + 1)
                    at_least(pool, p1_done, 6 * n + l - 1)
                    pool.tensor_tensor(ltm[:], lt[:], per_chunk(lev(l)), ALU.mult).then_inc(ltm_ready, 1)
            if q == 3:
                pool.wait_ge(ksq_done, n + 1)
                pool.wait_ge(s0_loaded, 16 * n + 16)
                pool.tensor_tensor(s0[:], s0[:], sample3(gcb[:])[:, :, NT - 1:NT].to_broadcast([P, NB, P]),
                                   ALU.mult).then_inc(s0_scaled, 1)
                pool.wait_ge(vns_ready, n + 1)
                pool.tensor_tensor(vx[S_, :, :], vns[S_, :].unsqueeze(1).to_broadcast([NS, NB, P]),
                                   cst[S_, C_BM:C_BM + NB].unsqueeze(2).to_broadcast([NS, NB, P]), ALU.mult).then_inc(vx_ready, 1)
                pool.wait_ge(rno_ready, n + 1)
                pool.tensor_tensor(rno, rno, zs[:], ALU.mult).then_inc(rz_ready, 1)

        def pe_delta(n):
            chunk = lambda x, c: x[:, c * P:(c + 1) * P]

            def norms(pe):
                pe.wait_ge(sq_done, n + 1)
                at_least(pe, oa_done, n)
                at_least(pe, s0_new, n)
                for i in range(4):
                    mm = pe.matmul(dk[:, i, 0:HALF], ones, SQ[:, i // 2, (i % 2) * HALF:(i % 2 + 1) * HALF], start=True, stop=True)
                mm.then_inc(ssq_done, 1)

            def gram(pe):
                pe.wait_ge(kq_normed, n + 1)
                for c in range(CH):
                    pe.matmul(dk[:, c // 2, (c % 2) * 256:(c % 2) * 256 + 256].rearrange("p (r n) -> p r n", r=2),
                              chunk(kq[:, 0], c), kq[:, 0:2, c * P:(c + 1) * P], start=True, stop=True)
                pe.matmul(dk[S_, 2, 0:2 * NS].rearrange("p (r n) -> p r n", r=2), kq[:, 0, SEQ:TOK], kq[:, 0:2, SEQ:TOK],
                          start=True, stop=True)
                pe.transpose(dk[S_, 2, P:2 * P], kq[:, 0, SEQ:TOK], ident)
                for c in range(CH):
                    mm = pe.transpose(chunk(dk[:, 3], c), chunk(kq[:, 0], c), ident)
                mm.then_inc(kk_done, 1)

            def turn_v(pe):
                pe.wait_ge(kd_ready, n + 1)
                pe.wait_ge(vz_silu, n + 1)
                for c in range(CH):
                    mm = pe.transpose(chunk(dk[:, 3], c), chunk(vs, c), ident)
                mm.then_inc(v_turned, 1)

            def turn_u(pe):
                pe.wait_ge(u_ready, n + 1)
                for c in range(CH):
                    pe.transpose(chunk(dk[:, 0], c), uu[:, c, :], ident)
                pe.transpose(dk[S_, 1, 0:NS], us[S_, :], ident[S_, S_]).then_inc(t0_done, 1)

            def level_p(l):
                def step(pe):
                    pe.wait_ge(ltm_ready, 6 * n + l)
                    if l == 1:
                        pe.wait_ge(t_ready, n + 1)
                    else:
                        pe.wait_ge(u_next, 6 * n + l - 1)
                    if l == 1:
                        pe.wait_ge(vb_ready, n + 1)
                        pe.wait_ge(slm_ready, n + 1)
                    for c in range(CH):
                        mm = pe.matmul(chunk(dk[:, 0], c), ltm[:, c, :], tt_[:, c, :], start=True, stop=True)
                    mm.then_inc(p1_done, 1)
                    if l == 1:
                        pe.matmul(dk[S_, 3, 0:NS], slm[S_, :], ts_[S_, :], start=True, stop=True).then_inc(sp1_done, 1)
                return step

            def level_u(l):
                def step(pe):
                    pe.wait_ge(p1_ready, 6 * n + l)
                    if l == 2:
                        pe.wait_ge(sp1_ready, n + 1)
                    if l < LEVELS - 1:
                        for c in range(CH):
                            pe.matmul(chunk(dk[:, 1], c), uu[:, c, :], p1[:, c, :], start=True, stop=True)
                    for c in range(CH):
                        mm = pe.matmul(chunk(dk[:, 2], c), p1[:, c, :], uu[:, c, :], start=True, stop=True)
                    mm.then_inc(tu_done, 1)
                    if l == 2:
                        pe.matmul(dk[S_, 3, NS:2 * NS], p1s[S_, :], us[S_, :], start=True, stop=True).then_inc(su_done, 1)
                return step

            def state_k(c):
                def step(pe):
                    pe.wait_ge(s_ready, 4 * n + c)
                    pe.matmul(dk[:, 0, 0:P], chunk(kq[:, 0], c), sst[:, (c + 1) % 2, :], start=True, stop=True).then_inc(ks_done, 1)
                return step

            def v_new(c):
                def step(pe):
                    if c == 0:
                        pe.wait_ge(u_next, 6 * n + 6)
                        pe.wait_ge(us_ready, n + 1)
                        pe.wait_ge(qg_ready, n + 1)
                        pe.wait_ge(at_ready, n + 1)
                    else:
                        pe.wait_ge(r_ready, 3 * n + c)
                    pe.matmul(dk[:, 1, 0:P], uu[:, c, :], vb[:, 0, :] if c == 0 else rr[:], start=True, stop=True).then_inc(vn_done, 1)
                return step

            def state_o(c):
                def step(pe):
                    pe.wait_ge(vn_ready, 4 * n + c + 1)
                    if c == 1:
                        pe.wait_ge(rt_step, 2 * n + 1)
                    if c == 2:
                        pe.wait_ge(rs_ready, n + 1)
                    pe.matmul(dk[:, 2, 0:P], kd[:, c, :], vn[:], start=True, stop=True)
                    if c > 0:
                        pe.matmul(chunk(dk[:, 3], c), sst[:, (c + 1) % 2, :], chunk(kq[:, 2], c), start=True, stop=False)
                    pe.matmul(chunk(dk[:, 3], c), vn[:], at_[:, c, :], start=(c == 0), stop=True).then_inc(so_done, 1)
                return step

            def sample_ks(pe):
                pe.wait_ge(s0_loaded, 16 * n + 16)
                pe.wait_ge(s_ready, 4 * n + 1)
                for b in range(NB):
                    mm = pe.matmul(dk[:, 2, 256 + 8 * b:264 + 8 * b].rearrange("p (r t) -> p r t", r=2), s0[:, b, :],
                                   kq[:, 0:3:2, SEQ + NT * b:SEQ + NT * (b + 1)], start=True, stop=True)
                mm.then_inc(ksq_done, 1)

            def sample_turn(pe):
                pe.wait_ge(rt_ready, n + 1)
                pe.wait_ge(s_ready, 4 * n + 2)
                pe.transpose(dk[S_, 2, P:2 * P], rt, ident).then_inc(rt_turned, 1)

            def sample_v(pe):
                pe.matmul(dk[S_, 0, P:2 * P], us[S_, :], rs_s[S_, :], start=True, stop=True).then_inc(vns_done, 1)

            def sample_o(pe):
                pe.wait_ge(vns_ready, n + 1)
                pe.wait_ge(s_ready, 4 * n + 4)
                pe.matmul(dk[:, 2, P:P + NS], vns[S_, :], ats[S_, :], start=True, stop=True).then_inc(os_done, 1)

            def sample_s(pe):
                pe.wait_ge(vx_ready, n + 1)
                for r in range(2):
                    mm = pe.matmul(dk[:, r, :], kds[S_, :], vx[S_, 4 * r:4 * r + 4, :].rearrange("p b n -> p (b n)"),
                                   start=True, stop=True)
                mm.then_inc(sup_done, 1)

            def o_norm(pe):
                pe.wait_ge(o_squared, n + 1)
                pe.wait_ge(s0_new, n + 1)
                for b in range(2):
                    mm = pe.matmul(dk[:, b, 0:HALF], ones, sqo[:, b * HALF:(b + 1) * HALF], start=True, stop=True)
                mm.then_inc(osum_done, 1)

            return [norms, gram, turn_v, turn_u] + [f(l) for l in range(1, LEVELS) for f in (level_p, level_u)] + [
                v_new(0), state_o(0), sample_ks, state_k(1), v_new(1), state_o(1), state_k(2), sample_turn, v_new(2),
                state_o(2), state_k(3), v_new(3), sample_v, state_o(3), sample_o, sample_s, o_norm]

        PLACE = [(0, 10), (1, 0), (1, 4), (1, 5)] + [(1, 7), (1, 8), (1, 10), (1, 11), (1, 13), (1, 15),
                 (2, 1), (2, 3), (2, 5), (2, 7), (2, 10), (2, 12)] + [
                 (3, 0), (3, 1), (3, 1), (3, 2), (3, 3), (3, 4), (3, 5), (3, 5), (3, 6), (3, 7), (3, 8), (3, 9), (3, 9),
                 (3, 10), (3, 11), (3, 12), (3, 14)]

        def delta_steps(n):
            steps = [{}, {}, {}, {}]
            for (q, k), f in zip(PLACE, pe_delta(n)):
                steps[q].setdefault(k, []).append(f)
            return steps

        def sp_delta(sp, n, q):
            if q == 0:
                at_least(sp, oa_done, n)
                for i, o in enumerate((gcb, betab)):
                    sp.dma_start(o[:], row_d[i, bass.ds(n, 1), :].to_broadcast([P, TOK])).then_inc(row_loaded, 16)
                at_least(sp, s0_stored, 16 * n)
                sp.dma_start(s0[:], t["state_delta"][0, :, bass.ds(n, 1), :, :].rearrange("b o k v -> k (b o) v")).then_inc(s0_loaded, 16)

        def sp_delta_out(sp, n):
            sp.wait_ge(s_ready, 4 * n + 4)
            sp.dma_start(t["delta_prompt"][0, 0, bass.ds(n, 1), :, :].rearrange("o k v -> k (o v)"), sst[:, 1, :]).then_inc(s_stored, 16)
            sp.wait_ge(s0_new, n + 1)
            sp.dma_start(t["delta_sample"][0, :, bass.ds(n, 1), :, :].rearrange("b o k v -> k (b o) v"), s0[:]).then_inc(s0_stored, 16)

        def loop_heads(eng, body, peel_last=False):
            body(0)
            body(1)
            with eng.Fori(2, HEADS - 1 if peel_last else HEADS) as h:
                body(h)
            if peel_last:
                body(HEADS - 1)

        def is_first(h):
            return isinstance(h, int) and h == 0

        def sp_heads(sp):
            def body(h):
                for q in range(4):
                    load_ahead(sp, "head", h, q)
                    if is_first(h):
                        if q == 1:
                            store_k_or_v(sp, 7, True)
                        sp_rows(sp, q)
                    else:
                        if q == 0:
                            sp.wait_ge(row_stored, 32)
                        sp_delta(sp, h - 1, q)
                    if q > 0:
                        sp_st(sp, h, q - 1)
                    if q == 3 and not is_first(h):
                        sp_delta_out(sp, h - 1)
            loop_heads(sp, body, True)

        def act_heads(act):
            def body(h):
                for q in range(4):
                    cast_high(act, "head", h, q + 1)
                    if is_first(h):
                        act_rows_all(act, q)
                        if q == 3:
                            act.wait_ge(mst_stored, 128)
                    if q > 0:
                        act_st(act, h, q - 1)
                    if not is_first(h):
                        act_delta(act, h - 1, q)
                    act_take(act, h, q)
            loop_heads(act, body)

        def act_rows_all(act, q):
            if q in ACT_ROWS_BEFORE:
                act_rows(act, q)

        def dve_heads(dve):
            def body(h):
                for q in range(4):
                    split_low(dve, "head", h, q + 1)
                    if is_first(h):
                        dve_rows(dve, q)
                        if q == 3:
                            dve.wait_ge(mst_stored, 128)
                    else:
                        dve_delta(dve, h - 1, q)
                    if q > 0:
                        dve_conv(dve, h, q - 1)
            loop_heads(dve, body)

        def pool_heads(pool):
            pool_rows(pool)

            def body(h):
                for q in range(4):
                    if q > 0:
                        pool_last(pool, h, q - 1)
                    if is_first(h) and q == 3:
                        pool.wait_ge(mst_stored, 128)
                    if not is_first(h):
                        pool_delta(pool, h - 1, q)
                    if q < 3:
                        pool_ext(pool, h, q)
            loop_heads(pool, body)

        def pe_heads(pe):
            def body(h):
                steps = delta_steps(h - 1) if not is_first(h) else [{0: [pe_rows]}, {}, {}, {4: [pe_cols]}]
                for q in range(4):
                    if q > 0:
                        steps[q].setdefault(2, []).append(pe_ext(h, q - 1))
                    at_least(pe, st_ready, (3 * h, 0, 3 * h + 1, 3 * h + 2)[q])
                    multiply(pe, "head", h, q, tokens(a_hi), tokens(a_lo), TOK, steps[q])
            loop_heads(pe, body)

        take = area(M_W, M_W + 3528)
        ux = take("ux", [UN])
        us_a = take("us_a", [UN])
        us_b = take("us_b", [UN])
        dpool = take("dpool", [2, TOK])
        take = area(M_W + 3528, M_HIMIX)
        pw = take("pw", [2, 2, P])
        take = area(M_END - 576, M_END)
        spool = take("spool", [2 * P])
        ust = take("ust", [2, P])
        ucol = take("ucol", [NS])
        mix_hi = put("mix_hi", [KT, TOK], F32R, M_HIMIX)
        mix_lo = put("mix_lo", [KT, TOK], F32R, M_B)
        (spool_loaded, spool_turned, ux_zero, ucol_ready, ux_turned, ust_ready, ust_stored, win_step, d_tile, pw_loaded,
         pooled, ob_done, mix_high, mix_low, old_rows) = (sem(n) for n in (
            "spool_loaded", "spool_turned", "ux_zero", "ucol_ready", "ux_turned", "ust_ready", "ust_stored", "win_step",
            "d_tile", "pw_loaded", "pooled", "ob_done", "mix_high", "mix_low", "old_rows"))

        def u_sample(x):
            return x[:, BUF + SEQ:UN].rearrange("p (b s) -> p b s", b=NB)

        def sp_pool(sp):
            def body(g):
                first = is_first(g)
                for q in range(4):
                    load_ahead(sp, "pool", g, q)
                    if first:
                        sp_delta(sp, HEADS - 1, q)
                    if q == 0:
                        if first:
                            sp.dma_start(t["pool_sample"][0, :, 0:BUF - NT, :], t["state_pool"][0, :, NT:BUF, :]).then_inc(old_rows, 16)
                            sp.wait_ge(ext_state, 24)
                        at_least(sp, spool_turned, 2 * g)
                        sp.dma_start(spool[0:NB * BUF, :], t["state_pool"].rearrange("o b j n -> (o b j) n")[:, bass.ds(g * 256, 256)]).then_inc(spool_loaded, 16)
                        if not first:
                            sp_ust(sp, g - 1, 1)
                            at_least(sp, oa_done, HEADS)
                            at_least(sp, pooled, g - 1)
                            for k in range(2):
                                sp.dma_start(pw[:, k], t["pool_w"][0, bass.ds(g - 1, 1), k * P:(k + 1) * P, :].rearrange(
                                    "o c (d n) -> c (o d) n", d=2)).then_inc(pw_loaded, 16)
                    if q == 3:
                        sp_ust(sp, g, 0)
                if first:
                    sp_delta_out(sp, HEADS - 1)
            for g in range(NG):
                body(g)

        def sp_ust(sp, g, i):
            sp.wait_ge(ust_ready, 2 * g + i + 1)
            c = slice(g * 256 + i * P, g * 256 + i * P + P)
            sp.dma_start(t["pool_prompt"][0, 0, :, c], ust[0:BUF, 0, :]).then_inc(ust_stored, 16)
            for b in range(NB):
                sp.dma_start(t["pool_sample"][0, b, BUF - NT:BUF, c], ust[NT * b:NT * b + NT, 1, :]).then_inc(ust_stored, 16)

        def act_pool(act):
            def body(g):
                first = is_first(g)
                for q in range(4):
                    cast_high(act, "pool", g, q + 1)
                    w = 4 * (16 + g) + q
                    if q == 0 and not first:
                        act_ust(act, g - 1, 1)
                    if q == 3:
                        act_ust(act, g, 0)
                    if first:
                        act_delta(act, HEADS - 1, q)
                    if q == 0 and g == 1:
                        act.wait_ge(s0_stored, 128)
                        act.wait_ge(s_stored, 128)
                    if g == 1 and q == 2:
                        mix_take_high(act, 0)
                    if g == 2 and q == 2:
                        mix_take_high(act, 1)
                    act.wait_ge(tile_done, w + 1)
                    if q < 2:
                        act.activation(halves(mixo[:, 8 + 2 * g + q, :]), product(q), ACT.Silu).then_inc(pj_read, 1)
                        continue
                    b, i = 2 * (q % 2), q - 2
                    at_least(act, ux_turned, 2 * g + i)
                    at_least(act, d_tile, 2 * g + i)
                    act.wait_ge(ux_zero, 1)
                    act.activation(ux[:, BUF:BUF + HALF], pj[:, b, 0:HALF], ACT.Copy)
                    act.activation(ux[:, BUF + HALF:BUF + SEQ], pj[:, b + 1, 0:SEQ - HALF], ACT.Copy)
                    act.activation(u_sample(ux)[:, :, BUF:USEG],
                                   pj[:, b + 1, SEQ - HALF:HALF].rearrange("p (b t) -> p b t", b=NB), ACT.Copy)
                    act.activation(u_sample(ux)[:, :, 0:BUF],
                                   pj[:, b, HALF:HALF + NB * BUF].rearrange("p (b j) -> p b j", b=NB), ACT.Copy).then_inc(pj_read, 1)
            for g in range(NG):
                body(g)

        def act_ust(act, g, i):
            act.wait_ge(ux_turned, 2 * g + i + 1)
            at_least(act, ust_stored, 16 * 9 * (2 * g + i))
            act.activation(ust[0:BUF, 0, :], pj[0:BUF, 2 * i, 0:P], ACT.Copy)
            act.activation(ust[0:NS, 1, :], pj[0:NS, 2 * i, P:2 * P], ACT.Copy).then_inc(ust_ready, 1)

        MIX_PARTS = ((0, 4), (4, 8), (8, 14), (14, 16))

        def mix_take_high(act, m):
            a, b = MIX_PARTS[m]
            if m < 2:
                act.wait_ge(oa_done, HEADS)
            else:
                act.wait_ge(ob_done, 2 * (m + 1))
            if m == 2:
                act.wait_ge(ust_stored, 16 * 9 * 7)
            act.activation(mix_hi[:, a:b, :], mixo[:, a:b, :], ACT.Copy).then_inc(mix_high, 1)

        def mix_take_low(dve, m):
            a, b = MIX_PARTS[m]
            dve.wait_ge(mix_high, m + 1)
            dve.tensor_tensor(mix_lo[:, a:b, :], mixo[:, a:b, :], mix_hi[:, a:b, :].bitcast(F32), ALU.subtract).then_inc(mix_low, 1)

        def dve_windows(dve, g, i):
            n = 2 * g + i
            dve.wait_ge(pj_read, 4 * (16 + g) + 2 + i + 1)
            src = ux[:]
            for m in range(g + 1):
                dst = (us_a, us_b)[m % 2][:]
                lo = (2 << m) - 1
                dve.tensor_tensor(dst[:, lo:UN], src[:, lo:UN], src[:, lo - (1 << m):UN - (1 << m)], ALU.add).then_inc(win_step, 1)
                wn[0] += 1
                dve.wait_ge(win_step, wn[0])
                src = dst
            other = (us_b, us_a)[g % 2][:]
            if i == 0:
                at_least(dve, pooled, g)
            iw = 1.0 / WINDOWS[g]
            dve.tensor_tensor(other[:, 0:16], src[:, BUF:BUF + 16], cst[:, C_INV + 16 * g:C_INV + 16 * g + 16], ALU.mult).then_inc(win_step, 1)
            wn[0] += 1
            dve.wait_ge(win_step, wn[0])
            dve.tensor_tensor(dpool[:, i, 0:16], other[:, 0:16], ux[:, BUF:BUF + 16], ALU.subtract)
            dve.scalar_tensor_tensor(dpool[:, i, 16:SEQ], src[:, BUF + 16:BUF + SEQ], iw, ux[:, BUF + 16:BUF + SEQ], ALU.mult, ALU.subtract)
            dve.scalar_tensor_tensor(sample3(dpool[:, i]), u_sample(src)[:, :, BUF:USEG], iw, u_sample(ux[:])[:, :, BUF:USEG],
                                     ALU.mult, ALU.subtract).then_inc(d_tile, 1)
        wn = [0]

        def dve_map(dve, g):
            dve.wait_ge(pooled, g + 1)
            for d in range(2):
                o = halves(mixo[:, 8 + 2 * g + d, :])
                dve.scalar_tensor_tensor(o, dk[:, 2 * d:2 * d + 2, 0:HALF], gain[:, G_POOL + 2 * g + d:G_POOL + 2 * g + d + 1],
                                         o, ALU.mult, ALU.mult).then_inc(ob_done, 1)

        def dve_pool(dve):
            for g in range(NG):
                for q in range(4):
                    split_low(dve, "pool", g, q + 1)
                    if g == 0:
                        dve_delta(dve, HEADS - 1, q)
                    if g > 0 and q == 0:
                        dve_windows(dve, g - 1, 1)
                    if g > 0 and q == 1:
                        dve_map(dve, g - 1)
                    if g in (1, 2) and q == 2:
                        mix_take_low(dve, g - 1)
                    if q == 3:
                        dve_windows(dve, g, 0)

        def pool_pool(pool):
            for g in range(NG):
                for q in range(4):
                    if q == 3:
                        pool_ucol(pool, g, 0)
                    if g == 0:
                        pool_delta(pool, HEADS - 1, q)
                    if g == 0 and q == 0:
                        pool.wait_ge(conv_done, 24)
                        pool.wait_ge(st_stored, 16 * 48)
                        pool.wait_ge(vz_silu, HEADS)
                        pool.memset(ux[:, 0:BUF], 0.0).then_inc(ux_zero, 1)
                    if q == 0 and g > 0:
                        pool_ucol(pool, g - 1, 1)
            pool_ucol(pool, NG - 1, 1)

        def pool_ucol(pool, g, i):
            pool.wait_ge(pj_read, 4 * (16 + g) + 2 + i + 1)
            at_least(pool, ux_turned, 2 * g + i)
            pool.tensor_copy(ucol[:].rearrange("p (b t) -> p b t", b=NB), u_sample(ux[:])[:, :, BUF:USEG]).then_inc(ucol_ready, 1)

        def pe_ux(g, i):
            def step(pe):
                pe.wait_ge(ucol_ready, 2 * g + i + 1)
                pe.transpose(pj[0:BUF, 2 * i, 0:P], ux[:, SEQ:SEQ + BUF], ident)
                pe.transpose(pj[0:NS, 2 * i, P:2 * P], ucol[:], ident).then_inc(ux_turned, 1)
            return step

        def pe_map(g):
            def step(pe):
                pe.wait_ge(d_tile, 2 * g + 2)
                pe.wait_ge(pw_loaded, 32 * g + 32)
                at_least(pe, ob_done, 2 * g)
                pe.wait_ge(oa_done, HEADS)
                for d in range(2):
                    for b in range(2):
                        for k in range(2):
                            mm = pe.matmul(dk[:, 2 * d + b, 0:HALF], pw[:, k, d, :], dpool[:, k, b * HALF:(b + 1) * HALF],
                                           start=(k == 0), stop=(k == 1))
                mm.then_inc(pooled, 1)
            return step

        def pe_pool(pe):
            def body(g):
                first = is_first(g)
                steps = delta_steps(HEADS - 1) if first else [{}, {}, {}, {}]
                if not first:
                    steps[0][2] = [pe_ux(g - 1, 1)]
                    steps[1][4] = [pe_map(g - 1)]
                steps[3].setdefault(2, []).append(pe_ux(g, 0))
                for q in range(4):
                    w = 4 * (16 + g) + q
                    if first and q == 0:
                        pe.wait_ge(st_ready, 24)
                    if not first:
                        pe.wait_ge(ust_ready, (2 * g - 1, 2 * g, 2 * g, 2 * g)[q])
                    if q >= 2:
                        pe.wait_ge(spool_loaded, 16 * g + 16)
                        pe.wait_ge(pj_read, w - 1)
                        pe.transpose(pj[:, 2 * (q % 2), HALF:HALF + NB * BUF], spool[0:NB * BUF, (q - 2) * P:(q - 1) * P],
                                     ident[0:NB * BUF, 0:NB * BUF]).then_inc(spool_turned, 1)
                    multiply(pe, "pool", g, q, tokens(a_hi), tokens(a_lo), TOK, steps[q])
            body(0)
            with pe.Fori(1, NG) as g:
                body(g)

        take = area(M_W, M_HIMIX)
        xr = [take(f"xr{i}", [TOK]) for i in range(2)]
        x2 = [take(f"x2_{i}", [TOK]) for i in range(2)]
        sqx = take("sqx", [TOK])
        acc = take("acc", [TOK])
        take = area(M_W + 3528, M_HIMIX)
        xr_loaded = [sem(f"xr_loaded{i}") for i in range(2)]
        x2_stored = [sem(f"x2_stored{i}") for i in range(2)]
        (h_high, h_low, sqx_ready, acc_zero, acc_done) = (sem(n) for n in (
            "h_high", "h_low", "sqx_ready", "acc_zero", "acc_done"))

        def sp_residual(sp, stage, j, q):
            src = xT_d if stage == "out" else x2T_d
            r = (0 if stage == "out" else 16) + 4 * j + q
            if not (isinstance(r, int) and r < 2):
                sp.wait_ge(pj_read, 4 * FIRST[stage] + 4 * j + q - 1)
            sp.dma_start(xr[q % 2][:], src[bass.ds(4 * j + q, 1), :, :].rearrange("k p n -> p (k n)")).then_inc(xr_loaded[q % 2], 16)

        def sp_out(sp):
            def body(j):
                for q in range(4):
                    load_ahead(sp, "out", j, q)
                    if is_first(j) and q == 0:
                        sp_ust(sp, NG - 1, 1)
                        for k in range(2):
                            if k == 0:
                                sp.wait_ge(pooled, NG - 1)
                            sp.dma_start(pw[:, k], t["pool_w"][0, NG - 1, k * P:(k + 1) * P, :].rearrange(
                                "c (d n) -> c d n", d=2)).then_inc(pw_loaded, 16)
                        sp.wait_ge(d_tile, 8)
                        sp.wait_ge(ux_turned, 8)
                    sp_residual(sp, "out", j, q)
                    sp.wait_ge(pj_read, 80 + 4 * j + q) if q or not is_first(j) else None
                    if q:
                        sp_x2(sp, j, q - 1)
                    elif not is_first(j):
                        sp_x2(sp, j - 1, 3)
            body(0)
            body(1)
            body(2)
            body(3)

        def sp_x2(sp, j, q):
            sp.dma_start(x2T_d[4 * j + q, :, :], x2[q % 2][:]).then_inc(x2_stored[q % 2], 16)

        def act_out(act):
            def body(j):
                for q in range(4):
                    cast_high(act, "out", j, q + 1)
                    if is_first(j) and q == 0:
                        act_ust(act, NG - 1, 1)
                        mix_take_high(act, 2)
                        mix_take_high(act, 3)
                    i = 4 * j + q
                    act.wait_ge(pj_read, 80 + i + 1)
                    act.activation(a_hi[:, bass.ds(i, 1), :].rearrange("p o n -> p (o n)"), x2[q % 2][:], ACT.Copy,
                                   scale=gain[:, bass.ds(G_CROSS + i, 1)]).then_inc(h_high, 1)
                    at_least(act, acc_done, i)
                    act.activation(sqx[:], x2[q % 2][:], ACT.Square).then_inc(sqx_ready, 1)
            body(0)
            with act.Fori(1, 4) as j:
                body(j)

        def dve_out(dve):
            def body(j):
                for q in range(4):
                    split_low(dve, "out", j, q + 1)
                    if is_first(j) and q == 0:
                        dve_windows(dve, NG - 1, 1)
                        dve_map(dve, NG - 1)
                        mix_take_low(dve, 2)
                        mix_take_low(dve, 3)
                    i = 4 * j + q
                    dve.wait_ge(tile_done, 80 + i + 1)
                    dve.wait_ge(xr_loaded[q % 2], 32 * j + 16 * (q // 2) + 16)
                    at_least(dve, x2_stored[q % 2], 32 * j + 16 * (q // 2))
                    at_least(dve, sqx_ready, i - 1)
                    at_least(dve, h_low, i - 1)
                    dve.tensor_tensor(halves(x2[q % 2][:]), product(q), halves(xr[q % 2][:]), ALU.add).then_inc(pj_read, 1)
                    dve.wait_ge(h_high, i + 1)
                    dve.scalar_tensor_tensor(a_lo[:, bass.ds(i, 1), :].rearrange("p o n -> p (o n)"), x2[q % 2][:],
                                             gain[:, bass.ds(G_CROSS + i, 1)],
                                             a_hi[:, bass.ds(i, 1), :].rearrange("p o n -> p (o n)").bitcast(F32),
                                             ALU.mult, ALU.subtract).then_inc(h_low, 1)
            body(0)
            with dve.Fori(1, 4) as j:
                body(j)

        def pool_sum(pool, r0):
            if r0 == 0:
                pool.wait_ge(pooled, NG)
                pool.memset(acc[:], 0.0).then_inc(acc_zero, 1)
            else:
                pool.wait_ge(sv_done.sem, sv_done.at(32))
                pool.memset(acc[:], 0.0).then_inc(acc_zero, 1)
            pool.wait_ge(acc_zero, 1 if r0 == 0 else 2)

            def body(i):
                pool.wait_ge(sqx_ready, r0 + i + 1)
                at_least(pool, acc_done, r0 + i)
                pool.tensor_tensor(acc[:], acc[:], sqx[:], ALU.add).then_inc(acc_done, 1)
            body(0)
            with pool.Fori(1, 16) as i:
                body(i)

        def pe_out(pe):
            def split(m):
                return lambda pe: pe.wait_ge(mix_low, m)
            pe.wait_ge(ust_ready, 7)
            pe.wait_ge(mix_low, 2)
            for q in range(4):
                steps = {}
                if q == 0:
                    steps = {0: [pe_ux(NG - 1, 1)], 2: [pe_map(NG - 1)], 7: [split(3)], 13: [split(4)]}
                if q == 1:
                    pe.wait_ge(ust_ready, 8)
                multiply(pe, "out", 0, q, tokens(mix_hi), tokens(mix_lo), TOK, steps)
            with pe.Fori(1, 4) as j:
                for q in range(4):
                    multiply(pe, "out", j, q, tokens(mix_hi), tokens(mix_lo))

        qx = put("qx", [KT, TOK], F32, M_B)
        col2 = put("col2", [16], F32, M_END - 64)
        rsb = put("rsb", [NS], F32, M_END - 48)
        sums_done, col2_root, col2_inv, col2_ready, qs_scaled = (sem(n) for n in (
            "sums_done", "col2_root", "col2_inv", "col2_ready", "qs_scaled"))

        def sp_cq(sp):
            def body(j):
                for q in range(4):
                    load_ahead(sp, "cq", j, q)
                    if is_first(j) and q == 0:
                        sp.wait_ge(pj_read, 96)
                        sp_x2(sp, 3, 3)
            body(0)
            with sp.Fori(1, 3) as j:
                body(j)
            body(3)

        def act_cq(act):
            def body(j):
                for q in range(4):
                    cast_high(act, "cq", j, q + 1)
                    if is_first(j) and q == 1:
                        act.wait_ge(sums_done, 1)
                        act.activation(col2[:, 0:4], dk[:, 0, 0:4], ACT.Sqrt, scale=1.0 / D, bias=eps_col)
                        act.activation(rsb[:], dk[:, 1, 0:NS], ACT.Sqrt, scale=1.0 / D, bias=eps_col).then_inc(col2_root, 1)
                    act.wait_ge(tile_done, 96 + 4 * j + q + 1)
                    act.activation(halves(qx[:, bass.ds(4 * j + q, 1), :].rearrange("p o n -> p (o n)")), product(q),
                                   ACT.Copy).then_inc(pj_read, 1)
            body(0)
            with act.Fori(1, 4) as j:
                body(j)

        def dve_cq(dve):
            def body(j):
                for q in range(4):
                    split_low(dve, "cq", j, q + 1)
                    if is_first(j) and q == 1:
                        dve.wait_ge(col2_root, 1)
                        dve.reciprocal(col2[:, 0:4], col2[:, 0:4])
                        dve.reciprocal(rsb[:], rsb[:]).then_inc(col2_inv, 1)
                        dve.wait_ge(col2_inv, 1)
                        dve.tensor_scalar(col2[:, 0:4], col2[:, 0:4], XD ** -0.5, None, ALU.mult)
                        dve.tensor_scalar(rsb[:], rsb[:], XD ** -0.5, None, ALU.mult).then_inc(col2_ready, 1)
            body(0)
            with dve.Fori(1, 4) as j:
                body(j)
            dve.wait_ge(pj_read, 112)
            dve.wait_ge(col2_ready, 1)
            dve.tensor_tensor(qx[:, :, SEQ:TOK], qx[:, :, SEQ:TOK], rsb[:].unsqueeze(1).to_broadcast([P, KT, NS]),
                              ALU.mult).then_inc(qs_scaled, 1)

        def token_sums(pe, first):
            pe.wait_ge(acc_done, 16 if first else 32)
            for i in range(4):
                pe.matmul(dk[:, 0, i:i + 1], acc[:, i * P:(i + 1) * P], ones[:, 0:1], start=True, stop=True)
            if first:
                pe.matmul(dk[:, 1, 0:NS], ones, acc[:, SEQ:TOK], start=True, stop=True).then_inc(sums_done, 1)
            else:
                pe.matmul(dk[S_, 0, 4:5], acc[:, SEQ:TOK], ones[:, 0:1], start=True, stop=True).then_inc(sums_done, 1)

        def pe_cq(pe):
            pe.wait_ge(h_low, 15)
            multiply(pe, "cq", 0, 0, tokens(a_hi), tokens(a_lo), TOK,
                     {14: [lambda pe: pe.wait_ge(h_low, 16)], 15: [lambda pe: token_sums(pe, True)]})
            for q in range(1, 4):
                multiply(pe, "cq", 0, q, tokens(a_hi), tokens(a_lo))
            with pe.Fori(1, 4) as j:
                for q in range(4):
                    multiply(pe, "cq", j, q, tokens(a_hi), tokens(a_lo))

        take = area(M_W, M_END - 64)
        kc = [take(f"kc{i}", [2, XD]) for i in range(4)]
        kct = [take(f"kct{i}", [DT, MEM]) for i in range(2)]
        ktb = [take(f"ktb{i}", [DT, MEM]) for i in range(2)]
        vtb = take("vtb", [2, XD])
        prb = take("prb", [4, MEM])
        ptb = take("ptb", [2, SEQ])
        scs = take("scs", [2, P])
        prs = take("prs", [MEM])
        prt = take("prt", [2, P])
        m4 = put("m4", [16], F32, M_END - 16)
        kc_loaded = [sem(f"kc_loaded{i}") for i in range(4)]
        ktb_loaded = [sem(f"ktb_loaded{i}") for i in range(2)]
        vtb_loaded = sem("vtb_loaded")
        kc_turned = Reused(t0_done, HEADS)
        sk_done = Reused(p1_done, (LEVELS - 1) * HEADS)
        scs_turned = Reused(kk_done, HEADS)
        prs_turned = Reused(v_turned, HEADS)
        sv_done = Reused(tu_done, (LEVELS - 1) * HEADS)
        sc_done = Reused(ks_done, 3 * HEADS)
        p_turned = Reused(vn_done, 4 * HEADS)
        cx_done = Reused(so_done, 4 * HEADS)
        kct_a = Reused(p1_ready, (LEVELS - 1) * HEADS)
        scs_ready = Reused(sq_done, HEADS)
        exp_s = Reused(ln_done, HEADS)
        prt_ready = Reused(rn_done, HEADS)
        sv_high = Reused(d_exp, HEADS)
        exp_p = Reused(eg_ready, HEADS)
        ptb_a = Reused(oln_done, HEADS)
        cx_high = Reused(rno_ready, HEADS)
        kct_v = Reused(u_next, (LEVELS - 1) * HEADS)
        nmax_s = Reused(d_ready, HEADS)
        prs_ready = Reused(kq_normed, HEADS)
        ctx_low_s = Reused(qg_ready, HEADS)
        mx_done = Reused(at_ready, HEADS)
        nmax = Reused(u_ready, HEADS)
        prb_ready = Reused(kd_ready, HEADS)
        ptb_v = Reused(vb_ready, HEADS)
        cx_low = Reused(r_ready, 3 * HEADS)
        rcp_p = Reused(vn_ready, 4 * HEADS)
        rcp_s = Reused(hc_ready, HEADS)
        mm_s = Reused(us_ready, (LEVELS - 6) * HEADS)

        def cache(x, b, h):
            return x[0, bass.ds(b, 1), :, h, :].rearrange("o (m p) d -> p (o m) d", p=P)

        def sp_attention(sp):
            sp.wait_ge(tile_done, 96)
            sp.wait_ge(sums_done, 1)
            for i in range(2):
                sp_ktb(sp, i)
            sp_vtb(sp, 0)

            def keys(b):
                for h in range(XH):
                    if not is_first(b):
                        sp.wait_ge(kc_turned.sem, kc_turned.at(4 * b + h - 3))
                    sp.dma_start(kc[h][:], cache(t["cache_mem_k"], b, h)).then_inc(kc_loaded[h], 16)

            def values(b):
                for h in range(XH):
                    if is_first(b):
                        sp.wait_ge(kc_turned.sem, kc_turned.at(29 + h))
                    else:
                        sp.wait_ge(sv_done.sem, sv_done.at(4 * b + h - 3))
                    sp.dma_start(kc[h][:], cache(t["cache_mem_v"], b, h)).then_inc(kc_loaded[h], 16)
            keys(0)
            with sp.Fori(1, NB) as b:
                keys(b)
            values(0)
            for h in range(1, XH):
                if h + 1 < XH:
                    sp.wait_ge(sc_done.sem, sc_done.at(h))
                    sp_ktb(sp, h + 1)
                sp.wait_ge(cx_done.sem, cx_done.at(4 * h))
                sp_vtb(sp, h)
            with sp.Fori(1, NB) as b:
                values(b)

        def sp_ktb(sp, h):
            sp.dma_start(ktb[h % 2][:], kT_d[DT * h:DT * h + DT].rearrange("k p m -> p k m")).then_inc(ktb_loaded[h % 2], 16)

        def sp_vtb(sp, h):
            sp.dma_start(vtb[:], t["mem_v_prompt"][0, 0, :, h, :].rearrange("(m p) d -> p m d", p=P)).then_inc(vtb_loaded, 16)

        def pe_sample_keys(pe):
            def turn(b, h):
                pe.wait_ge(kc_loaded[h], 16 * b + 16)
                u = 4 * b + h
                at_least(pe, kct_a, u - 1)
                at_least(pe, kct_v, u - 1)
                for d in range(DT):
                    for m in range(2):
                        o = (d % 2) * 256 + m * P
                        mm = pe.transpose(dk[:, 2 * (h % 2) + d // 2, o:o + P], kc[h][:, m, d * P:(d + 1) * P], ident)
                mm.then_inc(kc_turned.sem, 1)

            def scores(b, h):
                u = 4 * b + h
                pe.wait_ge(kct_a.sem, kct_a.at(u + 1))
                pe.wait_ge(kct_v.sem, kct_v.at(u + 1))
                for m in range(2):
                    for d in range(DT):
                        mm = pe.matmul(pj[:, 0, bass.ds(m * P + 16 * b + NT * h, NT)], kct[h % 2][:, d, m * P:(m + 1) * P],
                                       qx[:, DT * h + d, bass.ds(SEQ + NT * b, NT)], start=(d == 0), stop=(d == DT - 1))
                mm.then_inc(sk_done.sem, 1)
            pe.wait_ge(qs_scaled, 1)
            pe.wait_ge(col2_root, 1)

            def body(b):
                turn(b, 0)
                for h in range(XH):
                    if h + 1 < XH:
                        turn(b, h + 1)
                    scores(b, h)
            body(0)
            with pe.Fori(1, NB) as b:
                body(b)

        def take_keys(eng, b, mine):
            for h in range(XH):
                u = 4 * b + h
                eng.wait_ge(kc_turned.sem, kc_turned.at(u + 1))
                at_least(eng, sk_done, u - 1)
                o, i = kct[h % 2][:, 2 * mine:2 * mine + 2, :].rearrange("p d m -> p (d m)"), dk[:, 2 * (h % 2) + mine, :]
                if mine:
                    eng.tensor_copy(o, i).then_inc(kct_v.sem, 1)
                else:
                    eng.activation(o, i, ACT.Copy).then_inc(kct_a.sem, 1)

        def pe_attention(pe):
            pe_sample_keys(pe)

            def scores(h):
                pe.wait_ge(ktb_loaded[h % 2], 16 * (h // 2) + 16)
                at_least(pe, exp_p, h)
                if h == 0:
                    pe.wait_ge(kct_a.sem, kct_a.at(32))
                    pe.wait_ge(kct_v.sem, kct_v.at(32))
                for i in range(4):
                    for d in range(DT):
                        mm = pe.matmul(dk[:, i // 2, (i % 2) * 256:(i % 2) * 256 + 256], qx[:, DT * h + d, i * P:(i + 1) * P],
                                       ktb[h % 2][:, d, :], start=(d == 0), stop=(d == DT - 1))
                mm.then_inc(sc_done.sem, 1)

            def turn(h):
                pe.wait_ge(prb_ready.sem, prb_ready.at(h + 1))
                at_least(pe, ptb_a, h)
                at_least(pe, ptb_v, h)
                for m in range(2):
                    for i in range(4):
                        mm = pe.transpose(dk[:, 2 + m, i * P:(i + 1) * P], prb[:, i, m * P:(m + 1) * P], ident)
                mm.then_inc(p_turned.sem, 1)

            def context(h):
                pe.wait_ge(ptb_a.sem, ptb_a.at(h + 1))
                pe.wait_ge(ptb_v.sem, ptb_v.at(h + 1))
                pe.wait_ge(vtb_loaded, 16 * h + 16)
                for d in range(DT):
                    at_least(pe, cx_low, 4 * h + d - 1)
                    for m in range(2):
                        mm = pe.matmul(pj[:, 2 + d % 2, :], vtb[:, m, d * P:(d + 1) * P], ptb[:, m, :], start=(m == 0), stop=(m == 1))
                    mm.then_inc(cx_done.sem, 1)

            scores(0)
            for h in range(XH):
                if h == 0:
                    pe.wait_ge(scs_ready.sem, scs_ready.at(1))
                    for m in range(2):
                        mm = pe.transpose(pj[:, 1, m * P:(m + 1) * P], scs[:, m, :], ident)
                    mm.then_inc(scs_turned.sem, 1)
                if h == 1:
                    pe.wait_ge(prs_ready.sem, prs_ready.at(1))
                    for m in range(2):
                        mm = pe.transpose(pj[:, 0, m * P:(m + 1) * P], prs[:, m * P:(m + 1) * P], ident)
                    mm.then_inc(prs_turned.sem, 1)
                if h + 1 < XH:
                    scores(h + 1)
                turn(h)
                context(h)

            def values(b):
                for h in range(XH):
                    pe.wait_ge(kc_loaded[h], 16 * (NB + 1) + 16 * b)
                    for d in range(DT):
                        for m in range(2):
                            mm = pe.matmul(pj[:, 1, bass.ds((DT * h + d) * NS + NT * b, NT)], kc[h][:, m, d * P:(d + 1) * P],
                                           prt[:, m, bass.ds(16 * b + NT * h, NT)], start=(m == 0), stop=(m == 1))
                    mm.then_inc(sv_done.sem, 1)
            pe.wait_ge(prt_ready.sem, prt_ready.at(1))
            with pe.Fori(0, NB) as b:
                values(b)

        def act_attention(act):
            act.wait_ge(tile_done, 96)

            def body(b):
                take_keys(act, b, 0)
            body(0)
            with act.Fori(1, NB) as b:
                body(b)
            act.wait_ge(sk_done.sem, sk_done.at(32))
            act.activation(scs[:].rearrange("p m n -> p (m n)"), pj[:, 0, 0:MEM], ACT.Copy).then_inc(scs_ready.sem, 1)

            for h in range(XH):
                act.wait_ge(nmax.sem, nmax.at(h + 1))
                at_least(act, p_turned, h)
                for i in range(4):
                    a = act.activation(prb[:, i, :], dk[:, i // 2, (i % 2) * 256:(i % 2) * 256 + 256], ACT.Exp,
                                       scale=col2[:, i:i + 1], bias=m4[:, 4 + i:5 + i], accum_out=m4[:, 8 + i:9 + i])
                a.then_inc(exp_p.sem, 1)
                if h == 0:
                    act.wait_ge(nmax_s.sem, nmax_s.at(1))
                    act.activation(prs[:], pj[:, 1, 0:MEM], ACT.Exp, bias=m4[:, 12:13], accum_out=m4[:, 13:14]).then_inc(exp_s.sem, 1)
                if h == 1:
                    act.wait_ge(prs_turned.sem, prs_turned.at(1))
                    act.activation(prt[:].rearrange("p m n -> p (m n)"), pj[:, 0, 0:MEM], ACT.Copy).then_inc(prt_ready.sem, 1)
                act.wait_ge(p_turned.sem, p_turned.at(h + 1))
                at_least(act, cx_done, 4 * h)
                act.activation(ptb[:, 0, :], dk[:, 2, :], ACT.Copy).then_inc(ptb_a.sem, 1)
                for d in range(DT):
                    act.wait_ge(cx_done.sem, cx_done.at(4 * h + d + 1))
                    act.activation(a_hi[:, DT * h + d, 0:SEQ], pj[:, 2 + d % 2, :], ACT.Copy).then_inc(cx_high.sem, 1)
            act.wait_ge(sv_done.sem, sv_done.at(32))
            act.activation(a_hi[:, :, SEQ:TOK], pj[:, 1, :].rearrange("p (k n) -> p k n", k=KT), ACT.Copy).then_inc(sv_high.sem, 1)

        def dve_attention(dve):
            dve.wait_ge(tile_done, 96)

            def body(b):
                take_keys(dve, b, 1)
            body(0)
            with dve.Fori(1, NB) as b:
                body(b)
            for h in range(XH):
                dve.wait_ge(sc_done.sem, sc_done.at(h + 1))
                dve.tensor_reduce(m4[:, 0:4], dk[:, 0:2, :].rearrange("p b (i m) -> p (b i) m", i=2), AX_X, ALU.max).then_inc(mx_done.sem, 1)
                dve.wait_ge(mx_done.sem, mx_done.at(h + 1))
                at_least(dve, exp_p, h)
                dve.scalar_tensor_tensor(m4[:, 4:8], m4[:, 0:4], -1.0, col2[:, 0:4], ALU.mult, ALU.mult).then_inc(nmax.sem, 1)
                if h == 0:
                    dve.wait_ge(scs_turned.sem, scs_turned.at(1))
                    dve.tensor_reduce(m4[:, 14:15], pj[:, 1, 0:MEM], AX_X, ALU.max).then_inc(mm_s.sem, 1)
                    dve.wait_ge(mm_s.sem, mm_s.at(1))
                    dve.tensor_scalar(m4[:, 12:13], m4[:, 14:15], -1.0, None, ALU.mult).then_inc(nmax_s.sem, 1)
                dve.wait_ge(exp_p.sem, exp_p.at(h + 1))
                dve.reciprocal(m4[:, 0:4], m4[:, 8:12]).then_inc(rcp_p.sem, 1)
                dve.wait_ge(rcp_p.sem, rcp_p.at(h + 1))
                dve.tensor_tensor(prb[:], prb[:], m4[:, 0:4].unsqueeze(2).to_broadcast([P, 4, MEM]), ALU.mult).then_inc(prb_ready.sem, 1)
                if h == 0:
                    dve.wait_ge(exp_s.sem, exp_s.at(1))
                    dve.reciprocal(m4[:, 15:16], m4[:, 13:14]).then_inc(rcp_s.sem, 1)
                    dve.wait_ge(rcp_s.sem, rcp_s.at(1))
                    dve.tensor_scalar(prs[:], prs[:], m4[:, 15:16], None, ALU.mult).then_inc(prs_ready.sem, 1)
                dve.wait_ge(p_turned.sem, p_turned.at(h + 1))
                at_least(dve, cx_done, 4 * h)
                dve.tensor_copy(ptb[:, 1, :], dk[:, 3, :]).then_inc(ptb_v.sem, 1)
                for d in range(DT):
                    dve.wait_ge(cx_high.sem, cx_high.at(4 * h + d + 1))
                    dve.tensor_tensor(a_lo[:, DT * h + d, 0:SEQ], pj[:, 2 + d % 2, :], a_hi[:, DT * h + d, 0:SEQ].bitcast(F32),
                                      ALU.subtract).then_inc(cx_low.sem, 1)
            dve.wait_ge(sv_high.sem, sv_high.at(1))
            dve.tensor_tensor(a_lo[:, :, SEQ:TOK], pj[:, 1, :].rearrange("p (k n) -> p k n", k=KT),
                              a_hi[:, :, SEQ:TOK].bitcast(F32), ALU.subtract).then_inc(ctx_low_s.sem, 1)

        xg = put("xg", [KT, TOK], F32, M_B)
        take = area(M_W + 6 * TOK + 64, M_END - 64)
        yb = [take(f"yb{i}", [D]) for i in range(2)]
        rs3 = take("rs3", [8])
        y_stored = [sem(f"y_stored{i}") for i in range(2)]
        (xg_ready, root3, rs3_ready, y_turned, y_act, y_dve) = (sem(n) for n in (
            "xg_ready", "root3", "rs3_ready", "y_turned", "y_act", "y_dve"))

        def sp_co(sp):
            def body(j):
                for q in range(4):
                    load_ahead(sp, "co", j, q)
                    if is_first(j) and q == 0:
                        for i in range(2):
                            sp.wait_ge(x2_stored[i], 128)
                        sp.wait_ge(sv_done.sem, sv_done.at(32))
                    sp_residual(sp, "co", j, q)
            body(0)
            with sp.Fori(1, 3) as j:
                body(j)
            body(3)
            for n in range(5):
                rows = P if n < 4 else NS
                sp.wait_ge(y_act, 2 * n + 2)
                sp.wait_ge(y_dve, 2 * n + 2)
                dst = t["y_prompt"][0, n * P:(n + 1) * P, :] if n < 4 else t["y_sample"].rearrange("b t d -> (b t) d")
                sp.dma_start(dst, yb[n % 2][0:rows, :]).then_inc(y_stored[n % 2], 16)
            sp.wait_ge(y_stored[0], 48)
            sp.wait_ge(y_stored[1], 32)
            for s, v in ((mst_stored, 128), (kts_stored, 64), (xts_stored, 80), (st_stored, 768), (s_stored, 128),
                         (s0_stored, 128), (ust_stored, 16 * 72), (old_rows, 16), (x2_stored[0], 128), (x2_stored[1], 128)):
                sp.wait_ge(s, v)

        def act_co(act):
            def body(j):
                for q in range(4):
                    cast_high(act, "co", j, q + 1)
                    i = 4 * j + q
                    act.wait_ge(pj_read, 112 + i + 1)
                    act.activation(xg[:, bass.ds(i, 1), :].rearrange("p o n -> p (o n)"), x2[q % 2][:], ACT.Copy,
                                   scale=gain[:, bass.ds(G_FINAL + i, 1)]).then_inc(xg_ready, 1)
                    act.wait_ge(acc_done, 16 + i)
                    act.activation(sqx[:], x2[q % 2][:], ACT.Square).then_inc(sqx_ready, 1)
            body(0)
            with act.Fori(1, 3) as j:
                body(j)
            body(3)
            act.wait_ge(sums_done, 2)
            act.activation(rs3[:, 0:4], dk[:, 0, 0:4], ACT.Sqrt, scale=1.0 / D, bias=eps_col)
            act.activation(rs3[S_, 4:5], dk[S_, 0, 4:5], ACT.Sqrt, scale=1.0 / D, bias=eps_col[S_, :]).then_inc(root3, 1)
            act.wait_ge(rs3_ready, 1)
            for n in range(5):
                rows = P if n < 4 else NS
                for c in (0, 2):
                    act.wait_ge(y_turned, 4 * n + c + 1)
                    at_least(act, y_stored[n % 2], 16 * (n // 2))
                    act.activation(yb[n % 2][0:rows, c * 512:(c + 1) * 512], pj[0:rows, c, :], ACT.Copy,
                                   scale=rs3[0:rows, n:n + 1]).then_inc(y_act, 1)

        def dve_co(dve):
            def body(j):
                for q in range(4):
                    split_low(dve, "co", j, q + 1)
                    i = 4 * j + q
                    dve.wait_ge(tile_done, 112 + i + 1)
                    dve.wait_ge(xr_loaded[q % 2], 128 + 32 * j + 16 * (q // 2) + 16)
                    dve.wait_ge(sqx_ready, 16 + i - 1)
                    at_least(dve, xg_ready, i - 1)
                    dve.tensor_tensor(halves(x2[q % 2][:]), product(q), halves(xr[q % 2][:]), ALU.add).then_inc(pj_read, 1)
            body(0)
            with dve.Fori(1, 3) as j:
                body(j)
            body(3)
            dve.wait_ge(root3, 1)
            dve.reciprocal(rs3[:, 0:4], rs3[:, 0:4])
            dve.reciprocal(rs3[S_, 4:5], rs3[S_, 4:5]).then_inc(rs3_ready, 1)
            dve.wait_ge(rs3_ready, 1)
            for n in range(5):
                rows = P if n < 4 else NS
                for c in (1, 3):
                    dve.wait_ge(y_turned, 4 * n + c + 1)
                    at_least(dve, y_stored[n % 2], 16 * (n // 2))
                    dve.tensor_scalar(yb[n % 2][0:rows, c * 512:(c + 1) * 512], pj[0:rows, c, :], rs3[0:rows, n:n + 1], None,
                                      ALU.mult).then_inc(y_dve, 1)

        def pe_co(pe):
            pe.wait_ge(ctx_low_s.sem, ctx_low_s.at(1))
            pe.wait_ge(cx_low.sem, cx_low.at(16))
            with pe.Fori(0, 4) as j:
                for q in range(4):
                    multiply(pe, "co", j, q, tokens(a_hi), tokens(a_lo))
            token_sums(pe, False)
            pe.wait_ge(xg_ready, 16)
            pe.wait_ge(pj_read, 128)
            for n in range(5):
                rows = P if n < 4 else NS
                for c in range(4):
                    if n > 0:
                        pe.wait_ge(y_dve if c % 2 else y_act, 2 * (n - 1) + c // 2 + 1)
                    for m in range(4):
                        mm = pe.transpose(pj[0:rows, c, m * P:(m + 1) * P], xg[:, 4 * c + m, n * P:n * P + rows], ident)
                    mm.then_inc(y_turned, 1)

        block = ctx.enter_context(nc.Block())

        @block.sync
        def _(sp):
            sp_mem(sp)
            sp_heads(sp)
            sp_pool(sp)
            sp_out(sp)
            sp_cq(sp)
            sp_attention(sp)
            sp_co(sp)

        @block.scalar
        def _(act):
            act_mem(act)
            act_heads(act)
            act_pool(act)
            act_out(act)
            act_cq(act)
            act_attention(act)
            act_co(act)

        @block.vector
        def _(dve):
            dve_mem(dve)
            dve_heads(dve)
            dve_pool(dve)
            dve_out(dve)
            dve_cq(dve)
            dve_attention(dve)
            dve_co(dve)

        @block.gpsimd
        def _(pool):
            pool_heads(pool)
            pool_pool(pool)
            pool_sum(pool, 0)
            pool_sum(pool, 16)

        @block.tensor
        def _(pe):
            pe_mem(pe)
            pe_heads(pe)
            pe_pool(pe)
            pe_out(pe)
            pe_cq(pe)
            pe_attention(pe)
            pe_co(pe)


INPUTS = ("x_prompt", "x_sample", "mem_prompt", "cache_mem_k", "cache_mem_v", "state_delta", "state_conv", "state_pool",
          "norm_mix", "w_in", "conv_w", "a_log", "dt_bias", "gdn_norm", "pool_w", "pool_scale", "w_out", "norm_mem",
          "norm_cross", "w_cq", "w_ck", "w_cv", "w_co", "norm_final")
OUTPUTS = (("y_prompt", (1, SEQ, D)), ("y_sample", (NB, NT, D)),
           ("mem_k_prompt", (1, 1, MEM, XH, XD)), ("mem_v_prompt", (1, 1, MEM, XH, XD)),
           ("delta_prompt", (1, 1, HEADS, P, P)), ("conv_prompt", (1, 1, 3, QKV)), ("pool_prompt", (1, 1, BUF, MIX)),
           ("delta_sample", (1, NB, HEADS, P, P)), ("conv_sample", (1, NB, 3, QKV)), ("pool_sample", (1, NB, BUF, MIX)))


def kernel(**inputs):
    import concourse.bacc as bacc
    from concourse.bass_utils import run_bass_kernel_spmd

    nc = bacc.Bacc("TRN2", target_bir_lowering=False, num_devices=1)
    arrays, t = {}, {}
    for name in INPUTS:
        arrays[f"in_{name}_dram"] = np.ascontiguousarray(inputs[name])
    arrays["in_consts_dram"] = constants()
    for name in INPUTS + ("consts",):
        a = arrays[f"in_{name}_dram"]
        t[name] = nc.dram_tensor(f"in_{name}_dram", a.shape, mybir.dt.from_np(a.dtype), kind="ExternalInput").ap()
    for i, (name, shape) in enumerate(OUTPUTS):
        t[name] = nc.dram_tensor(f"out_{i}_dram", shape, F32, kind="ExternalOutput").ap()
    build(nc, t)
    r = run_bass_kernel_spmd(nc, [arrays], core_ids=[0])
    return tuple(r.results[0][f"out_{i}_dram"] for i in range(len(OUTPUTS)))
```

```python
from contextlib import ExitStack

import numpy as np

import concourse.bass as bass
from concourse import mybir

F32 = mybir.dt.float32
F32R = mybir.dt.float32r
ALU = mybir.AluOpType
ACT = mybir.ActivationFunctionType
AX_X = mybir.AxisListType.X

P = 128
D = 2048
KT = D // P
SEQ = 512
NB, NT = 8, 4
NS = NB * NT
TOK = SEQ + NS
HALF = TOK // 2
HEADS = 8
MEM = 256
XH, XD = 4, 512
DT = XD // P
MIX = 1024
QKV = 3 * MIX
NQKV = QKV // P
COL_A = 4 * MIX
COL_U = COL_A + 2 * HEADS
COL_ZB = COL_U + MIX
WINDOWS = (2, 4, 8, 16)
NG = 4
BUF = 15
EPS = 1e-6
CH = SEQ // P
LEVELS = 7
CSEG = 3 + NT
EXTN = 3 + SEQ + NB * CSEG
YN = EXTN - 3
USEG = BUF + NT
UN = BUF + SEQ + NB * USEG
NTILE = 128

C_ID, C_ONE, C_INCL, C_LEV = 0, 128, 256, 384
C_SINCL = C_LEV + LEVELS * P
C_SL1, C_SL2, C_BM = C_SINCL + 32, C_SINCL + 64, C_SINCL + 96
C_INV = C_BM + NB
C_EPS = C_INV + NG * 16
C_LNQ = C_EPS + 1
NCONST = C_EPS + 2
C_REQ = NCONST
NCONST_ALL = C_REQ + NB * NS

G_MIX, G_MEM, G_CROSS, G_FINAL, G_GDN, G_POOL = 0, 16, 32, 48, 64, 65
NGAIN = 73
NCONV = 4 * NQKV


def constants():
    c = np.zeros((P, NCONST_ALL), np.float32)
    j, i = np.arange(P)[:, None], np.arange(P)[None, :]

    def level(s, j, i):
        return (i // (2 * s) == j // (2 * s)) & ((i // s) % 2 == 1) & ((j // s) % 2 == 0)

    c[:, C_ID:C_ID + P] = np.eye(P)
    c[:, C_ONE:C_ONE + P] = 1
    c[:, C_INCL:C_INCL + P] = i >= j
    for n in range(LEVELS):
        c[:, C_LEV + n * P:C_LEV + (n + 1) * P] = level(1 << n, j, i) * (-1.0 if n == 0 else 1.0)
    j, i = j[:NS], i[:, :NS]
    c[:NS, C_SINCL:C_SINCL + NS] = (i // NT == j // NT) & (i >= j)
    c[:NS, C_SL1:C_SL1 + NS] = -1.0 * level(1, j, i)
    c[:NS, C_SL2:C_SL2 + NS] = level(2, j, i)
    c[:NS, C_BM:C_BM + NB] = j // NT == np.arange(NB)[None, :]
    for g, w in enumerate(WINDOWS):
        c[:, C_INV + 16 * g:C_INV + 16 * g + 16] = 1.0 / np.minimum(w, np.arange(16) + 1)
    c[:, C_EPS] = EPS
    c[:, C_LNQ] = -0.5 * np.log(P)
    c[:, C_REQ:] = (np.arange(NS)[None, :] // NT == np.arange(NB)[:, None]).reshape(1, NB * NS)
    return c


class Reused:

    def __init__(self, sem, left_at):
        self.sem, self.left_at = sem, left_at

    def at(self, v):
        return v + self.left_at


def build(nc, t):
    with ExitStack() as ctx:
        ARENA, ARENA_END = 16512, 229344

        def sem(name):
            return ctx.enter_context(nc.semaphore(name))

        def put(name, shape, dtype, at):
            return nc.alloc_sbuf_tensor_at(name, [P] + list(shape), dtype, offset=ARENA + 4 * at)

        def area(start, end):
            pos = [start]

            def take(name, shape, dtype=F32):
                n = int(np.prod(shape))
                o = put(name, shape, dtype, pos[0])
                pos[0] += -(-n // 8) * 8
                assert pos[0] <= end, (name, pos[0], end)
                return o
            take.pos = pos
            return take

        M_RAW = 0
        M_HIGH = M_RAW + 4 * D
        M_A = M_HIGH + 2 * D
        M_B = M_A + 2 * KT * TOK
        M_C = M_B + KT * TOK
        M_END = (ARENA_END - ARENA) // 32 * 8
        raw = [put(f"w_raw{i}", [KT, P], F32, M_RAW + i * D) for i in range(4)]
        low = [put(f"w_low{i}", [KT, P], F32R, M_RAW + i * D) for i in range(4)]
        high = [put(f"w_high{i}", [KT, P], F32R, M_HIGH + i * D) for i in range(2)]
        a_hi = put("a_hi", [KT, TOK], F32R, M_A)
        a_lo = put("a_lo", [KT, TOK], F32R, M_A + KT * TOK)
        keep = area(M_C, M_END)
        cst = keep("cst", [NCONST])
        gain = keep("gain", [NGAIN])
        convw = keep("convw", [4, 3, HEADS])
        cols = keep("cols", [4, 5, HEADS])
        stat = keep("stat", [16])
        M_W = keep.pos[0]
        M_HIMIX = M_END - KT * TOK
        M_DELTA = M_W + 3528
        M_ROWS = M_END - 576
        ident = cst[:, C_ID:C_ID + P]
        ones = cst[:, C_ONE:C_ONE + P]
        eps_col = cst[:, C_EPS:C_EPS + 1]

        pj = ctx.enter_context(nc.psum_tensor("pj", [P, 4, 512], F32))
        dk = ctx.enter_context(nc.psum_tensor("dk", [P, 4, 512], F32))

        xT_d = nc.dram_tensor("xT_scratch", [KT, P, TOK], F32, kind="Internal").ap()
        x2T_d = nc.dram_tensor("x2T_scratch", [KT, P, TOK], F32, kind="Internal").ap()
        kT_d = nc.dram_tensor("kT_scratch", [KT, P, MEM], F32, kind="Internal").ap()
        row_d = nc.dram_tensor("row_scratch", [2, HEADS, TOK], F32, kind="Internal").ap()

        def at_least(eng, s, v):
            if not (isinstance(v, int) and v <= 0):
                if isinstance(s, Reused):
                    eng.wait_ge(s.sem, s.at(v))
                else:
                    eng.wait_ge(s, v)

        w_loaded = [sem(f"w_loaded{i}") for i in range(4)]
        hi_cast = sem("hi_cast")
        lo_split = sem("lo_split")
        tile_done = sem("tile_done")
        pj_read = sem("pj_read")

        STAGES = ("mem", "head", "pool", "out", "cq", "co")
        FIRST = {"mem": 0, "head": 8, "pool": 16, "out": 20, "cq": 24, "co": 28}
        COUNT = {"mem": 8, "head": 8, "pool": 4, "out": 4, "cq": 4, "co": 4}
        w_in, w_out, w_cq, w_ck, w_cv, w_co = (t[n].rearrange("o (k p) n -> p (o k) n", p=P)
                                               for n in ("w_in", "w_out", "w_cq", "w_ck", "w_cv", "w_co"))

        def source(stage, j, q, v=False):
            if stage == "mem":
                return w_cv[:, :, bass.ds((j - 4) * 512 + q * P, P)] if v else w_ck[:, :, bass.ds(j * 512 + q * P, P)]
            if stage == "head":
                return w_in[:, :, bass.ds(j * P + q * MIX, P)]
            if stage == "pool":
                return w_in[:, :, bass.ds(j * 256 + (COL_ZB if q < 2 else COL_U) + (q % 2) * P, P)]
            return {"out": w_out, "cq": w_cq, "co": w_co}[stage][:, :, bass.ds(j * 512 + q * P, P)]

        def load_ahead(sp, stage, j, q, v=False):
            n = FIRST[stage] + j
            if q == 0:
                src = source(stage, j, 3, v)
            elif isinstance(j, int) and j + 1 == COUNT[stage]:
                if stage == "co":
                    return
                src = source(STAGES[STAGES.index(stage) + 1], 0, q - 1)
            else:
                src = source(stage, j + 1, q - 1, v or (isinstance(j, int) and j == 3))
            at_least(sp, tile_done, 4 * n + q)
            sp.dma_start(raw[(q + 3) % 4][:], src).then_inc(w_loaded[(q + 3) % 4], 16)

        def cast_high(act, stage, j, q):
            n = FIRST[stage] + j + q // 4
            q = q % 4
            if isinstance(n, int) and 4 * n >= NTILE:
                return
            act.wait_ge(w_loaded[q], 16 * n + 16)
            at_least(act, tile_done, 4 * n + q - 1)
            act.activation(high[q % 2][:], raw[q][:], ACT.Copy).then_inc(hi_cast, 1)

        def split_low(dve, stage, j, q):
            n = FIRST[stage] + j + q // 4
            q = q % 4
            if isinstance(n, int) and 4 * n >= NTILE:
                return
            dve.wait_ge(hi_cast, 4 * n + q + 1)
            dve.tensor_tensor(low[q][:], raw[q][:], high[q % 2][:].bitcast(F32), ALU.subtract).then_inc(lo_split, 1)

        def multiply(pe, stage, j, q, xh, xl, n_tok=TOK, steps=None):
            w = 4 * (FIRST[stage] + j) + q
            steps = steps or {}
            pe.wait_ge(lo_split, w + 1)
            at_least(pe, pj_read, w - 1)
            parts = [(0, HALF), (HALF, HALF)] if n_tok == TOK else [(0, n_tok)]
            for k in range(KT):
                for m, (wt, x) in enumerate(((high[q % 2], xh), (high[q % 2], xl), (low[q], xh))):
                    for b, (o, n) in enumerate(parts):
                        mm = pe.matmul(pj[:, 2 * (q % 2) + b, 0:n], wt[:, k, :], x(k, o, n),
                                       start=(k == 0 and m == 0), stop=(k == KT - 1 and m == 2))
                if k == KT - 1:
                    mm.then_inc(tile_done, 1)
                for step in steps.get(k, ()):
                    step(pe)

        def tokens(x):
            return lambda k, o, n: x[:, k, o:o + n]

        def product(q, n_tok=TOK):
            return pj[:, 2 * (q % 2):2 * (q % 2) + 2, 0:HALF] if n_tok == TOK else pj[:, 2 * (q % 2), 0:n_tok]

        def halves(x):
            return x.rearrange("p (b n) -> p b n", b=2)

        hm_hi = put("hm_hi", [KT, MEM], F32R, M_B)
        hm_lo = put("hm_lo", [KT, MEM], F32R, M_B + KT * MEM)
        vrow = put("vrow", [2, P], F32, M_A)
        scrow = put("scrow", [QKV], F32, M_A + 2 * P)
        sct = put("sct", [3, HEADS, NB, 3], F32, M_END - 3 * HEADS * NB * 3)
        take = area(M_W, M_END - 576)
        xin = [take(f"xin{i}", [D]) for i in range(2)]
        xst = take("xst", [D])
        xsm = put("xsm", [D], F32, M_A + KT * TOK)
        xts = take("xts", [KT, P])
        kts = take("kts", [4, MEM])
        mst = take("mst", [2, 512])

        const_loaded, vec_loaded, vec_turned, vec_ready = (sem(n) for n in (
            "const_loaded", "vec_loaded", "vec_turned", "vec_ready"))
        x_loaded, squared, rooted, inverted, x_scaled = (sem(n) for n in (
            "x_loaded", "squared", "rooted", "inverted", "x_scaled"))
        x_turned = sem("x_turned")
        x_high = sem("x_high")
        x_bank = sem("x_bank")
        xts_stored, kts_stored, m_turned, mst_ready, mst_stored = (sem(n) for n in (
            "xts_stored", "kts_stored", "m_turned", "mst_ready", "mst_stored"))

        def banks_before(n):
            return 4 * n if isinstance(n, int) and n < 2 else 8 * (n - 1)

        def x_stats(act, n, src, rows):
            act.wait_ge(x_loaded, 16 * (n + 1))
            xs, o = (xsm, 4) if isinstance(n, int) and n == 1 else (xst, 0)
            if not (isinstance(n, int) and n == 1):
                at_least(act, x_turned, banks_before(n))
            act.activation(xs[0:rows, :], src[0:rows, :], ACT.Square,
                           accum_out=stat[0:rows, o:o + 1]).then_inc(squared, 1)
            act.wait_ge(squared, n + 1)
            act.activation(stat[0:rows, o + 1:o + 2], stat[0:rows, o:o + 1], ACT.Sqrt, scale=1.0 / D,
                           bias=eps_col[0:rows, :]).then_inc(rooted, 1)

        def x_scale(dve, n, src, rows):
            xs, o = (xsm, 4) if isinstance(n, int) and n == 1 else (xst, 0)
            dve.wait_ge(rooted, n + 1)
            dve.reciprocal(stat[0:rows, o + 2:o + 3], stat[0:rows, o + 1:o + 2]).then_inc(inverted, 1)
            dve.wait_ge(inverted, n + 1)
            dve.tensor_scalar(xs[0:rows, :], src[0:rows, :], stat[0:rows, o + 2:o + 3], None, ALU.mult).then_inc(x_scaled, 1)

        def x_turn(pe, src, c, slot, part, rows):
            at_least(pe, x_bank, c - 1)
            for m in range(4):
                k = 4 * part + m
                mm = pe.transpose(dk[:, slot % 3, m * rows:(m + 1) * rows], src[0:rows, k * P:(k + 1) * P],
                                  ident[0:rows, 0:rows])
            mm.then_inc(x_turned, 1)

        def x_take_high(act, c, slot, part, dst, lo, rows, g0):
            act.wait_ge(x_turned, c + 1)
            for m in range(4):
                k = 4 * part + m
                a = act.activation(dst[:, k, bass.ds(lo, rows)], dk[:, slot % 3, m * rows:(m + 1) * rows], ACT.Copy,
                                   scale=gain[:, g0 + k:g0 + k + 1])
            a.then_inc(x_high, 1)

        def x_take_low(dve, nhigh, slot, part, hi, dst, lo, rows, g0):
            dve.wait_ge(x_high, nhigh + 1)
            for m in range(4):
                k = 4 * part + m
                a = dve.scalar_tensor_tensor(dst[:, k, bass.ds(lo, rows)], dk[:, slot % 3, m * rows:(m + 1) * rows],
                                             gain[:, g0 + k:g0 + k + 1], hi[:, k, bass.ds(lo, rows)].bitcast(F32),
                                             ALU.mult, ALU.subtract)
            a.then_inc(x_bank, 1)

        def store_keys_turned(sp, j):
            sp.wait_ge(pj_read, 4 * j + 4)
            sp.dma_start(kT_d[bass.ds(4 * j, 4), :, :].rearrange("k p r -> p k r"), kts[:]).then_inc(kts_stored, 16)

        def store_k_or_v(sp, j, v):
            dst = (t["mem_v_prompt"] if v else t["mem_k_prompt"])[0, 0].rearrange("(m p) h d -> p m (h d)", p=P)
            sp.wait_ge(mst_ready, 4 * j + 4)
            sp.dma_start(dst[:, :, bass.ds((j - 4 if v else j) * 512, 512)], mst[:]).then_inc(mst_stored, 16)

        def sp_mem(sp):
            sp.dma_start(xin[0][:], t["mem_prompt"][0, 0:P, :]).then_inc(x_loaded, 16)
            sp.dma_start(cst[:], t["consts"][:, 0:NCONST]).then_inc(const_loaded, 16)
            for name, o, n in (("norm_mix", G_MIX, 16), ("norm_mem", G_MEM, 16), ("norm_cross", G_CROSS, 16),
                               ("norm_final", G_FINAL, 16), ("gdn_norm", G_GDN, 1), ("pool_scale", G_POOL, 8)):
                src = t[name].rearrange("(o n) -> o n", o=1) if name == "norm_final" else t[name]
                sp.dma_start(vrow[o:o + n, 0, :], src.rearrange("o (k p) -> (o k) p", p=P)).then_inc(vec_loaded, 16)
            sp.dma_start(vrow[0:NCONV, 1, :], t["conv_w"].rearrange("o j (k p) -> (o j k) p", p=P)).then_inc(vec_loaded, 16)
            sp.dma_start(scrow[0:24, :], t["state_conv"].rearrange("o b j n -> (o b j) n")).then_inc(vec_loaded, 16)
            sp.wait_ge(x_loaded, 16)
            sp.dma_start(xin[1][:], t["mem_prompt"][0, P:MEM, :]).then_inc(x_loaded, 16)
            for q in range(3):
                sp.dma_start(raw[q][:], source("mem", 0, q)).then_inc(w_loaded[q], 16)
            sp.wait_ge(x_loaded, 32)

            sp.wait_ge(x_scaled, 1)
            sp.dma_start(xin[0][:], t["x_prompt"][0, 0:P, :]).then_inc(x_loaded, 16)

            def group(j, v, x, store_v):
                for q in range(4):
                    load_ahead(sp, "mem", j, q, v)
                    if q == 0 and not (isinstance(j, int) and j == 0) and not store_v:
                        store_keys_turned(sp, j - 1)
                    if q == 1 and not (isinstance(j, int) and j == 0):
                        store_k_or_v(sp, j - 1, store_v)
                    if q == 2 and x == "x":
                        sp.wait_ge(x_scaled, j + 3)
                        sp.wait_ge(x_turned, 8 * (j + 1) + 4)
                        if isinstance(j, int) and j == 3:
                            sp.dma_start(xin[0][0:NS, :], t["x_sample"].rearrange("b t d -> (b t) d")).then_inc(x_loaded, 16)
                        else:
                            sp.dma_start(xin[0][:], t["x_prompt"][0, bass.ds(j * P + P, P), :]).then_inc(x_loaded, 16)
                    if q == 2 and x is not None:
                        rows = NS if x == "sample" else P
                        sp.wait_ge(x_bank, 8 * (j + 1) + 4)
                        sp.dma_start(xT_d[:, :, bass.ds((j + 1) * P - P, rows)].rearrange("k p r -> p k r"),
                                     xts[:, :, 0:rows]).then_inc(xts_stored, 16)

            group(0, False, "x", False)
            with sp.Fori(1, 3) as j:
                group(j, False, "x", False)
            group(3, False, "x", False)
            group(4, True, "sample", False)
            with sp.Fori(5, 7) as j:
                group(j, True, None, True)
            sp_rows(sp, None)
            group(7, True, None, True)

        def pe_mem(pe):
            pe.wait_ge(const_loaded, 16)
            pe.wait_ge(vec_loaded, 16 * 8)
            pe.transpose(dk[:, 3, 0:NGAIN], vrow[0:NGAIN, 0, :], ident[0:NGAIN, 0:NGAIN])
            pe.transpose(dk[:, 3, P:P + NCONV], vrow[0:NCONV, 1, :], ident[0:NCONV, 0:NCONV]).then_inc(vec_turned, 1)
            for k in range(NQKV):
                mm = pe.transpose(pj[:, k // 16, (k % 16) * 24:(k % 16) * 24 + 24], scrow[0:24, k * P:(k + 1) * P],
                                  ident[0:24, 0:24])
            mm.then_inc(vec_turned, 1)

            def turn_mem(c):
                def step(pe):
                    if c < 2:
                        pe.wait_ge(x_scaled, c + 1)
                    x_turn(pe, (xst, xsm)[c % 2], c, c, c // 2, P)
                return step

            def split_mem(c):
                return lambda pe: pe.wait_ge(x_bank, c)
            for c in range(3):
                turn_mem(c)(pe)
            split_mem(2)(pe)
            pe.wait_ge(vec_ready, 2)

            def turn_out(q, w):
                def step(pe):
                    pe.wait_ge(pj_read, w)
                    at_least(pe, mst_ready, w - 1)
                    for m in range(2):
                        mm = pe.transpose(dk[:, 3, m * P:(m + 1) * P], kts[:, (q + 3) % 4, m * P:(m + 1) * P], ident)
                    mm.then_inc(m_turned, 1)
                return step

            def group(j, x):
                rows = NS if x == "sample" else P
                for q in range(4):
                    steps = {}
                    if x is not None:
                        def turn(b):
                            def step(pe):
                                if b == 0:
                                    pe.wait_ge(x_loaded, 16 * (j + 3))
                                if b == 4:
                                    pe.wait_ge(x_scaled, j + 3)
                                x_turn(pe, xin[0] if b < 4 else xst, 8 * (j + 1) + b, b + 2, b % 4, rows)
                            return step
                        steps = {5: [turn(2 * q)], 12: [turn(2 * q + 1)]}
                        if isinstance(j, int) and j == 0 and q == 0:
                            steps = {0: [turn_mem(3)], 1: [turn_mem(4)], 3: [split_mem(4), turn_mem(5)], 4: [turn_mem(6)],
                                     5: [turn_mem(7)], 7: [split_mem(6)], 11: [split_mem(8), turn(0)], 13: [turn(1)]}
                    if not (isinstance(j, int) and j == 0 and q == 0):
                        steps[8] = [turn_out(q, 4 * j + q)]
                    multiply(pe, "mem", j, q, tokens(hm_hi), tokens(hm_lo), MEM, steps)

            group(0, "x")
            with pe.Fori(1, 4) as j:
                group(j, "x")
            group(4, "sample")
            with pe.Fori(5, 8) as j:
                group(j, None)
            turn_out(0, 32)(pe)

        def act_mem(act):
            act.wait_ge(const_loaded, 16)
            for n in range(2):
                x_stats(act, n, xin[n], P)
            cast_high(act, "mem", 0, 0)
            act.wait_ge(vec_ready, 1)
            for c in range(8):
                x_take_high(act, c, c, c // 2, hm_hi, (c % 2) * P, P, G_MEM)

            def group(j, x, keys):
                rows = NS if x == "sample" else P
                for q in range(4):
                    cast_high(act, "mem", j, q + 1)
                    if x is not None and q == 1:
                        x_stats(act, j + 2, xin[0], rows)
                    if x is not None and q > 1:
                        for b in (2 * q, 2 * q + 1):
                            x_take_high(act, 8 * (j + 1) + b, b + 2, b % 4, a_hi, j * P, rows, G_MIX)
                    act.wait_ge(tile_done, 4 * j + q + 1)
                    at_least(act, m_turned, 4 * j + q - 3)
                    if q == 0 and keys:
                        at_least(act, kts_stored, 16 * j)
                    act.activation(kts[:, q, :], product(q, MEM), ACT.Copy).then_inc(pj_read, 1)

            group(0, "x", True)
            with act.Fori(1, 4) as j:
                group(j, "x", True)
            group(4, "sample", True)
            with act.Fori(5, 8) as j:
                group(j, None, False)

        def dve_mem(dve):
            x_scale(dve, 0, xin[0], P)
            dve.wait_ge(vec_turned, 1)
            dve.tensor_copy(gain[:], dk[:, 3, 0:NGAIN])
            dve.tensor_copy(convw[:].rearrange("p j g h -> p (j g h)"), dk[:, 3, P:P + NCONV]).then_inc(vec_ready, 1)
            dve.wait_ge(vec_ready, 1)
            x_scale(dve, 1, xin[1], P)
            dve.wait_ge(vec_turned, 2)
            flat = sct[:].rearrange("p g h b j -> p (g h b j)")
            dve.tensor_copy(flat[:, 0:384], pj[:, 0, 0:384])
            dve.tensor_copy(flat[:, 384:576], pj[:, 1, 0:192]).then_inc(vec_ready, 1)
            split_low(dve, "mem", 0, 0)
            for c in range(8):
                x_take_low(dve, c, c, c // 2, hm_hi, hm_lo, (c % 2) * P, P, G_MEM)

            def read_out(q, w):
                dve.wait_ge(m_turned, w)
                if q == 1:
                    at_least(dve, mst_stored, 4 * (w - 1))
                dve.tensor_copy(mst[:, :, (q + 3) % 4 * P:(q + 3) % 4 * P + P],
                                dk[:, 3, 0:2 * P].rearrange("p (m n) -> p m n", m=2)).then_inc(mst_ready, 1)

            def group(j, x):
                rows = NS if x == "sample" else P
                for q in range(4):
                    split_low(dve, "mem", j, q + 1)
                    if x is not None:
                        for b in (2 * q, 2 * q + 1):
                            if b < 4:
                                dve.wait_ge(x_turned, 8 * (j + 1) + b + 1)
                                if b == 0:
                                    at_least(dve, xts_stored, 16 * j)
                                dve.tensor_copy(xts[:, 4 * b:4 * b + 4, 0:rows],
                                                dk[:, (b + 2) % 3, 0:4 * rows].rearrange("p (m r) -> p m r", m=4)).then_inc(x_bank, 1)
                            else:
                                x_take_low(dve, 8 + 4 * j + b - 4, b + 2, b % 4, a_hi, a_lo, j * P, rows, G_MIX)
                            if b == 2 * q and not (isinstance(j, int) and j == 0 and q == 0):
                                read_out(q, 4 * j + q)
                        if q == 1:
                            x_scale(dve, j + 2, xin[0], rows)
                    else:
                        read_out(q, 4 * j + q)

            group(0, "x")
            with dve.Fori(1, 4) as j:
                group(j, "x")
            group(4, "sample")
            with dve.Fori(5, 8) as j:
                group(j, None)
            read_out(0, 32)

        low_area = area(M_W, M_HIMIX)
        ext = low_area("ext", [EXTN])
        yq = low_area("yq", [3, EXTN])
        st = low_area("st", [3, 2, P])
        ecol = low_area("ecol", [NB, 3])
        ecol_ready = sem("ecol_ready")
        hw = low_area("hw", [4, 3])
        hc = low_area("hc", [4, 5])
        take = area(M_DELTA, M_ROWS)
        kq = take("kq", [3, TOK])
        vs = take("vs", [TOK])
        gcb = take("gcb", [TOK])
        betab = take("betab", [TOK])
        dd = take("dd", [2, TOK])
        at_ = take("at", [CH, P])
        lt = take("lt", [CH, P])
        ltm = take("ltm", [CH, P])
        x1 = take("x1", [3, CH, P])
        vbk = take("vbk", [2 * TOK])
        smp = take("smp", [12, NS])
        SQ = put("sq", [2, TOK], F32, M_DELTA + 8 * TOK + 3 * CH * P)
        take = area(M_B + 10 * TOK, M_B + 16 * TOK)
        s0 = take("s0", [NB, P])
        zraw = take("zraw", [TOK])
        zs = take("zs", [TOK])
        sst = take("sst", [2, P])
        rr = take("rr", [P])
        vn = take("vn", [P])
        kds = take("kds", [P])
        rs_s = take("rs_s", [P])
        vns = take("vns", [P])
        mixo = put("mixo", [KT, TOK], F32, M_B)

        d_, db_ = dd[:, 0, 0:SEQ].rearrange("p (c n) -> p c n", c=CH), dd[:, 1, 0:SEQ].rearrange("p (c n) -> p c n", c=CH)
        tt_, uu, p1 = x1[:, 0], x1[:, 1], x1[:, 2]
        rn = vbk[:, 0:2 * TOK]
        vb = vbk[:, 0:SEQ].rearrange("p (c n) -> p c n", c=CH)
        kd = vbk[:, SEQ:2 * SEQ].rearrange("p (c n) -> p c n", c=CH)
        ds_, dbs, lts, us, ts_, p1s, ats, rt, tmp, qs_, os_, slm = (smp[:, i, :] for i in range(12))
        slm_ready = sem("slm_ready")
        incl = cst[:, C_INCL:C_INCL + P]
        lev = lambda l: cst[:, C_LEV + l * P:C_LEV + (l + 1) * P]
        S_ = slice(0, NS)

        def per_chunk(x):
            return x.unsqueeze(1).to_broadcast([P, CH, P])

        (row_ready, row_stored, row_loaded, s0_loaded, hw_ready, hc_ready, ext_state, ext_turned, st_ready, st_stored,
         conv_step, conv_done) = (sem(n) for n in (
            "row_ready", "row_stored", "row_loaded", "s0_loaded", "hw_ready", "hc_ready", "ext_state", "ext_turned",
            "st_ready", "st_stored", "conv_step", "conv_done"))
        (qk_silu, vz_silu, sq_done, ssq_done, ln_done, rn_done, d_ready, d_exp, eg_ready, kq_normed, qg_ready,
         dmi_ready, db_ready, kk_done, at_ready, lt_ready, u_seed, u_ready, kd_ready, v_turned, vb_ready) = (
            sem(n) for n in (
                "qk_silu", "vz_silu", "sq_done", "ssq_done", "ln_done", "rn_done", "d_ready", "d_exp", "eg_ready",
                "kq_normed", "qg_ready", "dmi_ready", "db_ready", "kk_done", "at_ready", "lt_ready", "u_seed",
                "u_ready", "kd_ready", "v_turned", "vb_ready"))
        (t0_done, t_ready, ltm_ready, p1_done, p1_ready, tu_done, u_next, sp1_done, sp1_ready, su_done, us_ready) = (
            sem(n) for n in ("t0_done", "t_ready", "ltm_ready", "p1_done", "p1_ready", "tu_done", "u_next", "sp1_done",
                             "sp1_ready", "su_done", "us_ready"))
        (ks_done, r_ready, vn_done, vn_ready, so_done, s_ready, s_stored, ksq_done, qs_ready, rt_step, rt_ready,
         rt_turned, rs_ready, vns_done, vns_ready, vx_ready, os_done, os_ready, s0_scaled, sup_done, s0_new,
         s0_stored) = (sem(n) for n in (
            "ks_done", "r_ready", "vn_done", "vn_ready", "so_done", "s_ready", "s_stored", "ksq_done", "qs_ready",
            "rt_step", "rt_ready", "rt_turned", "rs_ready", "vns_done", "vns_ready", "vx_ready", "os_done", "os_ready",
            "s0_scaled", "sup_done", "s0_new", "s0_stored"))
        o_squared, osum_done, oln_done, rno_ready, rz_ready, oa_done = (sem(n) for n in (
            "o_squared", "osum_done", "oln_done", "rno_ready", "rz_ready", "oa_done"))
        sqo, rno = dd[:, 0, :], dd[:, 1, :]
        vx = put("vx", [NB, P], F32, M_DELTA + 6 * TOK)

        def sample3(x):
            return x[:, SEQ:TOK].rearrange("p (b t) -> p b t", b=NB)

        take = area(M_W + 4096, M_W + 8192)
        ab_raw = take("ab_raw", [KT, 16])
        ab_f = take("ab_f", [KT, 64])
        ab_hi = take("ab_hi", [KT, 64], F32R)
        ab_lo = take("ab_lo", [KT, 64], F32R)
        take = area(M_B, M_B + 10 * TOK)
        r_x, r_e, r_w, r_l, r_g, r_h = (take(f"r_{n}", [TOK]) for n in "xewlgh")
        r_beta, r_egl, r_nb = (take(f"r_{n}", [TOK]) for n in ("beta", "egl", "nb"))
        head_col = put("head_col", [4], F32, M_W + 8192 - 8)
        ab_loaded, ab_zero, ab_ready, ab_high, ab_low, ab_done, rowa, rowd, col_turned, cols_ready = (sem(n) for n in (
            "ab_loaded", "ab_zero", "ab_ready", "ab_high", "ab_low", "ab_done", "rowa", "rowd", "col_turned",
            "cols_ready"))
        H_ = slice(0, HEADS)

        def sp_rows(sp, q):
            if q is None:
                sp.wait_ge(x_turned, 48)
                sp.wait_ge(xts_stored, 80)
                with nc.allow_non_contiguous_dma(reason="16 columns"):
                    sp.dma_start(ab_raw[:], w_in[:, :, COL_A:COL_A + 16]).then_inc(ab_loaded, 16)
                    sp.dma_start(head_col[H_, 0:1], t["dt_bias"].rearrange("o h -> h o")).then_inc(ab_loaded, 16)
                    sp.dma_start(head_col[H_, 1:2], t["a_log"].rearrange("o h -> h o")).then_inc(ab_loaded, 16)
            if q == 3:
                sp.wait_ge(row_ready, 1)
                sp.dma_start(row_d[0], r_g[H_, :]).then_inc(row_stored, 16)
                sp.dma_start(row_d[1], r_beta[H_, :]).then_inc(row_stored, 16)

        def pool_rows(pool):
            pool.wait_ge(x_turned, 48)
            pool.memset(ab_f[:], 0.0).then_inc(ab_zero, 1)
            pool.wait_ge(ab_zero, 1)
            pool.wait_ge(ab_loaded, 48)
            pool.tensor_copy(ab_f[:, :, 0:8], ab_raw[:, :, 0:8])
            pool.tensor_copy(ab_f[:, :, 32:40], ab_raw[:, :, 8:16]).then_inc(ab_ready, 1)

        def pe_rows(pe):
            pe.wait_ge(ab_low, 1)
            pe.wait_ge(mst_ready, 32)
            for k in range(KT):
                for m, (wt, x) in enumerate(((ab_hi, a_hi), (ab_hi, a_lo), (ab_lo, a_hi))):
                    for b in range(2):
                        mm = pe.matmul(dk[0:64, b, 0:HALF], wt[:, k, :], x[:, k, b * HALF:(b + 1) * HALF],
                                       start=(k == 0 and m == 0), stop=(k == KT - 1 and m == 2))
            mm.then_inc(ab_done, 1)

        def act_rows(act, q):
            na = [0]

            def step(ins):
                na[0] += 1
                ins.then_inc(rowa, 1)
                act.wait_ge(rowa, ACT_ROWS_BEFORE[q] + na[0])
            if q == 0:
                act.wait_ge(ab_ready, 1)
                act.activation(ab_hi[:], ab_f[:], ACT.Copy).then_inc(ab_high, 1)
                step(act.activation(head_col[H_, 2:3], head_col[H_, 1:2], ACT.Exp))
                step(act.activation(head_col[H_, 3:4], head_col[H_, 2:3], ACT.Copy, scale=-1.0))
            if q == 1:
                act.wait_ge(ab_done, 1)
                step(act.activation(halves(r_x[H_, :]), dk[H_, 0:2, 0:HALF], ACT.Identity, bias=head_col[H_, 0:1]))
                step(act.activation(halves(r_beta[H_, :]), dk[32:40, 0:2, 0:HALF], ACT.Sigmoid))
                step(act.activation(r_e[H_, :], r_x[H_, :], ACT.Abs))
                step(act.activation(r_e[H_, :], r_e[H_, :], ACT.Exp, scale=-1.0))
                act.wait_ge(rowd, 1)
                step(act.activation(r_l[H_, :], r_w[H_, :], ACT.Ln))
            if q == 2:
                act.wait_ge(rowd, ROWD_GC)
                step(act.activation(r_nb[H_, :], r_g[H_, :], ACT.Exp))
                step(act.activation(r_egl[H_, :], r_egl[H_, :], ACT.Exp))
        ACT_ROWS_BEFORE = {0: 0, 1: 2, 2: 7}

        def dve_rows(dve, q):
            def step(ins):
                rd[0] += 1
                ins.then_inc(rowd, 1)
                dve.wait_ge(rowd, rd[0])
            if q == 0:
                dve.wait_ge(ab_high, 1)
                dve.tensor_tensor(ab_lo[:], ab_f[:], ab_hi[:].bitcast(F32), ALU.subtract).then_inc(ab_low, 1)
            if q == 1:
                x, e, w, l, g, u = (r[H_, :] for r in (r_x, r_e, r_w, r_l, r_g, r_h))
                dve.wait_ge(rowa, 6)
                step(dve.tensor_scalar(w, e, 1.0, None, ALU.add))
                step(dve.tensor_scalar(g, w, 1.0, None, ALU.is_equal))
                step(dve.scalar_tensor_tensor(u, w, -1.0, g, ALU.add, ALU.add))
                step(dve.reciprocal(u, u))
                dve.wait_ge(rowa, 7)
                step(dve.tensor_tensor(l, l, g, ALU.add))
                step(dve.tensor_tensor(l, l, u, ALU.mult))
                step(dve.tensor_tensor(l, l, e, ALU.mult))
                step(dve.scalar_tensor_tensor(l, x, 0.0, l, ALU.max, ALU.add))
                step(dve.tensor_scalar(g, l, head_col[H_, 3:4], None, ALU.mult))
                src, dst = g, u
                for s in (1, 2, 4, 8, 16, 32, 64, 128):
                    if s < 128:
                        a, b = (r[:, 0:SEQ].rearrange("p (c n) -> p c n", c=CH) for r in (src, dst))
                        dve.tensor_copy(b[:, :, 0:s], a[:, :, 0:s])
                        dve.tensor_tensor(b[:, :, s:P], a[:, :, s:P], a[:, :, 0:P - s], ALU.add)
                    else:
                        dve.tensor_copy(dst[:, 0:SEQ], src[:, 0:SEQ])
                    a, b = (r[:, SEQ:TOK].rearrange("p (c n) -> p c n", c=NB) for r in (src, dst))
                    m = s if s < NT else NT
                    last = dve.tensor_copy(b[:, :, 0:m], a[:, :, 0:m])
                    if s < NT:
                        last = dve.tensor_tensor(b[:, :, s:NT], a[:, :, s:NT], a[:, :, 0:NT - s], ALU.add)
                    step(last)
                    src, dst = dst, src
                a, b = (r[H_, 0:SEQ].rearrange("p (c n) -> p c n", c=CH) for r in (r_g, r_egl))
                dve.tensor_tensor(b, a[:, :, P - 1:P].to_broadcast([HEADS, CH, P]), a, ALU.subtract)
                a, b = (r[H_, SEQ:TOK].rearrange("p (c n) -> p c n", c=NB) for r in (r_g, r_egl))
                step(dve.tensor_tensor(b, a[:, :, NT - 1:NT].to_broadcast([HEADS, NB, NT]), a, ALU.subtract))
                assert rd[0] == ROWD_GC
            if q == 2:
                dve.wait_ge(rowa, 9)
                dve.scalar_tensor_tensor(r_nb[H_, :], r_nb[H_, :], -1.0, r_beta[H_, :], ALU.mult, ALU.mult).then_inc(row_ready, 1)
            if q == 3:
                dve.wait_ge(col_turned, 1)
                dve.tensor_copy(cols[:, :, 0:4, :], dk[:, 2, 0:128].rearrange("p (q b h) -> p q b h", q=4, b=4))
                dve.tensor_copy(cols[S_, :, 4, :], dk[S_, 2, 128:160].rearrange("p (q h) -> p q h", q=4)).then_inc(cols_ready, 1)
        rd = [0]
        ROWD_GC = 18

        def pe_cols(pe):
            pe.wait_ge(row_ready, 1)
            for i, r in enumerate((r_g, r_beta, r_egl, r_nb)):
                for b in range(4):
                    pe.transpose(dk[:, 2, i * 32 + b * 8:i * 32 + b * 8 + 8], r[H_, b * P:(b + 1) * P], ident[H_, H_])
                mm = pe.transpose(dk[S_, 2, 128 + i * 8:136 + i * 8], r[H_, SEQ:TOK], ident[H_, H_])
            mm.then_inc(col_turned, 1)

        def ext_prompt(x):
            return x[:, 3:3 + SEQ]

        def ext_sample(x):
            return x[:, 3 + SEQ:EXTN].rearrange("p (b s) -> p b s", b=NB)

        def pool_ext(pool, h, q):
            if isinstance(h, int) and h == 0 and q == 0:
                pool.wait_ge(x_turned, 48)
                pool.memset(ext[:, 0:3], 0.0)
            at_least(pool, conv_done, 3 * h + q)
            at_least(pool, ext_turned, 3 * h + q)
            pool.tensor_copy(ext_sample(ext)[:, :, 0:3], sct[:, q, bass.ds(h, 1), :, :]).then_inc(ext_state, 1)

        def pool_last(pool, h, q):
            pool.wait_ge(pj_read, 4 * (8 + h) + q + 1)
            at_least(pool, ext_turned, 3 * h + q)
            pool.tensor_tensor(ecol[:], ext_sample(ext)[:, :, NT:CSEG], ones[:, 0:3 * NB].rearrange("p (b j) -> p b j", b=NB),
                               ALU.mult).then_inc(ecol_ready, 1)

        def act_take(act, h, q):
            act.wait_ge(tile_done, 4 * (8 + h) + q + 1)
            if q == 3:
                at_least(act, vz_silu, h)
                if isinstance(h, int) and h == 0:
                    act.wait_ge(tile_done, 32)
                act.activation(halves(zraw[:]), product(q), ACT.Copy).then_inc(pj_read, 1)
                return
            b = 2 * (q % 2)
            act.wait_ge(ext_state, 3 * h + q + 1)
            act.activation(ext[:, 3:3 + HALF], pj[:, b, 0:HALF], ACT.Copy)
            act.activation(ext[:, 3 + HALF:3 + SEQ], pj[:, b + 1, 0:SEQ - HALF], ACT.Copy)
            act.activation(ext_sample(ext)[:, :, 3:CSEG],
                           pj[:, b + 1, SEQ - HALF:HALF].rearrange("p (b t) -> p b t", b=NB), ACT.Copy).then_inc(pj_read, 1)

        def pe_ext(h, q):
            def step(pe):
                pe.wait_ge(ecol_ready, 3 * h + q + 1)
                pe.transpose(pj[0:3, 2 * (q % 2), 0:P], ext[:, SEQ:SEQ + 3], ident)
                pe.transpose(pj[0:24, 2 * (q % 2), P:2 * P], ecol[:].rearrange("p b j -> p (b j)"), ident).then_inc(ext_turned, 1)
            return step

        def act_st(act, h, q):
            act.wait_ge(ext_turned, 3 * h + q + 1)
            at_least(act, st_stored, 96 * h)
            act.activation(st[0:3, q, 0, :], pj[0:3, 2 * (q % 2), 0:P], ACT.Copy)
            act.activation(st[0:24, q, 1, :], pj[0:24, 2 * (q % 2), P:2 * P], ACT.Copy).then_inc(st_ready, 1)

        def sp_st(sp, h, q):
            sp.wait_ge(st_ready, 3 * h + q + 1)
            c = bass.ds((h + 1) * P + (q * MIX - P), P)
            sp.dma_start(t["conv_prompt"][0, 0, :, c], st[0:3, q, 0, :]).then_inc(st_stored, 16)
            sp.dma_start(t["conv_sample"].rearrange("o b j n -> (o b j) n")[:, c], st[0:24, q, 1, :]).then_inc(st_stored, 16)

        def dve_conv(dve, h, q):
            if q == 0:
                at_least(dve, conv_done, 3 * h)
                dve.tensor_copy(hw[:], convw[:, :, :, bass.ds(h, 1)].rearrange("p j g o -> p j (g o)")).then_inc(hw_ready, 1)
                dve.wait_ge(hw_ready, h + 1)
            dve.wait_ge(pj_read, 4 * (8 + h) + q + 1)
            at_least(dve, qk_silu if q < 2 else vz_silu, h)
            y = yq[:, q, 0:YN]
            dve.tensor_scalar(y, ext[:, 0:YN], hw[:, 0, q:q + 1], None, ALU.mult).then_inc(conv_step, 1)
            for j in range(1, 4):
                dve.wait_ge(conv_step, 9 * h + 3 * q + j)
                a = dve.scalar_tensor_tensor(y, ext[:, j:j + YN], hw[:, j, q:q + 1], y, ALU.mult, ALU.add)
                a.then_inc(conv_step if j < 3 else conv_done, 1)

        def act_delta(act, n, q, cast, rows):
            if q in (0, 3):
                cast()
                rows()
            if q == 0:
                at_least(act, oa_done, n)
                act.wait_ge(conv_done, 3 * n + 3)
                for y, o in ((yq[:, 0], kq[:, 1]), (yq[:, 1], kq[:, 0])):
                    act.activation(o[:, 0:SEQ], y[:, 0:SEQ], ACT.Silu)
                    a = act.activation(sample3(o), ext_sample(y)[:, :, 0:NT], ACT.Silu)
                a.then_inc(qk_silu, 1)
                act.wait_ge(qk_silu, n + 1)
                act.activation(SQ[:], kq[:, 0:2], ACT.Square).then_inc(sq_done, 1)
                act.activation(vs[:, 0:SEQ], yq[:, 2, 0:SEQ], ACT.Silu)
                act.activation(sample3(vs), ext_sample(yq[:, 2])[:, :, 0:NT], ACT.Silu)
                act.wait_ge(pj_read, 4 * (8 + n) + 4)
                act.activation(zs[:], zraw[:], ACT.Silu).then_inc(vz_silu, 1)
                act.wait_ge(ssq_done, n + 1)
                act.activation(rn.rearrange("p (b m) -> p b m", b=4), dk[:, 0:4, 0:HALF], ACT.Ln, bias=eps_col).then_inc(ln_done, 1)
                act.wait_ge(ln_done, n + 1)
                act.activation(rn[:, 0:TOK], rn[:, 0:TOK], ACT.Exp, scale=-0.5)
                act.activation(rn[:, TOK:2 * TOK], rn[:, TOK:2 * TOK], ACT.Exp, scale=-0.5,
                               bias=cst[:, C_LNQ:C_LNQ + 1]).then_inc(rn_done, 1)
                act.wait_ge(d_ready, n + 1)
                act.activation(dd[:, 0, 0:SEQ], dd[:, 0, 0:SEQ], ACT.Exp)
                act.activation(ds_[S_, :], ds_[S_, :], ACT.Exp).then_inc(d_exp, 1)
                act.activation(gcb[:], gcb[:], ACT.Exp).then_inc(eg_ready, 1)
            if q == 1:
                act.wait_ge(t0_done, n + 1)
                act.activation(tt_, dk[:, 0, :].rearrange("p (c n) -> p c n", c=CH), ACT.Copy)
                act.activation(ts_[S_, :], dk[S_, 1, 0:NS], ACT.Copy).then_inc(t_ready, 1)
            for l in range(1, LEVELS):
                if LEVEL_PHASE[l] == q:
                    act.wait_ge(p1_done, 6 * n + l)
                    act.activation(p1, dk[:, 0, :].rearrange("p (c n) -> p c n", c=CH), ACT.Copy).then_inc(p1_ready, 1)
                    if l == 1:
                        act.wait_ge(sp1_done, n + 1)
                        act.activation(p1s[S_, :], dk[S_, 3, 0:NS], ACT.Copy).then_inc(sp1_ready, 1)
                    if l in (1, 4):
                        cast()
                        rows()
            if q == 3:
                act.wait_ge(so_done, 4 * n + 4)
                act.wait_ge(vx_ready, n + 1)
                act.wait_ge(sup_done, n + 1)
                act.activation(sqo[:, 0:SEQ], dk[:, 3, :], ACT.Square)
                act.wait_ge(os_ready, n + 1)
                act.activation(sqo[:, SEQ:TOK], os_, ACT.Square).then_inc(o_squared, 1)
                act.wait_ge(osum_done, n + 1)
                act.activation(halves(rno), dk[:, 0:2, 0:HALF], ACT.Ln, scale=1.0 / P, bias=eps_col).then_inc(oln_done, 1)
                act.wait_ge(oln_done, n + 1)
                act.activation(rno, rno, ACT.Exp, scale=-0.5).then_inc(rno_ready, 1)


        DVE_CONV, DVE_SPLIT, CONV_C = (1, 4), (2, 5), 3
        LTM_PHASE = {l: 1 if l < 5 else 2 for l in range(1, LEVELS)}
        LEVEL_PHASE = {l: 1 if l < 4 else 2 for l in range(1, LEVELS)}

        def dve_delta(dve, n, q, split, conv):
            if q == 0:
                split()
                conv()
                at_least(dve, oa_done, n)
                dve.wait_ge(cols_ready, 1)
                dve.tensor_copy(hc[:, :, 0:4], cols[:, :, 0:4, bass.ds(n, 1)].rearrange("p q b o -> p q (b o)"))
                dve.tensor_copy(hc[S_, :, 4:5], cols[S_, :, 4, bass.ds(n, 1)]).then_inc(hc_ready, 1)
                dve.wait_ge(hc_ready, n + 1)
                dve.wait_ge(row_loaded, 32 * n + 32)
                for c in range(CH):
                    dve.tensor_scalar(d_[:, c, :], gcb[:, c * P:(c + 1) * P], hc[:, 0, c:c + 1], 0.0, ALU.subtract, ALU.min)
                dve.tensor_scalar(ds_[S_, :], gcb[S_, SEQ:TOK], hc[S_, 0, 4:5], 0.0, ALU.subtract, ALU.min).then_inc(d_ready, 1)
                dve.wait_ge(rn_done, n + 1)
                dve.tensor_tensor(kq[:, 0:2].rearrange("p r n -> p (r n)"), kq[:, 0:2].rearrange("p r n -> p (r n)"), rn,
                                  ALU.mult).then_inc(kq_normed, 1)
                dve.wait_ge(eg_ready, n + 1)
                dve.wait_ge(kq_normed, n + 1)
                dve.tensor_tensor(kq[:, 2], kq[:, 1], gcb[:], ALU.mult).then_inc(qg_ready, 1)
            if q == 1:
                kk = dk[:, 0:2, :].rearrange("p b (c n) -> p (b c) n", n=2 * P)
                dve.wait_ge(kk_done, n + 1)
                dve.tensor_tensor(kd, dk[:, 3, :].rearrange("p (c n) -> p c n", c=CH),
                                  hc[:, 2, 0:4].unsqueeze(2).to_broadcast([P, CH, P]), ALU.mult)
                dve.tensor_scalar(kds[S_, :], dk[S_, 2, P:2 * P], hc[S_, 2, 4:5], None, ALU.mult).then_inc(kd_ready, 1)
                dve.wait_ge(db_ready, n + 1)
                dve.tensor_tensor(at_[:], kk[:, :, P:2 * P], d_, ALU.mult)
                dve.tensor_tensor(ats[S_, :], dk[S_, 2, NS:2 * NS], ds_[S_, :], ALU.mult).then_inc(at_ready, 1)
                dve.tensor_tensor(lt[:], kk[:, :, 0:P], db_, ALU.mult)
                dve.tensor_tensor(lts[S_, :], dk[S_, 2, 0:NS], dbs[S_, :], ALU.mult).then_inc(lt_ready, 1)
                dve.wait_ge(lt_ready, n + 1)
                dve.tensor_tensor(uu, lt[:], per_chunk(lev(0)), ALU.mult)
                dve.tensor_tensor(us[S_, :], lts[S_, :], cst[S_, C_SL1:C_SL1 + NS], ALU.mult).then_inc(u_seed, 1)
                dve.wait_ge(u_seed, n + 1)
                dve.tensor_tensor(uu, uu, per_chunk(ident), ALU.add)
                dve.tensor_tensor(us[S_, :], us[S_, :], ident[S_, S_], ALU.add).then_inc(u_ready, 1)
                dve.wait_ge(v_turned, n + 1)
                dve.tensor_tensor(vb, dk[:, 3, :].rearrange("p (c n) -> p c n", c=CH),
                                  hc[:, 1, 0:4].unsqueeze(2).to_broadcast([P, CH, P]), ALU.mult).then_inc(vb_ready, 1)
            for l in range(1, LEVELS):
                if LEVEL_PHASE[l] == q:
                    dve.wait_ge(tu_done, 6 * n + l)
                    if l < LEVELS - 1:
                        dve.tensor_tensor(tt_, tt_, dk[:, 1, :].rearrange("p (c n) -> p c n", c=CH), ALU.subtract)
                    dve.tensor_tensor(uu, uu, dk[:, 2, :].rearrange("p (c n) -> p c n", c=CH), ALU.subtract).then_inc(u_next, 1)
                    if l == 2:
                        dve.wait_ge(su_done, n + 1)
                        dve.tensor_tensor(us[S_, :], us[S_, :], dk[S_, 3, NS:2 * NS], ALU.subtract).then_inc(us_ready, 1)
                    if l in DVE_CONV:
                        conv()
                    if l in DVE_SPLIT:
                        split()
            if q == 3:
                for c in range(CH):
                    if c > 0:
                        dve.wait_ge(ks_done, 3 * n + c)
                        dve.scalar_tensor_tensor(rr[:], dk[:, 0, 0:P], hc[:, 3, c:c + 1], vb[:, c, :], ALU.mult,
                                                 ALU.add).then_inc(r_ready, 1)
                    dve.wait_ge(vn_done, 4 * n + c + 1)
                    if c == 0:
                        at_least(dve, s_stored, 16 * n)
                    dve.tensor_copy(vn[:], dk[:, 1, 0:P]).then_inc(vn_ready, 1)
                    if c == 0:
                        split()
                    if c == 1:
                        sample_r(dve, n)
                    if c == 2:
                        dve.wait_ge(rt_turned, n + 1)
                        dve.tensor_copy(rs_s[S_, :], dk[S_, 2, P:2 * P]).then_inc(rs_ready, 1)
                    if c == 3:
                        dve.wait_ge(vns_done, n + 1)
                        dve.tensor_copy(vns[S_, :], dk[S_, 0, P:2 * P]).then_inc(vns_ready, 1)
                    dve.wait_ge(so_done, 4 * n + c + 1)
                    if c == 0:
                        dve.tensor_copy(sst[:, 0, :], dk[:, 2, 0:P]).then_inc(s_ready, 1)
                    else:
                        dve.scalar_tensor_tensor(sst[:, c % 2, :], sst[:, (c + 1) % 2, :], gcb[:, c * P + P - 1:c * P + P],
                                                 dk[:, 2, 0:P], ALU.mult, ALU.add).then_inc(s_ready, 1)
                    if c == CONV_C:
                        conv()
                dve.wait_ge(os_done, n + 1)
                dve.tensor_tensor(os_, qs_, dk[:, 2, P:P + NS], ALU.add).then_inc(os_ready, 1)
                dve.wait_ge(sup_done, n + 1)
                dve.wait_ge(s0_scaled, n + 1)
                dve.tensor_tensor(s0[:].rearrange("p (r b) n -> p r (b n)", r=2), s0[:].rearrange("p (r b) n -> p r (b n)", r=2),
                                  dk[:, 0:2, :], ALU.add).then_inc(s0_new, 1)
                dve.wait_ge(rz_ready, n + 1)
                g = gain[:, G_GDN:G_GDN + 1]
                o = mixo[:, bass.ds(n, 1), :].rearrange("p o n -> p (o n)")
                dve.scalar_tensor_tensor(o[:, 0:SEQ], dk[:, 3, :], g, rno[:, 0:SEQ], ALU.mult, ALU.mult)
                dve.scalar_tensor_tensor(o[:, SEQ:TOK], os_, g, rno[:, SEQ:TOK], ALU.mult, ALU.mult).then_inc(oa_done, 1)

        def sample_r(dve, n):
            dve.wait_ge(ksq_done, n + 1)
            ks = dk[:, 2, 256:320].rearrange("p (b r t) -> p b r t", b=NB, r=2)
            dve.tensor_tensor(tmp.rearrange("p (b t) -> p b t", b=NB), ks[:, :, 0, :], sample3(gcb[:]), ALU.mult)
            dve.tensor_copy(qs_.rearrange("p (b t) -> p b t", b=NB), ks[:, :, 1, :]).then_inc(rt_step, 1)
            dve.wait_ge(rt_step, 2 * n + 1)
            dve.tensor_tensor(tmp, vs[:, SEQ:TOK], tmp, ALU.subtract).then_inc(rt_step, 1)
            dve.wait_ge(rt_step, 2 * n + 2)
            dve.tensor_tensor(rt, tmp, betab[:, SEQ:TOK], ALU.mult).then_inc(rt_ready, 1)

        POOL_OLD = (2, 5)

        def pool_delta(pool, n, q, old):
            if q == 0:
                old()
                pool.wait_ge(d_exp, n + 1)
                pool.wait_ge(row_loaded, 32 * n + 32)
                pool.tensor_tensor(d_, d_, per_chunk(incl), ALU.mult)
                pool.tensor_tensor(ds_[S_, :], ds_[S_, :], cst[S_, C_SINCL:C_SINCL + NS], ALU.mult).then_inc(dmi_ready, 1)
                pool.wait_ge(dmi_ready, n + 1)
                pool.tensor_tensor(db_, d_, betab[:, 0:SEQ].rearrange("p (c n) -> p c n", c=CH), ALU.mult)
                pool.tensor_tensor(dbs[S_, :], ds_[S_, :], betab[S_, SEQ:TOK], ALU.mult).then_inc(db_ready, 1)
            if q == 1:
                pool.wait_ge(lt_ready, n + 1)
                pool.tensor_tensor(slm[S_, :], lts[S_, :], cst[S_, C_SL2:C_SL2 + NS], ALU.mult).then_inc(slm_ready, 1)
            for l in range(1, LEVELS):
                if LTM_PHASE[l] == q:
                    pool.wait_ge(lt_ready, n + 1)
                    at_least(pool, p1_done, 6 * n + l - 1)
                    pool.tensor_tensor(ltm[:], lt[:], per_chunk(lev(l)), ALU.mult).then_inc(ltm_ready, 1)
                    if l in POOL_OLD:
                        old()
            if q == 3:
                pool.wait_ge(ksq_done, n + 1)
                pool.wait_ge(s0_loaded, 16 * n + 16)
                pool.tensor_tensor(s0[:], s0[:], sample3(gcb[:])[:, :, NT - 1:NT].to_broadcast([P, NB, P]),
                                   ALU.mult).then_inc(s0_scaled, 1)
                pool.wait_ge(vns_ready, n + 1)
                pool.tensor_tensor(vx[S_, :, :], vns[S_, :].unsqueeze(1).to_broadcast([NS, NB, P]),
                                   cst[S_, C_BM:C_BM + NB].unsqueeze(2).to_broadcast([NS, NB, P]), ALU.mult).then_inc(vx_ready, 1)
                pool.wait_ge(rno_ready, n + 1)
                pool.tensor_tensor(rno, rno, zs[:], ALU.mult).then_inc(rz_ready, 1)

        def pe_delta(n):
            chunk = lambda x, c: x[:, c * P:(c + 1) * P]

            def norms(pe):
                pe.wait_ge(sq_done, n + 1)
                at_least(pe, oa_done, n)
                at_least(pe, s0_new, n)
                for i in range(4):
                    mm = pe.matmul(dk[:, i, 0:HALF], ones, SQ[:, i // 2, (i % 2) * HALF:(i % 2 + 1) * HALF], start=True, stop=True)
                mm.then_inc(ssq_done, 1)

            def gram(pe):
                pe.wait_ge(kq_normed, n + 1)
                for c in range(CH):
                    pe.matmul(dk[:, c // 2, (c % 2) * 256:(c % 2) * 256 + 256].rearrange("p (r n) -> p r n", r=2),
                              chunk(kq[:, 0], c), kq[:, 0:2, c * P:(c + 1) * P], start=True, stop=True)
                pe.matmul(dk[S_, 2, 0:2 * NS].rearrange("p (r n) -> p r n", r=2), kq[:, 0, SEQ:TOK], kq[:, 0:2, SEQ:TOK],
                          start=True, stop=True)
                pe.transpose(dk[S_, 2, P:2 * P], kq[:, 0, SEQ:TOK], ident)
                for c in range(CH):
                    mm = pe.transpose(chunk(dk[:, 3], c), chunk(kq[:, 0], c), ident)
                mm.then_inc(kk_done, 1)

            def turn_v(pe):
                pe.wait_ge(kd_ready, n + 1)
                pe.wait_ge(vz_silu, n + 1)
                for c in range(CH):
                    mm = pe.transpose(chunk(dk[:, 3], c), chunk(vs, c), ident)
                mm.then_inc(v_turned, 1)

            def turn_u(pe):
                pe.wait_ge(u_ready, n + 1)
                for c in range(CH):
                    pe.transpose(chunk(dk[:, 0], c), uu[:, c, :], ident)
                pe.transpose(dk[S_, 1, 0:NS], us[S_, :], ident[S_, S_]).then_inc(t0_done, 1)

            def level_p(l):
                def step(pe):
                    pe.wait_ge(ltm_ready, 6 * n + l)
                    if l == 1:
                        pe.wait_ge(t_ready, n + 1)
                    else:
                        pe.wait_ge(u_next, 6 * n + l - 1)
                    if l == 1:
                        pe.wait_ge(vb_ready, n + 1)
                        pe.wait_ge(slm_ready, n + 1)
                    for c in range(CH):
                        mm = pe.matmul(chunk(dk[:, 0], c), ltm[:, c, :], tt_[:, c, :], start=True, stop=True)
                    mm.then_inc(p1_done, 1)
                    if l == 1:
                        pe.matmul(dk[S_, 3, 0:NS], slm[S_, :], ts_[S_, :], start=True, stop=True).then_inc(sp1_done, 1)
                return step

            def level_u(l):
                def step(pe):
                    pe.wait_ge(p1_ready, 6 * n + l)
                    if l == 2:
                        pe.wait_ge(sp1_ready, n + 1)
                    if l < LEVELS - 1:
                        for c in range(CH):
                            pe.matmul(chunk(dk[:, 1], c), uu[:, c, :], p1[:, c, :], start=True, stop=True)
                    for c in range(CH):
                        mm = pe.matmul(chunk(dk[:, 2], c), p1[:, c, :], uu[:, c, :], start=True, stop=True)
                    mm.then_inc(tu_done, 1)
                    if l == 2:
                        pe.matmul(dk[S_, 3, NS:2 * NS], p1s[S_, :], us[S_, :], start=True, stop=True).then_inc(su_done, 1)
                return step

            def state_k(c):
                def step(pe):
                    pe.wait_ge(s_ready, 4 * n + c)
                    pe.matmul(dk[:, 0, 0:P], chunk(kq[:, 0], c), sst[:, (c + 1) % 2, :], start=True, stop=True).then_inc(ks_done, 1)
                return step

            def v_new(c):
                def step(pe):
                    if c == 0:
                        pe.wait_ge(u_next, 6 * n + 6)
                        pe.wait_ge(us_ready, n + 1)
                        pe.wait_ge(qg_ready, n + 1)
                        pe.wait_ge(at_ready, n + 1)
                    else:
                        pe.wait_ge(r_ready, 3 * n + c)
                    pe.matmul(dk[:, 1, 0:P], uu[:, c, :], vb[:, 0, :] if c == 0 else rr[:], start=True, stop=True).then_inc(vn_done, 1)
                return step

            def state_o(c):
                def step(pe):
                    pe.wait_ge(vn_ready, 4 * n + c + 1)
                    if c == 1:
                        pe.wait_ge(rt_step, 2 * n + 1)
                    if c == 2:
                        pe.wait_ge(rs_ready, n + 1)
                    pe.matmul(dk[:, 2, 0:P], kd[:, c, :], vn[:], start=True, stop=True)
                    if c > 0:
                        pe.matmul(chunk(dk[:, 3], c), sst[:, (c + 1) % 2, :], chunk(kq[:, 2], c), start=True, stop=False)
                    pe.matmul(chunk(dk[:, 3], c), vn[:], at_[:, c, :], start=(c == 0), stop=True).then_inc(so_done, 1)
                return step

            def sample_ks(pe):
                pe.wait_ge(s0_loaded, 16 * n + 16)
                pe.wait_ge(s_ready, 4 * n + 1)
                for b in range(NB):
                    mm = pe.matmul(dk[:, 2, 256 + 8 * b:264 + 8 * b].rearrange("p (r t) -> p r t", r=2), s0[:, b, :],
                                   kq[:, 0:3:2, SEQ + NT * b:SEQ + NT * (b + 1)], start=True, stop=True)
                mm.then_inc(ksq_done, 1)

            def sample_turn(pe):
                pe.wait_ge(rt_ready, n + 1)
                pe.wait_ge(s_ready, 4 * n + 2)
                pe.transpose(dk[S_, 2, P:2 * P], rt, ident).then_inc(rt_turned, 1)

            def sample_v(pe):
                pe.matmul(dk[S_, 0, P:2 * P], us[S_, :], rs_s[S_, :], start=True, stop=True).then_inc(vns_done, 1)

            def sample_o(pe):
                pe.wait_ge(vns_ready, n + 1)
                pe.wait_ge(s_ready, 4 * n + 4)
                pe.matmul(dk[:, 2, P:P + NS], vns[S_, :], ats[S_, :], start=True, stop=True).then_inc(os_done, 1)

            def sample_s(pe):
                pe.wait_ge(vx_ready, n + 1)
                for r in range(2):
                    mm = pe.matmul(dk[:, r, :], kds[S_, :], vx[S_, 4 * r:4 * r + 4, :].rearrange("p b n -> p (b n)"),
                                   start=True, stop=True)
                mm.then_inc(sup_done, 1)

            def o_norm(pe):
                pe.wait_ge(o_squared, n + 1)
                pe.wait_ge(s0_new, n + 1)
                for b in range(2):
                    mm = pe.matmul(dk[:, b, 0:HALF], ones, sqo[:, b * HALF:(b + 1) * HALF], start=True, stop=True)
                mm.then_inc(osum_done, 1)

            return [norms, gram, turn_v, turn_u] + [f(l) for l in range(1, LEVELS) for f in (level_p, level_u)] + [
                v_new(0), state_o(0), sample_ks, state_k(1), v_new(1), state_o(1), state_k(2), sample_turn, v_new(2),
                state_o(2), state_k(3), v_new(3), sample_v, state_o(3), sample_o, sample_s, o_norm]

        PLACE = [
            (0, 11), (1, 1), (1, 3), (1, 4),
            (1, 5), (1, 6), (1, 8), (1, 8), (1, 12), (1, 14),
            (2, 1), (2, 3), (2, 5), (2, 10), (2, 13), (2, 15),
            (3, 0), (3, 1), (3, 4), (3, 4), (3, 4), (3, 4), (3, 5), (3, 5), (3, 6),
            (3, 7), (3, 8), (3, 9), (3, 9), (3, 10), (3, 11), (3, 12), (3, 14),
        ]

        def delta_steps(n):
            steps = [{}, {}, {}, {}]
            for (q, k), f in zip(PLACE, pe_delta(n)):
                steps[q].setdefault(k, []).append(f)
            return steps

        def sp_delta(sp, n, q):
            if q == 0:
                at_least(sp, oa_done, n)
                for i, o in enumerate((gcb, betab)):
                    sp.dma_start(o[:], row_d[i, bass.ds(n, 1), :].to_broadcast([P, TOK])).then_inc(row_loaded, 16)
                at_least(sp, s0_stored, 16 * n)
                sp.dma_start(s0[:], t["state_delta"][0, :, bass.ds(n, 1), :, :].rearrange("b o k v -> k (b o) v")).then_inc(s0_loaded, 16)

        def sp_delta_out(sp, n):
            sp.wait_ge(s_ready, 4 * n + 4)
            sp.dma_start(t["delta_prompt"][0, 0, bass.ds(n, 1), :, :].rearrange("o k v -> k (o v)"), sst[:, 1, :]).then_inc(s_stored, 16)
            sp.wait_ge(s0_new, n + 1)
            sp.dma_start(t["delta_sample"][0, :, bass.ds(n, 1), :, :].rearrange("b o k v -> k (b o) v"), s0[:]).then_inc(s0_stored, 16)

        def loop_heads(eng, body, peel_last=False):
            body(0)
            body(1)
            with eng.Fori(2, HEADS - 1 if peel_last else HEADS) as h:
                body(h)
            if peel_last:
                body(HEADS - 1)

        def is_first(h):
            return isinstance(h, int) and h == 0

        def sp_heads(sp):
            def body(h):
                for q in range(4):
                    load_ahead(sp, "head", h, q)
                    if is_first(h):
                        if q == 1:
                            store_k_or_v(sp, 7, True)
                        sp_rows(sp, q)
                    else:
                        if q == 0:
                            sp.wait_ge(row_stored, 32)
                        sp_delta(sp, h - 1, q)
                    if q > 0:
                        sp_st(sp, h, q - 1)
                    if q == 3 and not is_first(h):
                        sp_delta_out(sp, h - 1)
            loop_heads(sp, body, True)

        def act_heads(act):
            def body(h):
                for q in range(4):
                    def cast():
                        cast_high(act, "head", h, q + 1)

                    def rows():
                        if q > 0:
                            act_st(act, h, q - 1)
                    if is_first(h):
                        cast()
                        act_rows_all(act, q)
                        if q == 3:
                            act.wait_ge(mst_stored, 128)
                        rows()
                    else:
                        act_delta(act, h - 1, q, cast, rows)
                    act_take(act, h, q)
            loop_heads(act, body)

        def act_rows_all(act, q):
            for part in ((0, 1), (), (2,), ())[q]:
                act_rows(act, part)

        def dve_heads(dve):
            def body(h):
                for q in range(4):
                    def split():
                        split_low(dve, "head", h, q + 1)

                    def conv():
                        if q > 0:
                            dve_conv(dve, h, q - 1)
                    if is_first(h):
                        split()
                        for part in ((0, 1), (), (2,), (3,))[q]:
                            dve_rows(dve, part)
                        if q == 3:
                            dve.wait_ge(mst_stored, 128)
                        conv()
                    else:
                        dve_delta(dve, h - 1, q, split, conv)
            loop_heads(dve, body)

        def pool_heads(pool):
            pool_rows(pool)

            def body(h):
                for q in range(4):
                    if q > 0:
                        pool_last(pool, h, q - 1)
                    if is_first(h) and q == 3:
                        pool.wait_ge(mst_stored, 128)
                    def old():
                        if q < 3:
                            pool_ext(pool, h, q)
                    if is_first(h):
                        old()
                    else:
                        pool_delta(pool, h - 1, q, old)
            loop_heads(pool, body)

        def pe_heads(pe):
            def body(h):
                steps = delta_steps(h - 1) if not is_first(h) else [{5: [pe_rows]}, {}, {}, {4: [pe_cols]}]
                for q in range(4):
                    if q > 0:
                        steps[q].setdefault(2, []).append(pe_ext(h, q - 1))
                    at_least(pe, st_ready, (3 * h, 0, 3 * h + 1, 3 * h + 2)[q])
                    multiply(pe, "head", h, q, tokens(a_hi), tokens(a_lo), TOK, steps[q])
            loop_heads(pe, body)

        take = area(M_W, M_DELTA)
        ux = take("ux", [UN])
        us_a = take("us_a", [UN])
        us_b = take("us_b", [UN])
        dpool = take("dpool", [2, TOK])
        take = area(M_DELTA, M_HIMIX)
        pw = take("pw", [2, 2, P])
        take = area(M_ROWS, M_END)
        spool = take("spool", [2 * P])
        ust = take("ust", [2, P])
        ucol = take("ucol", [NS])
        mix_hi = put("mix_hi", [KT, TOK], F32R, M_HIMIX)
        mix_lo = put("mix_lo", [KT, TOK], F32R, M_B)
        (spool_loaded, spool_turned, ux_zero, ucol_ready, ux_turned, ust_ready, ust_stored, win_step, d_tile, pw_loaded,
         pooled, ob_done, mix_high, mix_low, old_rows) = (sem(n) for n in (
            "spool_loaded", "spool_turned", "ux_zero", "ucol_ready", "ux_turned", "ust_ready", "ust_stored", "win_step",
            "d_tile", "pw_loaded", "pooled", "ob_done", "mix_high", "mix_low", "old_rows"))

        def u_sample(x):
            return x[:, BUF + SEQ:UN].rearrange("p (b s) -> p b s", b=NB)

        def sp_pool(sp):
            def body(g):
                first = is_first(g)
                for q in range(4):
                    load_ahead(sp, "pool", g, q)
                    if first:
                        sp_delta(sp, HEADS - 1, q)
                    if q == 0:
                        if first:
                            sp.dma_start(t["pool_sample"][0, :, 0:BUF - NT, :], t["state_pool"][0, :, NT:BUF, :]).then_inc(old_rows, 16)
                            sp.wait_ge(ext_state, 24)
                        at_least(sp, spool_turned, 2 * g)
                        sp.dma_start(spool[0:NB * BUF, :], t["state_pool"].rearrange("o b j n -> (o b j) n")[:, bass.ds(g * 256, 256)]).then_inc(spool_loaded, 16)
                        if not first:
                            sp_ust(sp, g - 1, 1)
                            at_least(sp, oa_done, HEADS)
                            at_least(sp, pooled, g - 1)
                            for k in range(2):
                                sp.dma_start(pw[:, k], t["pool_w"][0, bass.ds(g - 1, 1), k * P:(k + 1) * P, :].rearrange(
                                    "o c (d n) -> c (o d) n", d=2)).then_inc(pw_loaded, 16)
                    if q == 3:
                        sp_ust(sp, g, 0)
                if first:
                    sp_delta_out(sp, HEADS - 1)
            for g in range(NG):
                body(g)

        def sp_ust(sp, g, i):
            sp.wait_ge(ust_ready, 2 * g + i + 1)
            c = slice(g * 256 + i * P, g * 256 + i * P + P)
            sp.dma_start(t["pool_prompt"][0, 0, :, c], ust[0:BUF, 0, :]).then_inc(ust_stored, 16)
            for b in range(NB):
                sp.dma_start(t["pool_sample"][0, b, BUF - NT:BUF, c], ust[NT * b:NT * b + NT, 1, :]).then_inc(ust_stored, 16)

        def act_pool(act):
            def body(g):
                first = is_first(g)
                for q in range(4):
                    if not first:
                        cast_high(act, "pool", g, q + 1)
                    w = 4 * (16 + g) + q
                    if q == 0 and not first:
                        act_ust(act, g - 1, 1)
                    if first:
                        def last_rows():
                            if q == 3:
                                act_ust(act, 0, 0)
                        act_delta(act, HEADS - 1, q, lambda: cast_high(act, "pool", 0, q + 1), last_rows)
                    elif q == 3:
                        act_ust(act, g, 0)
                    if q == 0 and g == 1:
                        act.wait_ge(s0_stored, 128)
                        act.wait_ge(s_stored, 128)
                    if g == 1 and q == 2:
                        mix_take_high(act, 0)
                    if g == 2 and q == 2:
                        mix_take_high(act, 1)
                    if g == 3 and q == 2:
                        mix_take_high(act, 2)
                    act.wait_ge(tile_done, w + 1)
                    if q < 2:
                        act.activation(halves(mixo[:, 8 + 2 * g + q, :]), product(q), ACT.Silu).then_inc(pj_read, 1)
                        continue
                    b, i = 2 * (q % 2), q - 2
                    at_least(act, ux_turned, 2 * g + i)
                    at_least(act, d_tile, 2 * g + i)
                    act.wait_ge(ux_zero, 1)
                    act.activation(ux[:, BUF:BUF + HALF], pj[:, b, 0:HALF], ACT.Copy)
                    act.activation(ux[:, BUF + HALF:BUF + SEQ], pj[:, b + 1, 0:SEQ - HALF], ACT.Copy)
                    act.activation(u_sample(ux)[:, :, BUF:USEG],
                                   pj[:, b + 1, SEQ - HALF:HALF].rearrange("p (b t) -> p b t", b=NB), ACT.Copy)
                    act.activation(u_sample(ux)[:, :, 0:BUF],
                                   pj[:, b, HALF:HALF + NB * BUF].rearrange("p (b j) -> p b j", b=NB), ACT.Copy).then_inc(pj_read, 1)
            for g in range(NG):
                body(g)

        def act_ust(act, g, i):
            act.wait_ge(ux_turned, 2 * g + i + 1)
            at_least(act, ust_stored, 16 * 9 * (2 * g + i))
            act.activation(ust[0:BUF, 0, :], pj[0:BUF, 2 * i, 0:P], ACT.Copy)
            act.activation(ust[0:NS, 1, :], pj[0:NS, 2 * i, P:2 * P], ACT.Copy).then_inc(ust_ready, 1)

        MIX_PARTS = ((0, 4), (4, 8), (8, 14), (14, 16))

        def mix_take_high(act, m):
            a, b = MIX_PARTS[m]
            if m < 2:
                act.wait_ge(oa_done, HEADS)
            else:
                act.wait_ge(ob_done, 2 * (m + 1))
            if m == 3:
                act.wait_ge(ust_stored, 16 * 9 * 8)
            act.activation(mix_hi[:, a:b, :], mixo[:, a:b, :], ACT.Copy).then_inc(mix_high, 1)

        def mix_take_low(dve, m):
            a, b = MIX_PARTS[m]
            dve.wait_ge(mix_high, m + 1)
            dve.tensor_tensor(mix_lo[:, a:b, :], mixo[:, a:b, :], mix_hi[:, a:b, :].bitcast(F32), ALU.subtract).then_inc(mix_low, 1)

        def dve_windows(dve, g, i):
            n = 2 * g + i
            dve.wait_ge(pj_read, 4 * (16 + g) + 2 + i + 1)
            src = ux[:]
            for m in range(g + 1):
                dst = (us_a, us_b)[m % 2][:]
                lo = (2 << m) - 1
                dve.tensor_tensor(dst[:, lo:UN], src[:, lo:UN], src[:, lo - (1 << m):UN - (1 << m)], ALU.add).then_inc(win_step, 1)
                wn[0] += 1
                dve.wait_ge(win_step, wn[0])
                src = dst
            other = (us_b, us_a)[g % 2][:]
            if i == 0:
                at_least(dve, pooled, g)
            iw = 1.0 / WINDOWS[g]
            dve.tensor_tensor(other[:, 0:16], src[:, BUF:BUF + 16], cst[:, C_INV + 16 * g:C_INV + 16 * g + 16], ALU.mult).then_inc(win_step, 1)
            wn[0] += 1
            dve.wait_ge(win_step, wn[0])
            dve.tensor_tensor(dpool[:, i, 0:16], other[:, 0:16], ux[:, BUF:BUF + 16], ALU.subtract)
            dve.scalar_tensor_tensor(dpool[:, i, 16:SEQ], src[:, BUF + 16:BUF + SEQ], iw, ux[:, BUF + 16:BUF + SEQ], ALU.mult, ALU.subtract)
            dve.scalar_tensor_tensor(sample3(dpool[:, i]), u_sample(src)[:, :, BUF:USEG], iw, u_sample(ux[:])[:, :, BUF:USEG],
                                     ALU.mult, ALU.subtract).then_inc(d_tile, 1)
        wn = [0]

        def dve_map(dve, g):
            dve.wait_ge(pooled, g + 1)
            for d in range(2):
                o = halves(mixo[:, 8 + 2 * g + d, :])
                dve.scalar_tensor_tensor(o, dk[:, 2 * d:2 * d + 2, 0:HALF], gain[:, G_POOL + 2 * g + d:G_POOL + 2 * g + d + 1],
                                         o, ALU.mult, ALU.mult).then_inc(ob_done, 1)

        def dve_pool(dve):
            for g in range(NG):
                for q in range(4):
                    if g > 0:
                        split_low(dve, "pool", g, q + 1)
                    else:
                        dve_delta(dve, HEADS - 1, q, lambda: split_low(dve, "pool", 0, q + 1), lambda: None)
                    if g > 0 and q == 0:
                        dve_windows(dve, g - 1, 1)
                    if g > 0 and q == 1:
                        dve_map(dve, g - 1)
                    if g > 0 and q == 2:
                        mix_take_low(dve, g - 1)
                    if q == 3:
                        dve_windows(dve, g, 0)

        def pool_pool(pool):
            for g in range(NG):
                for q in range(4):
                    if q == 3:
                        pool_ucol(pool, g, 0)
                    if g == 0:
                        pool_delta(pool, HEADS - 1, q, lambda: None)
                    if g == 0 and q == 0:
                        pool.wait_ge(conv_done, 24)
                        pool.wait_ge(st_stored, 16 * 48)
                        pool.wait_ge(vz_silu, HEADS)
                        pool.memset(ux[:, 0:BUF], 0.0).then_inc(ux_zero, 1)
                    if q == 0 and g > 0:
                        pool_ucol(pool, g - 1, 1)
            pool_ucol(pool, NG - 1, 1)

        def pool_ucol(pool, g, i):
            pool.wait_ge(pj_read, 4 * (16 + g) + 2 + i + 1)
            at_least(pool, ux_turned, 2 * g + i)
            pool.tensor_copy(ucol[:].rearrange("p (b t) -> p b t", b=NB), u_sample(ux[:])[:, :, BUF:USEG]).then_inc(ucol_ready, 1)

        def pe_ux(g, i):
            def step(pe):
                pe.wait_ge(ucol_ready, 2 * g + i + 1)
                pe.transpose(pj[0:BUF, 2 * i, 0:P], ux[:, SEQ:SEQ + BUF], ident)
                pe.transpose(pj[0:NS, 2 * i, P:2 * P], ucol[:], ident).then_inc(ux_turned, 1)
            return step

        def pe_map(g):
            def step(pe):
                pe.wait_ge(d_tile, 2 * g + 2)
                pe.wait_ge(pw_loaded, 32 * g + 32)
                at_least(pe, ob_done, 2 * g)
                pe.wait_ge(oa_done, HEADS)
                for d in range(2):
                    for b in range(2):
                        for k in range(2):
                            mm = pe.matmul(dk[:, 2 * d + b, 0:HALF], pw[:, k, d, :], dpool[:, k, b * HALF:(b + 1) * HALF],
                                           start=(k == 0), stop=(k == 1))
                mm.then_inc(pooled, 1)
            return step

        def pe_pool(pe):
            def body(g):
                first = is_first(g)
                steps = delta_steps(HEADS - 1) if first else [{}, {}, {}, {}]
                if not first:
                    steps[0][9] = [pe_ux(g - 1, 1)]
                    steps[1][4] = [pe_map(g - 1)]
                steps[3].setdefault(2, []).append(pe_ux(g, 0))
                for q in range(4):
                    w = 4 * (16 + g) + q
                    if first and q == 0:
                        pe.wait_ge(st_ready, 24)
                    if not first:
                        pe.wait_ge(ust_ready, (2 * g - 1, 2 * g, 2 * g, 2 * g)[q])
                    if q >= 2:
                        pe.wait_ge(spool_loaded, 16 * g + 16)
                        pe.wait_ge(pj_read, w - 1)
                        pe.transpose(pj[:, 2 * (q % 2), HALF:HALF + NB * BUF], spool[0:NB * BUF, (q - 2) * P:(q - 1) * P],
                                     ident[0:NB * BUF, 0:NB * BUF]).then_inc(spool_turned, 1)
                    multiply(pe, "pool", g, q, tokens(a_hi), tokens(a_lo), TOK, steps[q])
            body(0)
            with pe.Fori(1, NG) as g:
                body(g)

        take = area(M_W, M_HIMIX)
        xr = [take(f"xr{i}", [TOK]) for i in range(2)]
        x2 = [take(f"x2_{i}", [TOK]) for i in range(2)]
        sqx = take("sqx", [TOK])
        acc = take("acc", [TOK])
        xr_loaded = [sem(f"xr_loaded{i}") for i in range(2)]
        x2_stored = [sem(f"x2_stored{i}") for i in range(2)]
        (h_high, h_low, sqx_ready, acc_zero, acc_done) = (sem(n) for n in (
            "h_high", "h_low", "sqx_ready", "acc_zero", "acc_done"))

        def sp_residual(sp, stage, j, q):
            src = xT_d if stage == "out" else x2T_d
            r = (0 if stage == "out" else 16) + 4 * j + q
            if not (isinstance(r, int) and r < 2):
                sp.wait_ge(pj_read, 4 * FIRST[stage] + 4 * j + q - 1)
            sp.dma_start(xr[q % 2][:], src[bass.ds(4 * j + q, 1), :, :].rearrange("k p n -> p (k n)")).then_inc(xr_loaded[q % 2], 16)

        def sp_out(sp):
            def body(j):
                for q in range(4):
                    load_ahead(sp, "out", j, q)
                    if is_first(j) and q == 0:
                        sp.wait_ge(pooled, NG - 1)
                        for k in range(2):
                            sp.dma_start(pw[:, k], t["pool_w"][0, NG - 1, k * P:(k + 1) * P, :].rearrange(
                                "c (d n) -> c d n", d=2)).then_inc(pw_loaded, 16)
                        sp_ust(sp, NG - 1, 1)
                        sp.wait_ge(d_tile, 8)
                        sp.wait_ge(ux_turned, 8)
                    sp_residual(sp, "out", j, q)
                    if q or not is_first(j):
                        sp.wait_ge(pj_read, 80 + 4 * j + q)
                        sp_x2(sp, j if q else j - 1, (q - 1) % 4)
            body(0)
            body(1)
            body(2)
            body(3)

        def sp_x2(sp, j, q):
            sp.dma_start(x2T_d[4 * j + q, :, :], x2[q % 2][:]).then_inc(x2_stored[q % 2], 16)

        def act_out(act):
            def body(j):
                for q in range(4):
                    cast_high(act, "out", j, q + 1)
                    if is_first(j) and q == 0:
                        act_ust(act, NG - 1, 1)
                        mix_take_high(act, 3)
                    i = 4 * j + q
                    act.wait_ge(pj_read, 80 + i + 1)
                    act.activation(a_hi[:, bass.ds(i, 1), :].rearrange("p o n -> p (o n)"), x2[q % 2][:], ACT.Copy,
                                   scale=gain[:, bass.ds(G_CROSS + i, 1)]).then_inc(h_high, 1)
                    at_least(act, acc_done, i)
                    act.activation(sqx[:], x2[q % 2][:], ACT.Square).then_inc(sqx_ready, 1)
            body(0)
            with act.Fori(1, 4) as j:
                body(j)

        def dve_out(dve):
            def body(j):
                for q in range(4):
                    if is_first(j) and q == 0:
                        dve_windows(dve, NG - 1, 1)
                    split_low(dve, "out", j, q + 1)
                    if is_first(j) and q == 0:
                        dve_map(dve, NG - 1)
                        mix_take_low(dve, 3)
                    i = 4 * j + q
                    dve.wait_ge(tile_done, 80 + i + 1)
                    dve.wait_ge(xr_loaded[q % 2], 32 * j + 16 * (q // 2) + 16)
                    at_least(dve, x2_stored[q % 2], 32 * j + 16 * (q // 2))
                    at_least(dve, sqx_ready, i - 1)
                    at_least(dve, h_low, i - 1)
                    dve.tensor_tensor(halves(x2[q % 2][:]), product(q), halves(xr[q % 2][:]), ALU.add).then_inc(pj_read, 1)
                    dve.wait_ge(h_high, i + 1)
                    dve.scalar_tensor_tensor(a_lo[:, bass.ds(i, 1), :].rearrange("p o n -> p (o n)"), x2[q % 2][:],
                                             gain[:, bass.ds(G_CROSS + i, 1)],
                                             a_hi[:, bass.ds(i, 1), :].rearrange("p o n -> p (o n)").bitcast(F32),
                                             ALU.mult, ALU.subtract).then_inc(h_low, 1)
            body(0)
            with dve.Fori(1, 4) as j:
                body(j)

        def pool_sum(pool, r0):
            if r0 == 0:
                pool.wait_ge(pooled, NG)
                pool.memset(acc[:], 0.0).then_inc(acc_zero, 1)
            else:
                pool.wait_ge(sv_done.sem, sv_done.at(32))
                pool.memset(acc[:], 0.0).then_inc(acc_zero, 1)
            pool.wait_ge(acc_zero, 1 if r0 == 0 else 2)

            def body(i):
                pool.wait_ge(sqx_ready, r0 + i + 1)
                at_least(pool, acc_done, r0 + i)
                pool.tensor_tensor(acc[:], acc[:], sqx[:], ALU.add).then_inc(acc_done, 1)
            body(0)
            with pool.Fori(1, 16) as i:
                body(i)

        def pe_out(pe):
            def split(m):
                return lambda pe: pe.wait_ge(mix_low, m)
            pe.wait_ge(ust_ready, 7)
            pe.wait_ge(mix_low, 2)
            for q in range(4):
                steps = {}
                if q == 0:
                    steps = {1: [pe_ux(NG - 1, 1)], 6: [pe_map(NG - 1)], 7: [split(3)], 13: [split(4)]}
                if q == 1:
                    pe.wait_ge(ust_ready, 8)
                multiply(pe, "out", 0, q, tokens(mix_hi), tokens(mix_lo), TOK, steps)
            with pe.Fori(1, 4) as j:
                for q in range(4):
                    multiply(pe, "out", j, q, tokens(mix_hi), tokens(mix_lo))

        qx = put("qx", [KT, TOK], F32, M_B)
        col2 = put("col2", [16], F32, M_END - 64)
        rsb = put("rsb", [NS], F32, M_END - 48)
        own = put("own", [NB, NS], F32, M_END - 64 - NB * NS)
        req = put("req", [NB, NS], F32, M_END - 64 - 2 * NB * NS)
        own_loaded = Reused(vec_loaded, 16 * 8)
        sums_done, col2_root, col2_inv, col2_ready, qs_scaled = (sem(n) for n in (
            "sums_done", "col2_root", "col2_inv", "col2_ready", "qs_scaled"))

        def sp_cq(sp):
            def body(j):
                for q in range(4):
                    load_ahead(sp, "cq", j, q)
                    if is_first(j) and q == 0:
                        sp.wait_ge(pj_read, 96)
                        sp_x2(sp, 3, 3)
                        sp.wait_ge(tile_done, 96)
                        sp.dma_start(own[:], t["consts"][:, C_REQ:C_REQ + NB * NS].rearrange("p (b n) -> p b n", b=NB)).then_inc(
                            own_loaded.sem, 16)
            body(0)
            with sp.Fori(1, 3) as j:
                body(j)
            body(3)

        def act_cq(act):
            def body(j):
                for q in range(4):
                    cast_high(act, "cq", j, q + 1)
                    if is_first(j) and q == 1:
                        act.wait_ge(sums_done, 1)
                        act.activation(col2[:, 0:4], dk[:, 0, 0:4], ACT.Sqrt, scale=1.0 / D, bias=eps_col)
                        act.activation(rsb[:], dk[:, 1, 0:NS], ACT.Sqrt, scale=1.0 / D, bias=eps_col).then_inc(col2_root, 1)
                    act.wait_ge(tile_done, 96 + 4 * j + q + 1)
                    act.activation(halves(qx[:, bass.ds(4 * j + q, 1), :].rearrange("p o n -> p (o n)")), product(q),
                                   ACT.Copy).then_inc(pj_read, 1)
            body(0)
            with act.Fori(1, 4) as j:
                body(j)

        def dve_cq(dve):
            def body(j):
                for q in range(4):
                    split_low(dve, "cq", j, q + 1)
                    if is_first(j) and q == 1:
                        dve.wait_ge(col2_root, 1)
                        dve.reciprocal(col2[:, 0:4], col2[:, 0:4])
                        dve.reciprocal(rsb[:], rsb[:]).then_inc(col2_inv, 1)
                        dve.wait_ge(col2_inv, 1)
                        dve.tensor_scalar(col2[:, 0:4], col2[:, 0:4], XD ** -0.5, None, ALU.mult)
                        dve.tensor_scalar(rsb[:], rsb[:], XD ** -0.5, None, ALU.mult).then_inc(col2_ready, 1)
                        dve.wait_ge(own_loaded.sem, own_loaded.at(16))
                        dve.wait_ge(col2_ready, 1)
                        dve.tensor_tensor(req[:], own[:], rsb[:].unsqueeze(1).to_broadcast([P, NB, NS]),
                                          ALU.mult).then_inc(qs_scaled, 1)
            body(0)
            with dve.Fori(1, 4) as j:
                body(j)
            dve.wait_ge(pj_read, 112)
            dve.wait_ge(qs_scaled, 1)

        def token_sums(pe, first):
            pe.wait_ge(acc_done, 16 if first else 32)
            for i in range(4):
                pe.matmul(dk[:, 0, i:i + 1], acc[:, i * P:(i + 1) * P], ones[:, 0:1], start=True, stop=True)
            if first:
                pe.matmul(dk[:, 1, 0:NS], ones, acc[:, SEQ:TOK], start=True, stop=True).then_inc(sums_done, 1)
            else:
                pe.matmul(dk[S_, 0, 4:5], acc[:, SEQ:TOK], ones[:, 0:1], start=True, stop=True).then_inc(sums_done, 1)

        def pe_cq(pe):
            pe.wait_ge(h_low, 15)
            multiply(pe, "cq", 0, 0, tokens(a_hi), tokens(a_lo), TOK,
                     {14: [lambda pe: pe.wait_ge(h_low, 16)], 15: [lambda pe: token_sums(pe, True)]})
            for q in range(1, 4):
                multiply(pe, "cq", 0, q, tokens(a_hi), tokens(a_lo))
            with pe.Fori(1, 4) as j:
                for q in range(4):
                    multiply(pe, "cq", j, q, tokens(a_hi), tokens(a_lo))

        take = area(M_W, M_END - 64 - 2 * NB * NS)
        kc = [take(f"kc{i}", [2, XD]) for i in range(4)]
        kct = [take(f"kct{i}", [DT, MEM]) for i in range(2)]
        ktb = [take(f"ktb{i}", [DT, MEM]) for i in range(2)]
        vtb0 = take("vtb0", [2, XD])
        vtb = [vtb0, put("vtb1", [2, XD], F32, M_W + 4 * 2 * XD + 2 * 2 * XH * NS)]
        prb = take("prb", [4, MEM])
        ptb = take("ptb", [2, SEQ])
        prt = take("prt", [2, XH, NS])
        m8 = take("m8", [16])
        prs = put("prs", [XH, MEM], F32, M_A + KT * TOK + 12 * TOK)
        qmb = [put(f"qmb{i}", [KT, NS], F32, M_A + i * KT * NS) for i in range(2)]
        pmb = [put(f"pmb{i}", [2, XH, NS], F32, M_W + 4 * 2 * XD + i * 2 * XH * NS) for i in range(2)]
        svr = put("svr", [XH, XD], F32, M_W + 4 * 2 * XD + 2 * DT * MEM)
        m4 = put("m4", [16], F32, M_END - 16)
        kc_loaded = [sem(f"kc_loaded{i}") for i in range(4)]
        ktb_loaded = [sem(f"ktb_loaded{i}") for i in range(2)]
        vtb_loaded = [sem(f"vtb_loaded{i}") for i in range(2)]
        kc_turned = Reused(t0_done, HEADS)
        sk_done = Reused(p1_done, (LEVELS - 1) * HEADS)
        svr_turned = Reused(kk_done, HEADS)
        prs_turned = Reused(v_turned, HEADS)
        sv_done = Reused(tu_done, (LEVELS - 1) * HEADS)
        sc_done = Reused(ks_done, 3 * HEADS)
        p_turned = Reused(vn_done, 4 * HEADS)
        cx_done = Reused(so_done, 4 * HEADS)
        kct_a = Reused(p1_ready, (LEVELS - 1) * HEADS)
        svr_a = Reused(sq_done, HEADS)
        qm_ready = Reused(lt_ready, HEADS)
        pm_ready = Reused(u_seed, HEADS)
        svr_v = sem("svr_v")
        exp_s = Reused(ln_done, HEADS)
        prt_ready = Reused(rn_done, HEADS)
        sv_high = Reused(d_exp, HEADS)
        exp_p = Reused(eg_ready, HEADS)
        ptb_a = Reused(oln_done, HEADS)
        cx_high = Reused(rno_ready, HEADS)
        kct_v = Reused(u_next, (LEVELS - 1) * HEADS)
        nmax_s = Reused(d_ready, HEADS)
        prs_ready = Reused(kq_normed, HEADS)
        ctx_low_s = Reused(qg_ready, HEADS)
        mx_done = Reused(at_ready, HEADS)
        nmax = Reused(u_ready, HEADS)
        prb_ready = Reused(kd_ready, HEADS)
        ptb_v = Reused(vb_ready, HEADS)
        cx_low = Reused(r_ready, 3 * HEADS)
        rcp_p = Reused(vn_ready, 4 * HEADS)
        rcp_s = Reused(hc_ready, HEADS)
        mm_s = Reused(us_ready, (LEVELS - 6) * HEADS)

        def is_last(i):
            return isinstance(i, int) and i == NB // 2 - 1

        def cache(x, b, h):
            return x[0, bass.ds(b, 1), :, h, :].rearrange("o (m p) d -> p (o m) d", p=P)

        def sp_attention(sp):
            sp.wait_ge(tile_done, 96)
            sp.wait_ge(sums_done, 1)
            for i in range(2):
                sp_ktb(sp, i)
            sp_vtb(sp, 0)

            def keys(b):
                for h in range(XH):
                    if not is_first(b):
                        sp.wait_ge(kc_turned.sem, kc_turned.at(4 * b + h - 3))
                    sp.dma_start(kc[h][:], cache(t["cache_mem_k"], b, h)).then_inc(kc_loaded[h], 16)

            def values(b):
                for h in range(XH):
                    if is_first(b):
                        sp.wait_ge(kc_turned.sem, kc_turned.at(29 + h))
                    else:
                        sp.wait_ge(sv_done.sem, sv_done.at(4 * b + h - 3))
                    sp.dma_start(kc[h][:], cache(t["cache_mem_v"], b, h)).then_inc(kc_loaded[h], 16)
            keys(0)
            with sp.Fori(1, NB) as b:
                keys(b)
            values(0)
            sp.wait_ge(sk_done.sem, sk_done.at(32))
            sp_vtb(sp, 1)
            for h in range(2, XH):
                sp.wait_ge(sc_done.sem, sc_done.at(h - 1))
                sp_ktb(sp, h)
            for h in range(2, XH):
                sp.wait_ge(cx_done.sem, cx_done.at(4 * (h - 1)))
                sp_vtb(sp, h)
            with sp.Fori(1, NB) as b:
                values(b)

        def sp_ktb(sp, h):
            sp.dma_start(ktb[h % 2][:], kT_d[DT * h:DT * h + DT].rearrange("k p m -> p k m")).then_inc(ktb_loaded[h % 2], 16)

        def sp_vtb(sp, h):
            sp.dma_start(vtb[h % 2][:], t["mem_v_prompt"][0, 0, :, h, :].rearrange("(m p) d -> p m d", p=P)).then_inc(vtb_loaded[h % 2], 16)

        def pe_sample_keys(pe):
            def turn(b, h):
                pe.wait_ge(kc_loaded[h], 16 * b + 16)
                u = 4 * b + h
                at_least(pe, kct_a, u - 1)
                at_least(pe, kct_v, u - 1)
                for d in range(DT):
                    for m in range(2):
                        o = (d % 2) * 256 + m * P
                        mm = pe.transpose(dk[:, 2 * (h % 2) + d // 2, o:o + P], kc[h][:, m, d * P:(d + 1) * P], ident)
                mm.then_inc(kc_turned.sem, 1)

            def scores(b, h, par, first, last):
                u = 4 * b + h
                if h == 0:
                    pe.wait_ge(qm_ready.sem, qm_ready.at(b + 1))
                pe.wait_ge(kct_a.sem, kct_a.at(u + 1))
                pe.wait_ge(kct_v.sem, kct_v.at(u + 1))
                for d in range(DT):
                    mm = pe.matmul(pj[S_, h, 0:MEM], qmb[par][:, DT * h + d, :], kct[h % 2][:, d, :],
                                   start=(first and d == 0), stop=(last and d == DT - 1))
                mm.then_inc(sk_done.sem, 1)

            pe.wait_ge(pj_read, 112)
            pe.wait_ge(col2_root, 1)

            def body(i):
                for par in range(2):
                    b = 2 * i + par
                    turn(b, 0)
                    for h in range(XH):
                        if h + 1 < XH:
                            turn(b, h + 1)
                        scores(b, h, par, is_first(i) and par == 0, is_last(i) and par == 1)
            body(0)
            with pe.Fori(1, NB // 2 - 1) as i:
                body(i)
            body(NB // 2 - 1)

        def queries(dve, b, par):
            at_least(dve, sk_done, 4 * (b - 1))
            dve.tensor_tensor(qmb[par][:], qx[:, :, SEQ:TOK], req[:, bass.ds(b, 1), :].to_broadcast([P, KT, NS]),
                              ALU.mult).then_inc(qm_ready.sem, 1)

        def probabilities(dve, b, par):
            at_least(dve, sv_done, 4 * (b - 1))
            dve.tensor_tensor(pmb[par][:].rearrange("p m h n -> p (m h) n"), prt[:].rearrange("p m h n -> p (m h) n"),
                              own[:, bass.ds(b, 1), :].to_broadcast([P, 2 * XH, NS]), ALU.mult).then_inc(pm_ready.sem, 1)

        def take_keys(eng, b, mine):
            for h in range(XH):
                u = 4 * b + h
                eng.wait_ge(kc_turned.sem, kc_turned.at(u + 1))
                at_least(eng, sk_done, u - 1)
                o, i = kct[h % 2][:, 2 * mine:2 * mine + 2, :].rearrange("p d m -> p (d m)"), dk[:, 2 * (h % 2) + mine, :]
                if mine:
                    eng.tensor_copy(o, i).then_inc(kct_v.sem, 1)
                else:
                    eng.activation(o, i, ACT.Copy).then_inc(kct_a.sem, 1)

        def scp(h):
            return (dk, pj)[h % 2]

        def pe_attention(pe):
            pe_sample_keys(pe)

            def scores(h):
                pe.wait_ge(ktb_loaded[h % 2], 16 * (h // 2) + 16)
                at_least(pe, exp_p, h - 1)
                if h == 0:
                    pe.wait_ge(kct_a.sem, kct_a.at(32))
                    pe.wait_ge(kct_v.sem, kct_v.at(32))
                if h == 1:
                    pe.wait_ge(exp_s.sem, exp_s.at(1))
                for i in range(4):
                    for d in range(DT):
                        mm = pe.matmul(scp(h)[:, i // 2, (i % 2) * 256:(i % 2) * 256 + 256], qx[:, DT * h + d, i * P:(i + 1) * P],
                                       ktb[h % 2][:, d, :], start=(d == 0), stop=(d == DT - 1))
                mm.then_inc(sc_done.sem, 1)

            def turn(h):
                pe.wait_ge(prb_ready.sem, prb_ready.at(h + 1))
                if h == 0:
                    pe.wait_ge(prt_ready.sem, prt_ready.at(1))
                at_least(pe, ptb_a, h)
                at_least(pe, ptb_v, h)
                for m in range(2):
                    for i in range(4):
                        mm = pe.transpose(dk[:, 2 + m, i * P:(i + 1) * P], prb[:, i, m * P:(m + 1) * P], ident)
                mm.then_inc(p_turned.sem, 1)

            def context(h):
                pe.wait_ge(ptb_a.sem, ptb_a.at(h + 1))
                pe.wait_ge(ptb_v.sem, ptb_v.at(h + 1))
                pe.wait_ge(vtb_loaded[h % 2], 16 * (h // 2) + 16)
                for d in range(DT):
                    at_least(pe, cx_low, 4 * h + d - 1)
                    for m in range(2):
                        mm = pe.matmul(pj[:, 2 + d % 2, :], vtb[h % 2][:, m, d * P:(d + 1) * P], ptb[:, m, :], start=(m == 0), stop=(m == 1))
                    mm.then_inc(cx_done.sem, 1)

            scores(0)
            scores(1)
            pe.wait_ge(prs_ready.sem, prs_ready.at(1))
            for m in range(2):
                for h in range(XH):
                    mm = pe.transpose(dk[:, 2, (m * XH + h) * NS:(m * XH + h + 1) * NS], prs[S_, h, m * P:(m + 1) * P], ident[S_, S_])
            mm.then_inc(prs_turned.sem, 1)
            for h in range(XH):
                turn(h)
                if h + 2 < XH:
                    scores(h + 2)
                context(h)

            def values(i):
                for par in range(2):
                    b = 2 * i + par
                    pe.wait_ge(pm_ready.sem, pm_ready.at(b + 1))
                    for h in range(XH):
                        pe.wait_ge(kc_loaded[h], 16 * (NB + 1) + 16 * b)
                        for m in range(2):
                            mm = pe.matmul(pj[S_, h, :], pmb[par][:, m, h, :], kc[h][:, m, :],
                                           start=(is_first(i) and par == 0 and m == 0), stop=(is_last(i) and par == 1 and m == 1))
                        mm.then_inc(sv_done.sem, 1)
            pe.wait_ge(cx_low.sem, cx_low.at(16))
            pe.wait_ge(exp_p.sem, exp_p.at(4))
            values(0)
            with pe.Fori(1, NB // 2 - 1) as i:
                values(i)
            values(NB // 2 - 1)
            pe.wait_ge(svr_a.sem, svr_a.at(1))
            pe.wait_ge(svr_v, 1)
            for k in range(KT):
                mm = pe.transpose(dk[:, 0, k * NS:(k + 1) * NS], svr[S_, k // DT, (k % DT) * P:(k % DT + 1) * P], ident[S_, S_])
            mm.then_inc(svr_turned.sem, 1)

        def act_attention(act):
            act.wait_ge(tile_done, 96)

            def body(i):
                for par in range(2):
                    take_keys(act, 2 * i + par, 0)
            body(0)
            with act.Fori(1, NB // 2) as i:
                body(i)
            act.wait_ge(nmax_s.sem, nmax_s.at(1))
            for h in range(XH):
                a = act.activation(prs[S_, h, :], pj[S_, h, 0:MEM], ACT.Exp, bias=m8[S_, 4 + h:5 + h],
                                   accum_out=m8[S_, 8 + h:9 + h])
            a.then_inc(exp_s.sem, 1)

            def exps(h):
                act.wait_ge(nmax.sem, nmax.at(h + 1))
                at_least(act, p_turned, h)
                for i in range(4):
                    a = act.activation(prb[:, i, :], scp(h)[:, i // 2, (i % 2) * 256:(i % 2) * 256 + 256], ACT.Exp,
                                       scale=col2[:, i:i + 1], bias=m4[:, 4 + i:5 + i], accum_out=m4[:, 8 + i:9 + i])
                a.then_inc(exp_p.sem, 1)

            exps(0)
            act.wait_ge(prs_turned.sem, prs_turned.at(1))
            act.activation(prt[:].rearrange("p m h n -> p (m h n)"), dk[:, 2, 0:MEM], ACT.Copy).then_inc(prt_ready.sem, 1)
            for h in range(XH):
                act.wait_ge(p_turned.sem, p_turned.at(h + 1))
                at_least(act, cx_done, 4 * h)
                act.activation(ptb[:, 0, :], dk[:, 2, :], ACT.Copy).then_inc(ptb_a.sem, 1)
                if h + 1 < XH:
                    exps(h + 1)
                for d in range(DT):
                    act.wait_ge(cx_done.sem, cx_done.at(4 * h + d + 1))
                    act.activation(a_hi[:, DT * h + d, 0:SEQ], pj[:, 2 + d % 2, :], ACT.Copy).then_inc(cx_high.sem, 1)
            act.wait_ge(sv_done.sem, sv_done.at(32))
            act.activation(svr[S_, 0:2, :], pj[S_, 0:2, :], ACT.Copy).then_inc(svr_a.sem, 1)
            act.wait_ge(svr_turned.sem, svr_turned.at(1))
            act.activation(a_hi[:, :, SEQ:TOK], dk[:, 0, :].rearrange("p (k n) -> p k n", k=KT), ACT.Copy).then_inc(sv_high.sem, 1)

        def dve_attention(dve):
            dve.wait_ge(tile_done, 96)

            queries(dve, 0, 0)

            def body(i):
                for par in range(2):
                    b = 2 * i + par
                    if not (is_first(i) and par == 0):
                        queries(dve, b, par)
                    take_keys(dve, b, 1)
            body(0)
            with dve.Fori(1, NB // 2) as i:
                body(i)
            dve.wait_ge(sk_done.sem, sk_done.at(32))
            dve.tensor_reduce(m8[S_, 0:4], pj[S_, :, 0:MEM], AX_X, ALU.max).then_inc(mm_s.sem, 1)
            dve.wait_ge(mm_s.sem, mm_s.at(1))
            dve.tensor_scalar(m8[S_, 4:8], m8[S_, 0:4], -1.0, None, ALU.mult).then_inc(nmax_s.sem, 1)

            def maxima(h):
                dve.wait_ge(sc_done.sem, sc_done.at(h + 1))
                dve.tensor_reduce(m4[:, 12:16], scp(h)[:, 0:2, :].rearrange("p b (i m) -> p (b i) m", i=2), AX_X, ALU.max).then_inc(mx_done.sem, 1)
                dve.wait_ge(mx_done.sem, mx_done.at(h + 1))
                at_least(dve, exp_p, h)
                dve.scalar_tensor_tensor(m4[:, 4:8], m4[:, 12:16], -1.0, col2[:, 0:4], ALU.mult, ALU.mult).then_inc(nmax.sem, 1)

            def over_sums(h):
                dve.wait_ge(exp_p.sem, exp_p.at(h + 1))
                dve.reciprocal(m4[:, 0:4], m4[:, 8:12]).then_inc(rcp_p.sem, 1)
                dve.wait_ge(rcp_p.sem, rcp_p.at(h + 1))
                dve.tensor_tensor(prb[:], prb[:], m4[:, 0:4].unsqueeze(2).to_broadcast([P, 4, MEM]), ALU.mult).then_inc(prb_ready.sem, 1)

            maxima(0)
            dve.wait_ge(exp_s.sem, exp_s.at(1))
            dve.reciprocal(m8[S_, 0:4], m8[S_, 8:12]).then_inc(rcp_s.sem, 1)
            dve.wait_ge(rcp_s.sem, rcp_s.at(1))
            dve.tensor_tensor(prs[S_, :, :], prs[S_, :, :], m8[S_, 0:4].unsqueeze(2).to_broadcast([NS, XH, MEM]),
                              ALU.mult).then_inc(prs_ready.sem, 1)
            over_sums(0)
            for h in range(XH):
                if h + 1 < XH:
                    maxima(h + 1)
                dve.wait_ge(p_turned.sem, p_turned.at(h + 1))
                at_least(dve, cx_done, 4 * h)
                dve.tensor_copy(ptb[:, 1, :], dk[:, 3, :]).then_inc(ptb_v.sem, 1)
                for d in range(DT):
                    if d == 2 and h + 1 < XH:
                        over_sums(h + 1)
                    dve.wait_ge(cx_high.sem, cx_high.at(4 * h + d + 1))
                    dve.tensor_tensor(a_lo[:, DT * h + d, 0:SEQ], pj[:, 2 + d % 2, :], a_hi[:, DT * h + d, 0:SEQ].bitcast(F32),
                                      ALU.subtract).then_inc(cx_low.sem, 1)
            dve.wait_ge(prt_ready.sem, prt_ready.at(1))
            probabilities(dve, 0, 0)
            probabilities(dve, 1, 1)
            with dve.Fori(1, NB // 2) as i:
                for par in range(2):
                    probabilities(dve, 2 * i + par, par)
            dve.wait_ge(sv_done.sem, sv_done.at(32))
            dve.tensor_copy(svr[S_, 2:4, :], pj[S_, 2:4, :]).then_inc(svr_v, 1)
            dve.wait_ge(sv_high.sem, sv_high.at(1))
            dve.tensor_tensor(a_lo[:, :, SEQ:TOK], dk[:, 0, :].rearrange("p (k n) -> p k n", k=KT),
                              a_hi[:, :, SEQ:TOK].bitcast(F32), ALU.subtract).then_inc(ctx_low_s.sem, 1)

        xg = put("xg", [KT, TOK], F32, M_B)
        take = area(M_W + 6 * TOK + 64, M_END - 64)
        yb = [take(f"yb{i}", [D]) for i in range(2)]
        rs3 = take("rs3", [8])
        y_stored = [sem(f"y_stored{i}") for i in range(2)]
        (xg_ready, root3, rs3_ready, y_turned, y_act, y_dve) = (sem(n) for n in (
            "xg_ready", "root3", "rs3_ready", "y_turned", "y_act", "y_dve"))

        def sp_co(sp):
            def body(j):
                for q in range(4):
                    load_ahead(sp, "co", j, q)
                    if is_first(j) and q == 0:
                        for i in range(2):
                            sp.wait_ge(x2_stored[i], 128)
                        sp.wait_ge(sv_done.sem, sv_done.at(32))
                    sp_residual(sp, "co", j, q)
            body(0)
            with sp.Fori(1, 3) as j:
                body(j)
            body(3)
            for n in range(5):
                rows = P if n < 4 else NS
                sp.wait_ge(y_act, 2 * n + 2)
                sp.wait_ge(y_dve, 2 * n + 2)
                dst = t["y_prompt"][0, n * P:(n + 1) * P, :] if n < 4 else t["y_sample"].rearrange("b t d -> (b t) d")
                sp.dma_start(dst, yb[n % 2][0:rows, :]).then_inc(y_stored[n % 2], 16)
            sp.wait_ge(y_stored[0], 48)
            sp.wait_ge(y_stored[1], 32)
            for s, v in ((mst_stored, 128), (kts_stored, 64), (xts_stored, 80), (st_stored, 768), (s_stored, 128),
                         (s0_stored, 128), (ust_stored, 16 * 72), (old_rows, 16), (x2_stored[0], 128), (x2_stored[1], 128)):
                sp.wait_ge(s, v)

        def act_co(act):
            def body(j):
                for q in range(4):
                    cast_high(act, "co", j, q + 1)
                    i = 4 * j + q
                    act.wait_ge(pj_read, 112 + i + 1)
                    act.activation(xg[:, bass.ds(i, 1), :].rearrange("p o n -> p (o n)"), x2[q % 2][:], ACT.Copy,
                                   scale=gain[:, bass.ds(G_FINAL + i, 1)]).then_inc(xg_ready, 1)
                    act.wait_ge(acc_done, 16 + i)
                    act.activation(sqx[:], x2[q % 2][:], ACT.Square).then_inc(sqx_ready, 1)
            body(0)
            with act.Fori(1, 3) as j:
                body(j)
            body(3)
            act.wait_ge(sums_done, 2)
            act.activation(rs3[:, 0:4], dk[:, 0, 0:4], ACT.Sqrt, scale=1.0 / D, bias=eps_col)
            act.activation(rs3[S_, 4:5], dk[S_, 0, 4:5], ACT.Sqrt, scale=1.0 / D, bias=eps_col[S_, :]).then_inc(root3, 1)
            act.wait_ge(rs3_ready, 1)
            for n in range(5):
                rows = P if n < 4 else NS
                for c in (0, 2):
                    act.wait_ge(y_turned, 4 * n + c + 1)
                    at_least(act, y_stored[n % 2], 16 * (n // 2))
                    act.activation(yb[n % 2][0:rows, c * 512:(c + 1) * 512], pj[0:rows, c, :], ACT.Copy,
                                   scale=rs3[0:rows, n:n + 1]).then_inc(y_act, 1)

        def dve_co(dve):
            def body(j):
                for q in range(4):
                    split_low(dve, "co", j, q + 1)
                    i = 4 * j + q
                    dve.wait_ge(tile_done, 112 + i + 1)
                    dve.wait_ge(xr_loaded[q % 2], 128 + 32 * j + 16 * (q // 2) + 16)
                    dve.wait_ge(sqx_ready, 16 + i - 1)
                    at_least(dve, xg_ready, i - 1)
                    dve.tensor_tensor(halves(x2[q % 2][:]), product(q), halves(xr[q % 2][:]), ALU.add).then_inc(pj_read, 1)
            body(0)
            with dve.Fori(1, 3) as j:
                body(j)
            body(3)
            dve.wait_ge(root3, 1)
            dve.reciprocal(rs3[:, 0:4], rs3[:, 0:4])
            dve.reciprocal(rs3[S_, 4:5], rs3[S_, 4:5]).then_inc(rs3_ready, 1)
            dve.wait_ge(rs3_ready, 1)
            for n in range(5):
                rows = P if n < 4 else NS
                for c in (1, 3):
                    dve.wait_ge(y_turned, 4 * n + c + 1)
                    at_least(dve, y_stored[n % 2], 16 * (n // 2))
                    dve.tensor_scalar(yb[n % 2][0:rows, c * 512:(c + 1) * 512], pj[0:rows, c, :], rs3[0:rows, n:n + 1], None,
                                      ALU.mult).then_inc(y_dve, 1)

        def pe_co(pe):
            pe.wait_ge(ctx_low_s.sem, ctx_low_s.at(1))
            pe.wait_ge(cx_low.sem, cx_low.at(16))
            with pe.Fori(0, 4) as j:
                for q in range(4):
                    multiply(pe, "co", j, q, tokens(a_hi), tokens(a_lo))
            pe.wait_ge(xg_ready, 16)
            pe.wait_ge(pj_read, 128)
            for n in range(5):
                rows = P if n < 4 else NS
                if n == 1:
                    token_sums(pe, False)
                for c in range(4):
                    if n > 0:
                        pe.wait_ge(y_dve if c % 2 else y_act, 2 * (n - 1) + c // 2 + 1)
                    for m in range(4):
                        mm = pe.transpose(pj[0:rows, c, m * P:(m + 1) * P], xg[:, 4 * c + m, n * P:n * P + rows], ident)
                    mm.then_inc(y_turned, 1)

        block = ctx.enter_context(nc.Block())

        @block.sync
        def _(sp):
            sp_mem(sp)
            sp_heads(sp)
            sp_pool(sp)
            sp_out(sp)
            sp_cq(sp)
            sp_attention(sp)
            sp_co(sp)

        @block.scalar
        def _(act):
            act_mem(act)
            act_heads(act)
            act_pool(act)
            act_out(act)
            act_cq(act)
            act_attention(act)
            act_co(act)

        @block.vector
        def _(dve):
            dve_mem(dve)
            dve_heads(dve)
            dve_pool(dve)
            dve_out(dve)
            dve_cq(dve)
            dve_attention(dve)
            dve_co(dve)

        @block.gpsimd
        def _(pool):
            pool_heads(pool)
            pool_pool(pool)
            pool_sum(pool, 0)
            pool_sum(pool, 16)

        @block.tensor
        def _(pe):
            pe_mem(pe)
            pe_heads(pe)
            pe_pool(pe)
            pe_out(pe)
            pe_cq(pe)
            pe_attention(pe)
            pe_co(pe)


INPUTS = ("x_prompt", "x_sample", "mem_prompt", "cache_mem_k", "cache_mem_v", "state_delta", "state_conv", "state_pool",
          "norm_mix", "w_in", "conv_w", "a_log", "dt_bias", "gdn_norm", "pool_w", "pool_scale", "w_out", "norm_mem",
          "norm_cross", "w_cq", "w_ck", "w_cv", "w_co", "norm_final")
OUTPUTS = (("y_prompt", (1, SEQ, D)), ("y_sample", (NB, NT, D)),
           ("mem_k_prompt", (1, 1, MEM, XH, XD)), ("mem_v_prompt", (1, 1, MEM, XH, XD)),
           ("delta_prompt", (1, 1, HEADS, P, P)), ("conv_prompt", (1, 1, 3, QKV)), ("pool_prompt", (1, 1, BUF, MIX)),
           ("delta_sample", (1, NB, HEADS, P, P)), ("conv_sample", (1, NB, 3, QKV)), ("pool_sample", (1, NB, BUF, MIX)))


def kernel(**inputs):
    import concourse.bacc as bacc
    from concourse.bass_utils import run_bass_kernel_spmd

    nc = bacc.Bacc("TRN2", target_bir_lowering=False, num_devices=1)
    arrays, t = {}, {}
    for name in INPUTS:
        arrays[f"in_{name}_dram"] = np.ascontiguousarray(inputs[name])
    arrays["in_consts_dram"] = constants()
    for name in INPUTS + ("consts",):
        a = arrays[f"in_{name}_dram"]
        t[name] = nc.dram_tensor(f"in_{name}_dram", a.shape, mybir.dt.from_np(a.dtype), kind="ExternalInput").ap()
    for i, (name, shape) in enumerate(OUTPUTS):
        t[name] = nc.dram_tensor(f"out_{i}_dram", shape, F32, kind="ExternalOutput").ap()
    build(nc, t)
    r = run_bass_kernel_spmd(nc, [arrays], core_ids=[0])
    return tuple(r.results[0][f"out_{i}_dram"] for i in range(len(OUTPUTS)))
```
